# Optimizing a Trainium2 kernel written in Bass

```python
import jax, jax.numpy as jnp
from jax import lax
import numpy as np

D_MODEL = 1024
BATCH = 1
SEQ = 512
DEPTH = 1

PLE_DIM = 256
EPS = 1e-6
NEG = -1e30

GDN_HEADS = 4
GDN_DK = 128
GDN_DV = 128
GDN_CONV = 4
GDN_CHUNK = 64

NSA_HEADS = 8
NSA_GROUPS = 2
NSA_HPG = NSA_HEADS // NSA_GROUPS
NSA_DK = 64
NSA_DV = 64
CMP_LEN = 32
CMP_STRIDE = 16
CMP_HIDDEN = 256
SEL_BLOCK = 64
SEL_TOPN = 16
SEL_QCHUNK = 64
WINDOW = 512
WIN_QBLOCK = 128
FORCED_SCORE = 1e9

D_FF = 2816
FFN_CONV = 3

IN_SPLITS = (
    GDN_HEADS * GDN_DK,
    GDN_HEADS * GDN_DK,
    GDN_HEADS * GDN_DV,
    GDN_HEADS * GDN_DV,
    GDN_HEADS,
    GDN_HEADS,
    NSA_HEADS * NSA_DK,
    NSA_GROUPS * NSA_DK,
    NSA_GROUPS * NSA_DV,
    NSA_GROUPS * NSA_DK,
    NSA_GROUPS * NSA_DV,
    NSA_GROUPS * NSA_DK,
    NSA_GROUPS * NSA_DV,
    NSA_HEADS * 3,
    2 * D_MODEL,
)
D_IN = sum(IN_SPLITS)


def rmsnorm(x, w):
    xf = x.astype(jnp.float32)
    y = xf * lax.rsqrt(jnp.mean(xf * xf, axis=-1, keepdims=True) + EPS)
    return (y * w.astype(jnp.float32)).astype(x.dtype)

def l2norm(x):
    return x * lax.rsqrt(jnp.sum(x * x, axis=-1, keepdims=True) + EPS)

def causal_dwconv(x, w):
    width, c = w.shape
    return lax.conv_general_dilated(
        x, w[:, None, :].astype(x.dtype), window_strides=(1,), padding=((width - 1, 0),),
        dimension_numbers=('NWC', 'WIO', 'NWC'), feature_group_count=c)

def alibi_slopes(n):
    return 2.0 ** (-8.0 * jnp.arange(1, n + 1, dtype=jnp.float32) / n)

def masked_softmax(s, valid):
    p = jax.nn.softmax(jnp.where(valid, s, NEG), axis=-1)
    return jnp.where(valid, p, 0.0)

def chunk_gated_delta_rule(q, k, v, beta, g):
    B, S, H, dk = q.shape
    dv = v.shape[-1]
    C = GDN_CHUNK
    n = S // C

    def chunks(t):
        t = t.reshape((B, n, C, H) + t.shape[3:])
        return jnp.moveaxis(t, (1, 3), (0, 2))

    qc, kc, vc, bc = chunks(q), chunks(k), chunks(v), chunks(beta)
    gcum = jnp.cumsum(chunks(g), axis=-1)
    idx = jnp.arange(C)
    strict = idx[:, None] > idx[None, :]
    incl = idx[:, None] >= idx[None, :]
    gdiff = gcum[..., :, None] - gcum[..., None, :]
    dec_strict = jnp.where(strict, jnp.exp(jnp.where(strict, gdiff, 0.0)), 0.0)
    dec_incl = jnp.where(incl, jnp.exp(jnp.where(incl, gdiff, 0.0)), 0.0)
    lower = bc[..., None] * jnp.einsum('nbhid,nbhjd->nbhij', kc, kc) * dec_strict
    gam = jnp.exp(gcum)
    rhs = jnp.concatenate([(bc * gam)[..., None] * kc, bc[..., None] * vc], axis=-1)
    sol = lax.linalg.triangular_solve(lower + jnp.eye(C, dtype=q.dtype), rhs,
                                      left_side=True, lower=True, unit_diagonal=True)
    w_c, u0_c = sol[..., :dk], sol[..., dk:]
    qk = jnp.einsum('nbhid,nbhjd->nbhij', qc, kc) * dec_incl
    q_dec = qc * gam[..., None]
    k_tail = kc * jnp.exp(gcum[..., -1:] - gcum)[..., None]
    g_last = gam[..., -1]

    def step(state, inp):
        w_, u0_, qk_, qd_, kt_, gl_ = inp
        u = u0_ - jnp.einsum('bhcd,bhde->bhce', w_, state)
        o = jnp.einsum('bhcd,bhde->bhce', qd_, state) + jnp.einsum('bhij,bhje->bhie', qk_, u)
        new_state = gl_[..., None, None] * state + jnp.einsum('bhcd,bhce->bhde', kt_, u)
        return new_state, o

    s0 = jnp.zeros((B, H, dk, dv), q.dtype)
    _, o = lax.scan(step, s0, (w_c, u0_c, qk, q_dec, k_tail, g_last))
    return jnp.moveaxis(o, (0, 2), (1, 3)).reshape(B, S, H, dv)

def gdn_mixer(q, k, v, z, b, a, conv_w, a_log, dt_bias, norm_w):
    B, S, _ = q.shape
    H, dk, dv = GDN_HEADS, GDN_DK, GDN_DV
    f32 = jnp.float32
    qkv = jax.nn.silu(causal_dwconv(jnp.concatenate([q, k, v], axis=-1), conv_w))
    q, k, v = jnp.split(qkv, [H * dk, 2 * H * dk], axis=-1)
    q = l2norm(q.reshape(B, S, H, dk).astype(f32)) * (dk ** -0.5)
    k = l2norm(k.reshape(B, S, H, dk).astype(f32))
    v = v.reshape(B, S, H, dv).astype(f32)
    beta = jax.nn.sigmoid(b.astype(f32))
    g = -jnp.exp(a_log.astype(f32)) * jax.nn.softplus(a.astype(f32) + dt_bias.astype(f32))
    o = chunk_gated_delta_rule(q, k, v, beta, g).astype(z.dtype)
    o = rmsnorm(o, norm_w) * jax.nn.silu(z.reshape(B, S, H, dv))
    return o.reshape(B, S, H * dv)

def compress_blocks(x, pos, w1, w2):
    B, S, G, d = x.shape
    r = CMP_LEN // CMP_STRIDE
    xs = x.reshape(B, S // CMP_STRIDE, CMP_STRIDE, G, d)
    nc = S // CMP_STRIDE - r + 1
    blocks = jnp.concatenate([xs[:, i:i + nc] for i in range(r)], axis=2)
    blocks = blocks + pos[:, None, :]
    flat = jnp.moveaxis(blocks, 3, 2).reshape(B, nc, G, CMP_LEN * d)
    return jax.nn.gelu(flat @ w1) @ w2

def nsa_mixer(q, k_cmp, v_cmp, k_slc, v_slc, k_win, v_win, gate,
              cmp_pos_k, cmp_w1_k, cmp_w2_k, cmp_pos_v, cmp_w1_v, cmp_w2_v):
    B, S, _ = q.shape
    H, G, R, dk, dv = NSA_HEADS, NSA_GROUPS, NSA_HPG, NSA_DK, NSA_DV
    f32 = jnp.float32
    slopes = alibi_slopes(H).reshape(G, R)
    t = jnp.arange(S)
    qh = q.reshape(B, S, G, R, dk) * (dk ** -0.5)
    grp = lambda y, d: y.reshape(B, S, G, d)

    kc = compress_blocks(grp(k_cmp, dk), cmp_pos_k, cmp_w1_k, cmp_w2_k)
    vc = compress_blocks(grp(v_cmp, dv), cmp_pos_v, cmp_w1_v, cmp_w2_v)
    nc = kc.shape[1]
    blk_start = jnp.arange(nc) * CMP_STRIDE
    dist_c = t[:, None] - (blk_start + CMP_LEN - 1)[None, :]
    s_c = jnp.einsum('bsgrd,bngd->bgrsn', qh, kc).astype(f32) \
        - slopes[None, :, :, None, None] * dist_c.astype(f32)
    p_c = masked_softmax(s_c, dist_c >= 0)
    o_cmp = jnp.einsum('bgrsn,bngd->bsgrd', p_c.astype(vc.dtype), vc)

    ns = S // SEL_BLOCK
    sel_start = jnp.arange(ns) * SEL_BLOCK
    overlap = jnp.clip(jnp.minimum(blk_start[:, None] + CMP_LEN, sel_start[None, :] + SEL_BLOCK)
                       - jnp.maximum(blk_start[:, None], sel_start[None, :]), 0, None).astype(f32) / CMP_LEN
    imp = jnp.einsum('bgsn,nj->bgsj', p_c.sum(axis=2), overlap)
    cur = t // SEL_BLOCK
    j = jnp.arange(ns)
    forced = (j[None, :] == 0) | (j[None, :] == cur[:, None]) | (j[None, :] == cur[:, None] - 1)
    sel_valid = j[None, :] <= cur[:, None]
    imp = jnp.where(sel_valid, jnp.where(forced, FORCED_SCORE, imp), NEG)
    n_sel = min(SEL_TOPN, ns)
    _, sel_idx = lax.top_k(imp, n_sel)

    ks = k_slc.reshape(B, ns, SEL_BLOCK, G, dk).transpose(0, 3, 1, 2, 4)
    vs = v_slc.reshape(B, ns, SEL_BLOCK, G, dv).transpose(0, 3, 1, 2, 4)
    QC = SEL_QCHUNK
    nq = S // QC
    q_ch = qh.reshape(B, nq, QC, G, R, dk).transpose(1, 0, 3, 4, 2, 5)
    idx_ch = sel_idx.reshape(B, G, nq, QC, n_sel).transpose(2, 0, 1, 3, 4)
    t_ch = t.reshape(nq, QC)
    nk = n_sel * SEL_BLOCK

    def sel_chunk(args):
        qb, ib, tb = args
        flat = ib.reshape(B, G, QC * n_sel)[:, :, :, None, None]
        kg = jnp.take_along_axis(ks, flat, axis=2).reshape(B, G, QC, nk, dk)
        vg = jnp.take_along_axis(vs, flat, axis=2).reshape(B, G, QC, nk, dv)
        pos = (ib[..., None] * SEL_BLOCK + jnp.arange(SEL_BLOCK)).reshape(B, G, QC, nk)
        dist = tb[None, None, :, None] - pos
        s = jnp.einsum('bgrqd,bgqkd->bgrqk', qb, kg).astype(f32) \
            - slopes[None, :, :, None, None] * dist[:, :, None].astype(f32)
        pr = masked_softmax(s, (dist >= 0)[:, :, None])
        return jnp.einsum('bgrqk,bgqkd->bgrqd', pr.astype(vg.dtype), vg)

    o_slc = lax.map(sel_chunk, (q_ch, idx_ch, t_ch))
    o_slc = o_slc.transpose(1, 0, 4, 2, 3, 5).reshape(B, S, G, R, dv)

    QB = WIN_QBLOCK
    nb = S // QB
    nwb = WINDOW // QB

    def band(y, d):
        yb = y.reshape(B, nb, QB, G, d).transpose(1, 0, 3, 2, 4)
        yp = jnp.pad(yb, ((nwb, 0), (0, 0), (0, 0), (0, 0), (0, 0)))
        return jnp.concatenate([yp[i:i + nb] for i in range(nwb + 1)], axis=3)

    kband, vband = band(k_win, dk), band(v_win, dv)
    q_wb = qh.reshape(B, nb, QB, G, R, dk).transpose(1, 0, 3, 4, 2, 5)
    qpos = t.reshape(nb, QB)
    kpos = (jnp.arange(nb)[:, None] - nwb) * QB + jnp.arange((nwb + 1) * QB)[None, :]

    def win_block(args):
        qb, kb, vb, tq, tk = args
        dist = tq[:, None] - tk[None, :]
        valid = (dist >= 0) & (dist < WINDOW) & (tk[None, :] >= 0)
        s = jnp.einsum('bgrqd,bgkd->bgrqk', qb, kb).astype(f32) \
            - slopes[None, :, :, None, None] * dist.astype(f32)
        pr = masked_softmax(s, valid)
        return jnp.einsum('bgrqk,bgkd->bgrqd', pr.astype(vb.dtype), vb)

    o_win = lax.map(win_block, (q_wb, kband, vband, qpos, kpos))
    o_win = o_win.transpose(1, 0, 4, 2, 3, 5).reshape(B, S, G, R, dv)

    gates = jax.nn.sigmoid(gate).reshape(B, S, G, R, 3)
    o = gates[..., 0:1] * o_cmp + gates[..., 1:2] * o_slc + gates[..., 2:3] * o_win
    return o.reshape(B, S, H * dv)

def first_inputs(seed: int = 0) -> dict:
    key = jax.random.key(seed)
    ks = jax.random.split(key, 32)
    L, D = DEPTH, D_MODEL
    f32 = jnp.float32

    def nrm(k, shape, fan_in):
        return jax.random.normal(k, shape, f32) * (fan_in ** -0.5)

    def gain(k, n):
        return 1.0 + 0.05 * jax.random.normal(k, (L, n), f32)

    dt = jnp.exp(jax.random.uniform(ks[6], (L, GDN_HEADS), f32, minval=np.log(1e-3), maxval=np.log(1e-1)))
    return {
        'x': jax.random.normal(ks[0], (BATCH, SEQ, D), f32),
        'p': jax.random.normal(ks[1], (DEPTH, BATCH, SEQ, PLE_DIM), f32),
        'norm_mix_pre': gain(ks[2], D),
        'w_in': nrm(ks[3], (L, D, D_IN), D),
        'conv_qkv': nrm(ks[4], (L, GDN_CONV, 2 * GDN_HEADS * GDN_DK + GDN_HEADS * GDN_DV), GDN_CONV),
        'a_log': jnp.log(jax.random.uniform(ks[5], (L, GDN_HEADS), f32, minval=1.0, maxval=16.0)),
        'dt_bias': dt + jnp.log(-jnp.expm1(-dt)),
        'gdn_norm': gain(ks[7], GDN_DV),
        'cmp_pos_k': 0.1 * jax.random.normal(ks[8], (L, CMP_LEN, NSA_DK), f32),
        'cmp_w1_k': nrm(ks[9], (L, CMP_LEN * NSA_DK, CMP_HIDDEN), CMP_LEN * NSA_DK),
        'cmp_w2_k': nrm(ks[10], (L, CMP_HIDDEN, NSA_DK), CMP_HIDDEN),
        'cmp_pos_v': 0.1 * jax.random.normal(ks[11], (L, CMP_LEN, NSA_DV), f32),
        'cmp_w1_v': nrm(ks[12], (L, CMP_LEN * NSA_DV, CMP_HIDDEN), CMP_LEN * NSA_DV),
        'cmp_w2_v': nrm(ks[13], (L, CMP_HIDDEN, NSA_DV), CMP_HIDDEN),
        'w_a2d': nrm(ks[14], (L, GDN_HEADS * GDN_DV, D), GDN_HEADS * GDN_DV),
        'w_b2d': nrm(ks[15], (L, NSA_HEADS * NSA_DV, D), NSA_HEADS * NSA_DV),
        'w_o': nrm(ks[16], (L, D, D), D),
        'norm_mix_post': gain(ks[17], D),
        'norm_ffn_pre': gain(ks[18], D),
        'w_up': nrm(ks[19], (L, D, 2 * D_FF), D),
        'conv_ffn': nrm(ks[20], (L, FFN_CONV, 2 * D_FF), FFN_CONV),
        'conv_ffn_b': 0.02 * jax.random.normal(ks[21], (L, 2 * D_FF), f32),
        'w_down': nrm(ks[22], (L, D_FF, D), D_FF),
        'norm_ffn_post': gain(ks[23], D),
        'w_ple': nrm(ks[24], (L, PLE_DIM, D), PLE_DIM),
        'w_ple_gate': nrm(ks[25], (L, D, D), D),
        'norm_ple_post': gain(ks[26], D),
    }

def first_block(x, p, norm_mix_pre, w_in, conv_qkv, a_log, dt_bias, gdn_norm,
              cmp_pos_k, cmp_w1_k, cmp_w2_k, cmp_pos_v, cmp_w1_v, cmp_w2_v,
              w_a2d, w_b2d, w_o, norm_mix_post, norm_ffn_pre, w_up, conv_ffn, conv_ffn_b,
              w_down, norm_ffn_post, w_ple, w_ple_gate, norm_ple_post):
    offs = np.cumsum(IN_SPLITS)[:-1].tolist()
    h = x
    for i in range(DEPTH):
        u = rmsnorm(h, norm_mix_pre[i])
        (qa, ka, va, za, ba, aa, qb, kcm, vcm, ksl, vsl, kwi, vwi, gnsa, gmix) = \
            jnp.split(u @ w_in[i], offs, axis=-1)
        ya = gdn_mixer(qa, ka, va, za, ba, aa, conv_qkv[i], a_log[i], dt_bias[i], gdn_norm[i])
        yb = nsa_mixer(qb, kcm, vcm, ksl, vsl, kwi, vwi, gnsa,
                       cmp_pos_k[i], cmp_w1_k[i], cmp_w2_k[i], cmp_pos_v[i], cmp_w1_v[i], cmp_w2_v[i])
        g_a, g_b = jnp.split(jax.nn.sigmoid(gmix), 2, axis=-1)
        mixed = (g_a * (ya @ w_a2d[i]) + g_b * (yb @ w_b2d[i])) @ w_o[i]
        h = h + rmsnorm(mixed, norm_mix_post[i])
        f = rmsnorm(h, norm_ffn_pre[i]) @ w_up[i]
        f = causal_dwconv(f, conv_ffn[i]) + conv_ffn_b[i]
        f_gate, f_val = jnp.split(f, 2, axis=-1)
        f = (jax.nn.gelu(f_gate) * f_val) @ w_down[i]
        h = h + rmsnorm(f, norm_ffn_post[i])
        e = (p[i] @ w_ple[i]) * jax.nn.sigmoid(h @ w_ple_gate[i])
        h = h + rmsnorm(e, norm_ple_post[i])
    return h


ATTN_HEAD_DIM = 64
ATTN_HEADS = D_MODEL // ATTN_HEAD_DIM
ATTN_KV_HEADS = ATTN_HEADS // 4
ATTN_GROUP = ATTN_HEADS // ATTN_KV_HEADS
WINDOW_2 = 128

MLSTM_HEADS = 8
MLSTM_V_DIM = D_MODEL // MLSTM_HEADS
MLSTM_QK_DIM = MLSTM_V_DIM // 2
MLSTM_CHUNK = 64
CONV_WIDTH = 4
GATE_SOFTCAP = 15.0

D_FF_2 = ((8 * D_MODEL // 3 + 127) // 128) * 128
FFN_RESIDUAL_WEIGHT = 0.5
NORM_EPS = 1e-6

SZ_AQ = ATTN_HEADS * ATTN_HEAD_DIM
SZ_AK = ATTN_KV_HEADS * ATTN_HEAD_DIM
SZ_AV = ATTN_KV_HEADS * ATTN_HEAD_DIM
SZ_MQ = MLSTM_HEADS * MLSTM_QK_DIM
SZ_MK = MLSTM_HEADS * MLSTM_QK_DIM
SZ_MV = MLSTM_HEADS * MLSTM_V_DIM
SZ_MO = MLSTM_HEADS * MLSTM_V_DIM
SZ_MI = MLSTM_HEADS
SZ_MF = MLSTM_HEADS
SZ_GATES = 2 * D_MODEL
SPLIT_POINTS = (
    SZ_AQ,
    SZ_AQ + SZ_AK,
    SZ_AQ + SZ_AK + SZ_AV,
    SZ_AQ + SZ_AK + SZ_AV + SZ_MQ,
    SZ_AQ + SZ_AK + SZ_AV + SZ_MQ + SZ_MK,
    SZ_AQ + SZ_AK + SZ_AV + SZ_MQ + SZ_MK + SZ_MV,
    SZ_AQ + SZ_AK + SZ_AV + SZ_MQ + SZ_MK + SZ_MV + SZ_MO,
    SZ_AQ + SZ_AK + SZ_AV + SZ_MQ + SZ_MK + SZ_MV + SZ_MO + SZ_MI,
    SZ_AQ + SZ_AK + SZ_AV + SZ_MQ + SZ_MK + SZ_MV + SZ_MO + SZ_MI + SZ_MF,
)
F_OFFSET = SPLIT_POINTS[7]
IN_WIDTH = SPLIT_POINTS[8] + SZ_GATES


def rms_norm(x, g):
    xf = x.astype(jnp.float32)
    y = xf * lax.rsqrt(jnp.mean(xf * xf, axis=-1, keepdims=True) + NORM_EPS)
    return (y * g.astype(jnp.float32)).astype(x.dtype)

def swiglu(x, w_gate, w_up, w_down):
    return (jax.nn.silu(x @ w_gate) * (x @ w_up)) @ w_down

def causal_depthwise_conv(x, w):
    s = x.shape[1]
    xp = jnp.pad(x, ((0, 0), (CONV_WIDTH - 1, 0), (0, 0)))
    out = xp[:, 0:s] * w[0]
    for j in range(1, CONV_WIDTH):
        out = out + xp[:, j:j + s] * w[j]
    return out

def sliding_window_attention(q, k, v, sinks):
    b, s = q.shape[0], q.shape[1]
    nb = s // WINDOW_2
    qb = q.reshape(b, nb, WINDOW_2, ATTN_KV_HEADS, ATTN_GROUP, ATTN_HEAD_DIM)

    def band(t):
        tp = jnp.pad(t, ((0, 0), (WINDOW_2, 0), (0, 0), (0, 0)))
        tp = tp.reshape(b, nb + 1, WINDOW_2, ATTN_KV_HEADS, ATTN_HEAD_DIM)
        return jnp.concatenate([tp[:, :-1], tp[:, 1:]], axis=2)

    kb, vb = band(k), band(v)
    scale = ATTN_HEAD_DIM ** -0.5
    scores = jnp.einsum('bnqhgd,bnkhd->bhgnqk', qb, kb).astype(jnp.float32) * scale
    qi = jnp.arange(WINDOW_2)[:, None]
    kj = jnp.arange(2 * WINDOW_2)[None, :]
    in_window = (kj > qi) & (kj <= qi + WINDOW_2)
    is_pad = (jnp.arange(nb)[:, None, None] == 0) & (kj < WINDOW_2)[None]
    valid = in_window[None] & ~is_pad
    scores = jnp.where(valid, scores, -jnp.inf)
    sink = jnp.broadcast_to(
        sinks.astype(jnp.float32).reshape(ATTN_KV_HEADS, ATTN_GROUP)[None, :, :, None, None, None],
        scores.shape[:-1] + (1,))
    probs = jax.nn.softmax(jnp.concatenate([scores, sink], axis=-1), axis=-1)[..., :-1]
    out = jnp.einsum('bhgnqk,bnkhd->bnqhgd', probs.astype(v.dtype), vb)
    return out.reshape(b, s, ATTN_HEADS * ATTN_HEAD_DIM)

def mlstm_chunkwise(q, k, v, i_pre, f_pre):
    b, s = q.shape[0], q.shape[1]
    nc = s // MLSTM_CHUNK
    f32 = jnp.float32

    def to_chunks(t):
        return t.astype(f32).reshape(b, nc, MLSTM_CHUNK, MLSTM_HEADS, t.shape[-1]).transpose(1, 0, 3, 2, 4)

    def gate_chunks(t):
        return t.astype(f32).reshape(b, nc, MLSTM_CHUNK, MLSTM_HEADS).transpose(1, 0, 3, 2)

    qc, kc, vc = to_chunks(q), to_chunks(k), to_chunks(v)
    ic = gate_chunks(i_pre)
    lfc = jax.nn.log_sigmoid(gate_chunks(f_pre))
    causal = jnp.tril(jnp.ones((MLSTM_CHUNK, MLSTM_CHUNK), dtype=bool))

    def step(carry, inp):
        c_prev, n_prev, m_prev = carry
        q_, k_, v_, i_, lf_ = inp
        cum = jnp.cumsum(lf_, axis=-1)
        logw = cum[..., :, None] - cum[..., None, :] + i_[..., None, :]
        logw = jnp.where(causal, logw, -jnp.inf)
        log_inter = cum + m_prev[..., None]
        m_t = jnp.maximum(log_inter, jnp.max(logw, axis=-1))
        w_intra = jnp.exp(logw - m_t[..., None])
        w_inter = jnp.exp(log_inter - m_t)
        sc = jnp.einsum('bhtd,bhsd->bhts', q_, k_) * w_intra
        num = jnp.einsum('bhts,bhsv->bhtv', sc, v_) + w_inter[..., None] * jnp.einsum('bhtd,bhdv->bhtv', q_, c_prev)
        den = jnp.sum(sc, axis=-1) + w_inter * jnp.einsum('bhtd,bhd->bht', q_, n_prev)
        h = num / jnp.maximum(jnp.abs(den), jnp.exp(-m_t))[..., None]
        total = cum[..., -1]
        log_k = total[..., None] - cum + i_
        m_new = jnp.maximum(total + m_prev, jnp.max(log_k, axis=-1))
        wk = jnp.exp(log_k - m_new[..., None])
        decay = jnp.exp(total + m_prev - m_new)
        c_new = decay[..., None, None] * c_prev + jnp.einsum('bhs,bhsd,bhsv->bhdv', wk, k_, v_)
        n_new = decay[..., None] * n_prev + jnp.einsum('bhs,bhsd->bhd', wk, k_)
        return (c_new, n_new, m_new), h

    init = (jnp.zeros((b, MLSTM_HEADS, MLSTM_QK_DIM, MLSTM_V_DIM), f32),
            jnp.zeros((b, MLSTM_HEADS, MLSTM_QK_DIM), f32),
            jnp.zeros((b, MLSTM_HEADS), f32))
    _, hs = lax.scan(step, init, (qc, kc, vc, ic, lfc))
    return hs.transpose(1, 0, 3, 2, 4).reshape(b, s, MLSTM_HEADS, MLSTM_V_DIM)

def softcap(t):
    return GATE_SOFTCAP * jnp.tanh(t / GATE_SOFTCAP)

def second_inputs(seed: int = 0) -> dict:
    key = jax.random.key(seed)
    ks = jax.random.split(key, 24)
    f32 = jnp.float32

    def dense(k, fan_in, fan_out):
        return jax.random.normal(k, (DEPTH, fan_in, fan_out), f32) * fan_in ** -0.5

    def gain(k, shape):
        return 1.0 + 0.05 * jax.random.normal(k, shape, f32)

    b_in = 0.02 * jax.random.normal(ks[7], (DEPTH, IN_WIDTH), f32)
    f_bias = jnp.linspace(3.0, 6.0, MLSTM_HEADS, dtype=f32)
    b_in = b_in.at[:, F_OFFSET:F_OFFSET + SZ_MF].add(f_bias)
    return {
        "x": jax.random.normal(ks[0], (BATCH, SEQ, D_MODEL), f32),
        "ffn1_norm": gain(ks[1], (DEPTH, D_MODEL)),
        "ffn1_w_gate": dense(ks[2], D_MODEL, D_FF_2),
        "ffn1_w_up": dense(ks[3], D_MODEL, D_FF_2),
        "ffn1_w_down": dense(ks[4], D_FF_2, D_MODEL),
        "mix_norm": gain(ks[5], (DEPTH, D_MODEL)),
        "w_in": dense(ks[6], D_MODEL, IN_WIDTH),
        "b_in": b_in,
        "attn_sinks": 0.5 * jax.random.normal(ks[8], (DEPTH, ATTN_HEADS), f32),
        "mlstm_conv": jax.random.normal(ks[9], (DEPTH, CONV_WIDTH, SZ_MQ + SZ_MK), f32) * CONV_WIDTH ** -0.5,
        "mlstm_head_norm": gain(ks[10], (DEPTH, MLSTM_HEADS, MLSTM_V_DIM)),
        "w_proj_attn": dense(ks[11], SZ_AQ, D_MODEL),
        "w_proj_mlstm": dense(ks[12], SZ_MV, D_MODEL),
        "w_out": dense(ks[13], D_MODEL, D_MODEL),
        "ffn2_norm": gain(ks[14], (DEPTH, D_MODEL)),
        "ffn2_w_gate": dense(ks[15], D_MODEL, D_FF_2),
        "ffn2_w_up": dense(ks[16], D_MODEL, D_FF_2),
        "ffn2_w_down": dense(ks[17], D_FF_2, D_MODEL),
        "final_norm": gain(ks[18], (D_MODEL,)),
    }

def second_block(x, ffn1_norm, ffn1_w_gate, ffn1_w_up, ffn1_w_down, mix_norm, w_in, b_in,
              attn_sinks, mlstm_conv, mlstm_head_norm, w_proj_attn, w_proj_mlstm, w_out,
              ffn2_norm, ffn2_w_gate, ffn2_w_up, ffn2_w_down, final_norm):
    b, s, _ = x.shape
    for l in range(DEPTH):
        h = rms_norm(x, ffn1_norm[l])
        x = x + FFN_RESIDUAL_WEIGHT * swiglu(h, ffn1_w_gate[l], ffn1_w_up[l], ffn1_w_down[l])

        h = rms_norm(x, mix_norm[l])
        z = h @ w_in[l] + b_in[l]
        a_q, a_k, a_v, m_q, m_k, m_v, m_o, m_i, m_f, g_pre = jnp.split(z, SPLIT_POINTS, axis=-1)

        y_attn = sliding_window_attention(
            a_q.reshape(b, s, ATTN_HEADS, ATTN_HEAD_DIM),
            a_k.reshape(b, s, ATTN_KV_HEADS, ATTN_HEAD_DIM),
            a_v.reshape(b, s, ATTN_KV_HEADS, ATTN_HEAD_DIM),
            attn_sinks[l]) @ w_proj_attn[l]

        qk = jax.nn.silu(causal_depthwise_conv(jnp.concatenate([m_q, m_k], axis=-1), mlstm_conv[l]))
        mq = qk[..., :SZ_MQ].reshape(b, s, MLSTM_HEADS, MLSTM_QK_DIM)
        mk = qk[..., SZ_MQ:].reshape(b, s, MLSTM_HEADS, MLSTM_QK_DIM) * MLSTM_QK_DIM ** -0.5
        mv = m_v.reshape(b, s, MLSTM_HEADS, MLSTM_V_DIM)
        hm = mlstm_chunkwise(mq, mk, mv,
                             softcap(m_i.astype(jnp.float32)), softcap(m_f.astype(jnp.float32)))
        hm = rms_norm(hm, mlstm_head_norm[l]).reshape(b, s, SZ_MV)
        hm = (jax.nn.sigmoid(m_o.astype(jnp.float32)) * hm).astype(x.dtype)
        y_mlstm = hm @ w_proj_mlstm[l]

        gates = jax.nn.sigmoid(g_pre.astype(jnp.float32)).astype(x.dtype).reshape(b, s, 2, D_MODEL)
        merged = gates[:, :, 0] * y_attn + gates[:, :, 1] * y_mlstm
        x = x + merged @ w_out[l]

        h = rms_norm(x, ffn2_norm[l])
        x = x + FFN_RESIDUAL_WEIGHT * swiglu(h, ffn2_w_gate[l], ffn2_w_up[l], ffn2_w_down[l])
    return rms_norm(x, final_norm)


def setup_inputs(seed=0):
    out = dict(first_inputs(seed))
    for name, value in second_inputs(seed + 1).items():
        if name != "x":
            out[name + "_2"] = value
    return out


def reference(
    x, p, norm_mix_pre, w_in, conv_qkv, a_log, dt_bias, gdn_norm, cmp_pos_k, cmp_w1_k, cmp_w2_k,
    cmp_pos_v, cmp_w1_v, cmp_w2_v, w_a2d, w_b2d, w_o, norm_mix_post, norm_ffn_pre, w_up,
    conv_ffn, conv_ffn_b, w_down, norm_ffn_post, w_ple, w_ple_gate, norm_ple_post, ffn1_norm_2,
    ffn1_w_gate_2, ffn1_w_up_2, ffn1_w_down_2, mix_norm_2, w_in_2, b_in_2, attn_sinks_2,
    mlstm_conv_2, mlstm_head_norm_2, w_proj_attn_2, w_proj_mlstm_2, w_out_2, ffn2_norm_2,
    ffn2_w_gate_2, ffn2_w_up_2, ffn2_w_down_2, final_norm_2,
):
    x = first_block(
        x, p, norm_mix_pre, w_in, conv_qkv, a_log, dt_bias, gdn_norm, cmp_pos_k, cmp_w1_k,
        cmp_w2_k, cmp_pos_v, cmp_w1_v, cmp_w2_v, w_a2d, w_b2d, w_o, norm_mix_post, norm_ffn_pre,
        w_up, conv_ffn, conv_ffn_b, w_down, norm_ffn_post, w_ple, w_ple_gate, norm_ple_post,
    )
    return second_block(
        x, ffn1_norm_2, ffn1_w_gate_2, ffn1_w_up_2, ffn1_w_down_2, mix_norm_2, w_in_2, b_in_2,
        attn_sinks_2, mlstm_conv_2, mlstm_head_norm_2, w_proj_attn_2, w_proj_mlstm_2, w_out_2,
        ffn2_norm_2, ffn2_w_gate_2, ffn2_w_up_2, ffn2_w_down_2, final_norm_2,
    )


_drawn_inputs = setup_inputs


def setup_inputs(seed=0):
    import zlib

    import numpy as np

    out = dict(_drawn_inputs(seed))
    spreads = {}
    factors = {'cmp_pos_k': 8.0,
     'conv_ffn_b': 3.486,
     'ffn1_norm_2': 5.117,
     'mix_norm_2': 4.271,
     'attn_sinks_2': 64.0,
     'mlstm_head_norm_2': 22.84,
     'ffn2_norm_2': 5.483}
    for name, (base, spread) in spreads.items():
        noise = np.random.default_rng([zlib.crc32(name.encode()), seed]).standard_normal(out[name].shape)
        drawn = base * np.exp(spread * noise) if base else spread * noise
        out[name] = __import__('jax').numpy.asarray(drawn.astype(out[name].dtype))
    for name, factor in factors.items():
        out[name] = (out[name] * factor).astype(out[name].dtype)
    return out
```

```python
from contextlib import ExitStack

import numpy as np

import concourse.bass as bass
from concourse import mybir

F32 = mybir.dt.float32
F32R = mybir.dt.float32r
BF16 = mybir.dt.bfloat16
ALU = mybir.AluOpType
ACT = mybir.ActivationFunctionType
AX = mybir.AxisListType

P = 128
S = 512
NT = S // P
D = 1024
DC = D // P
KB = 1024

SLAB = 16
RAWS = 3
SPLITS = 2

GH = 4
LEVELS = 7
NH, NG, ND = 8, 2, 64
CL, CS, NCMP = 32, 16, 31
WH, WKV = 16, 4
MH = 8
FF = 2816
FC = FF // P
EPS = 1e-6
BIG = 3.0e38


def dense_layers():
    a = [("qkv", 12, 8, 0), ("rows1", 1, 8, 0), ("z0", 1, 8, 0), ("z1", 1, 8, 0), ("z2", 1, 8, 0), ("z3", 1, 8, 0),
         ("nq", 4, 8, 0), ("nk", 2, 8, 0), ("ncmp", 4, 8, 0), ("nv", 1, 8, 2),
         ("cmpk", 2, 16, 0), ("cmpv", 2, 16, 0)]
    for m in range(DC):
        a += [(f"gate_a{m}", 1, 8, 0), (f"a2d{m}", 1, 4, 0), (f"gate_b{m}", 1, 8, 0), (f"b2d{m}", 1, 4, 0)]
    a += [("w_o", 8, 8, 0), ("up", 2 * FC, 8, 0), ("down", 8, FC, 0)]
    for m in range(DC):
        a += [(f"ple{m}", 1, 2, 0), (f"ple_gate{m}", 1, 8, 0)]
    a += [("up1", 2 * FC, 8, 0), ("down1", 8, FC, 0),
          ("wq", 8, 8, 0), ("wk", 2, 8, 0), ("wv", 1, 8, 2)]
    for m in range(DC):
        a += [(f"gate_w{m}", 1, 8, 0), (f"proj_w{m}", 1, 8, 0)]
    a += [("mqk", 8, 8, 0), ("rows2", 1, 8, 0), ("mv0", 1, 8, 4), ("mv1", 1, 8, 4), ("mo", 8, 8, 0)]
    for m in range(DC):
        a += [(f"gate_m{m}", 1, 8, 0), (f"proj_m{m}", 1, 8, 0)]
    a += [("out", 8, 8, 0), ("up2", 2 * FC, 8, 0), ("down2", 8, FC, 0)]
    return a


def dense_plan():
    tile = group = 0
    start = {}
    for name, chunks, k, width in dense_layers():
        start[name] = (tile, group)
        tile += chunks * k * (width or 1)
        group += NT if width else chunks
    return start, tile, group


START, TILES, GROUPS = dense_plan()
NSLABS = -(-TILES // SLAB)

VECS = {}


def _vec_layout():
    at = 0
    for name, n in (("mix_pre", 8), ("conv_qkv", 48), ("gdn_norm", 1), ("mix_post", 8), ("ffn_pre", 8),
                    ("conv_ffn", 132), ("conv_ffn_b", 44), ("ffn_post", 8), ("ple_post", 8),
                    ("ffn1", 8), ("mix2", 8), ("b_wq", 8), ("b_wk", 2), ("b_mqk", 8), ("b_mo", 8),
                    ("b_rows2", 1), ("b_gate", 16), ("mconv", 32), ("head_norm", 8), ("ffn2", 8),
                    ("final", 8), ("a_log", 1), ("dt_bias", 1), ("sinks", 16)):
        VECS[name] = at
        at += n
    return at


NVEC = _vec_layout()


def build(nc, t):
    ctx = ExitStack()
    with ctx:
        base = 16512
        sem_names = []

        def at(name, offset, shape, dt=F32):
            return nc.alloc_sbuf_tensor_at(name, [P] + shape, dt, offset=base + offset)

        def sem(name):
            sem_names.append(name)
            return ctx.enter_context(nc.semaphore(name))

        raw = at("raw", 0, [RAWS, SLAB, P])
        w_hi = at("w_hi", 24 * KB, [SPLITS, SLAB, P], F32R)
        w_lo = at("w_lo", 40 * KB, [SPLITS, SLAB, P], F32R)
        h = at("h", 56 * KB, [DC, S])
        u_hi = at("u_hi", 72 * KB, [DC, S], F32R)
        u_lo = at("u_lo", 88 * KB, [DC, S], F32R)
        mo_u = at("mo_u", 72 * KB, [DC, S])
        vec = at("vec", 104 * KB, [448])
        ident = at("ident", 104 * KB + 1792, [P])
        ones = at("ones", 104 * KB + 2304, [P])
        small = at("small", 104 * KB + 2816, [256])
        A = 104 * KB + 3840
        assert NVEC <= 448

        def arena(name, kb, shape, dt=F32):
            return at(name, A + int(kb * KB), shape, dt)

        slot = [arena(f"slot{i}", 88 + 2 * i, [S]) for i in range(6)]

        qkv = arena("qkv", 0, [12, S])
        wk_t = arena("wk_t", 24, [NT, GH, P])
        kt_t = arena("kt_t", 32, [NT, GH, P])
        vb_t = arena("vb_t", 40, [NT, GH, P])
        g_row = arena("g_row", 48, [GH, S])
        b_row = arena("b_row", 56, [GH, S])
        t_inv = arena("t_inv", 56, [NT, GH, P])
        u_inv = arena("u_inv", 16, [NT, GH, P])
        o_t = arena("o_t", 56, [GH, S])
        qk_t = arena("qk_t", 64, [NT, GH, P])
        at_t = arena("at_t", 72, [NT, GH, P])
        wt_t = arena("wt_t", 72, [NT, GH, P])
        am = arena("am", 80, [2, GH, P])
        xs = arena("xs", 84, [2, GH, P])
        dec = arena("dec", 80, [2, GH, P])
        dmask = arena("dmask", 84, [2, GH, P])
        state = arena("state", 80, [2, GH, P])
        u_new = arena("u_new", 84, [2, GH, P])
        a_gate = arena("a_gate", 24, [S])
        b_gate = arena("b_gate", 26, [S])
        sp1 = arena("sp1", 28, [S])
        n_gate = arena("n_gate", 30, [S])
        sp2 = arena("sp2", 32, [S])
        g_sum = arena("g_sum", 34, [S])
        rowmask = arena("rowmask", 40, [S])
        masks = arena("masks", 98, [8, P], BF16)
        masks_in = arena("masks_in", 80, [8, P])
        ya_hi = arena("ya_hi", 0, [4, S], F32R)
        ya_lo = arena("ya_lo", 8, [4, S], F32R)
        cols1 = small[:, 0:32].rearrange("p (t c) -> p t c", t=NT)
        e_col = small[:, 32:48].rearrange("p (t c) -> p t c", t=NT)
        bg_col = small[:, 48:64].rearrange("p (t c) -> p t c", t=NT)
        tail_col = small[:, 64:80].rearrange("p (t c) -> p t c", t=NT)
        gl_col = small[:, 80:96].rearrange("p (t c) -> p t c", t=NT)
        gate_col = small[:, 96:192].rearrange("p (t c) -> p t c", t=NT)
        na_col = small[:, 192:193]

        nq = arena("nq", 16, [4, S])
        nk = arena("nk", 24, [2, S])
        nv = arena("nv", 28, [NT, 256])
        yb_hi = arena("yb_hi", 32, [4, S], F32R)
        yb_lo = arena("yb_lo", 40, [4, S], F32R)
        alibi = arena("alibi", 48, [NH, S])
        z_hi = [arena(f"z_hi{i}", 64 + 8.5 * i, [NG, 528], F32R) for i in range(2)]
        z_lo = [arena(f"z_lo{i}", 68.25 + 8.5 * i, [NG, 528], F32R) for i in range(2)]
        pos = arena("pos", 81, [2, 16, 2])
        pos_hi = arena("pos_hi", 81.25, [2, 16, 2], F32R)
        pos_lo = arena("pos_lo", 81.5, [2, 16, 2], F32R)
        w2 = arena("w2", 82, [2, 2, ND])
        hid = arena("hid", 83, [2, 2, NG, 32])
        kc = arena("kc", 84, [32])
        vc = arena("vc", 84.25, [NG, ND])
        pbias = arena("pbias", 84.75, [4])
        n_s = arena("n_s", 64, [3, S])
        n_pt = arena("n_pt", 70, [2, S])
        c_s = arena("c_s", 74, [NH, NCMP])
        c_pt = arena("c_pt", 76, [NH, P])
        c_bias = arena("c_bias", 88, [NT, NH, NCMP])
        c_mask = arena("c_mask", 92, [NT, NCMP])
        st = arena("st", 93, [64])
        mx_hi = arena("mx_hi", 48, [DC, S], F32R)
        mx_lo = arena("mx_lo", 64, [DC, S], F32R)

        a_hi = arena("a_hi", 0, [FC, S], F32R)
        a_lo = arena("a_lo", 44, [FC, S], F32R)
        p_raw = arena("p_raw", 0, [2, S])
        p_hi = arena("p_hi", 4, [2, S], F32R)
        p_lo = arena("p_lo", 8, [2, S], F32R)
        mo_a = arena("mo_a", 16, [DC, S])

        wq = arena("wq", 0, [8, S])
        wk = arena("wk", 16, [2, S])
        wv = arena("wv", 20, [NT, 256])
        wvb = arena("wvb", 24, [256])
        band = arena("band", 25, [256])
        yw_hi = arena("yw_hi", 26, [8, S], F32R)
        yw_lo = arena("yw_lo", 42, [8, S], F32R)
        w_s = arena("w_s", 58, [3, S])
        w_pt = arena("w_pt", 64, [2, S])
        st2 = arena("st2", 68, [96])
        ma = arena("ma", 0, [DC, S])
        sg = arena("sg", 70, [2, S])
        mqk = arena("mqk", 16, [8, S])
        mv = arena("mv", 32, [NT, 1024])
        mvb = arena("mvb", 80, [1024])
        m_hi = arena("m_hi", 48, [MH, S], F32R)
        m_lo = arena("m_lo", 64, [MH, S], F32R)
        so = arena("so", 64, [MH, S])
        cb2 = arena("cb2", 84, [2, S])
        wsc = arena("wsc", 80, [1280])
        emx = arena("emx", 90, [S])
        em_b = arena("em_b", 92, [S])
        hn = arena("hn", 94, [S])
        msq = arena("msq", 96, [S])
        mr = arena("mr", 98, [S])
        mxr = arena("mxr", 86, [S])
        acol = small[:, 0:32].rearrange("p (t c) -> p t c", t=NT)
        incl2 = small[:, 96:224]
        r_raw = arena("r_raw", 88, [S])
        r_i = arena("r_i", 92, [S])
        r_f = arena("r_f", 94, [S])
        r_one = arena("r_one", 96, [S])
        r_a = arena("r_a", 98, [S])
        mg_hi = arena("mg_hi", 16, [DC, S], F32R)
        mg_lo = arena("mg_lo", 32, [DC, S], F32R)

        result = arena("result", 0, [DC, S])

        bank = [ctx.enter_context(nc.psum_tensor(f"dense{i}", [P, S], F32)) for i in range(4)]
        misc = [ctx.enter_context(nc.psum_tensor(f"misc{i}", [P, S], F32)) for i in range(4)]

        def heads(ps):
            return ps[:, :].rearrange("p (h c) -> p h c", h=GH)

        def V(name, i=0, n=1):
            return vec[:, VECS[name] + i:VECS[name] + i + n]

        w_loaded = [sem(f"w_loaded{i}") for i in range(RAWS)]
        w_part = sem("w_part")
        w_split = sem("w_split")
        w_used = sem("w_used")
        dense_done = sem("dense_done")
        in_loaded = sem("in_loaded")
        x_loaded = sem("x_loaded")
        c1_loaded = sem("c1_loaded")
        c2_loaded = sem("c2_loaded")
        c3_loaded = sem("c3_loaded")
        c4_loaded = sem("c4_loaded")
        p_loaded = sem("p_loaded")
        out_stored = sem("out_stored")
        h_ready = sem("h_ready")
        sq_done = sem("sq_done")
        sq_used = sem("sq_used")
        rt_done = sem("rt_done")
        ux_done = sem("ux_done")
        u_part = sem("u_part")
        u_ready = sem("u_ready")
        po_copy = sem("po_copy")
        po_sq = sem("po_sq")
        po_acc = sem("po_acc")
        po_sum = sem("po_sum")
        po_rt = sem("po_rt")
        cv_lin = sem("cv_lin")
        cv_done = sem("cv_done")
        cv_silu = sem("cv_silu")
        rows1_done = sem("rows1_done")
        sp_done = sem("sp_done")
        sp_exp = sem("sp_exp")
        g_done = sem("g_done")
        tr1_done = sem("tr1_done")
        cols_done = sem("cols_done")
        bc_done = sem("bc_done")
        bc_copied = sem("bc_copied")
        ecol_in = sem("ecol_in")
        ecol_done = sem("ecol_done")
        l2_sq = sem("l2_sq")
        l2_sum = sem("l2_sum")
        l2_rt = sem("l2_rt")
        l2_done = sem("l2_done")
        kv_tr = sem("kv_tr")
        kv_done = sem("kv_done")
        dc_in = sem("dc_in")
        dc_exp = sem("dc_exp")
        kk_done = sem("kk_done")
        at_done = sem("at_done")
        eg_done = sem("eg_done")
        qd_done = sem("qd_done")
        am_done = sem("am_done")
        x_done = sem("x_done")
        xc_done = sem("xc_done")
        txu_done = sem("txu_done")
        t_upd = sem("t_upd")
        u_upd = sem("u_upd")
        wt_done = sem("wt_done")
        wt_copied = sem("wt_copied")
        un_done = sem("un_done")
        un_copied = sem("un_copied")
        og_done = sem("og_done")
        og_copied = sem("og_copied")
        ds_done = sem("ds_done")
        s_upd = sem("s_upd")
        on_sq = sem("on_sq")
        on_sum = sem("on_sum")
        on_rt = sem("on_rt")
        z_silu = sem("z_silu")
        y_done = sem("y_done")
        ya_part = sem("ya_part")
        ya_ready = sem("ya_ready")
        nqk_done = sem("nqk_done")
        nv_done = sem("nv_done")
        zp_zero = sem("zp_zero")
        z_part = sem("z_part")
        z_ready = sem("z_ready")
        pos_part = sem("pos_part")
        pos_ready = sem("pos_ready")
        pb_copied = sem("pb_copied")
        hid_done = sem("hid_done")
        kvc_done = sem("kvc_done")
        kvc_copied = sem("kvc_copied")
        cs_done = sem("cs_done")
        cs_shift = sem("cs_shift")
        cs_exp = sem("cs_exp")
        cp_ready = sem("cp_ready")
        mixa_sig = sem("mixa_sig")
        mix_a = sem("mix_a")
        mix_b = sem("mix_b")
        mx_part = sem("mx_part")
        mx_ready = sem("mx_ready")
        up_lin = sem("up_lin")
        up_conv = sem("up_conv")
        up_act = sem("up_act")
        a_raw = sem("a_raw")
        a_part = sem("a_part")
        a_ready = sem("a_ready")
        ps_part = sem("ps_part")
        ps_ready = sem("ps_ready")
        ple_sig = sem("ple_sig")
        wq_done = sem("wq_done")
        wk_done = sem("wk_done")
        wv_done = sem("wv_done")
        sg_done = sem("sg_done")
        ma_done = sem("ma_done")
        mqk_lin = sem("mqk_lin")
        mqk_b = sem("mqk_b")
        mqk_conv = sem("mqk_conv")
        mqk_silu = sem("mqk_silu")
        mv_done = sem("mv_done")
        so_done = sem("so_done")
        r2_act = sem("r2_act")
        r2_dve = sem("r2_dve")
        ac_tr = sem("ac_tr")
        ac_done = sem("ac_done")
        mb_done = sem("mb_done")
        mdg_in = sem("mdg_in")
        mw_exp = sem("mw_exp")
        msc_done = sem("msc_done")
        mws = sem("mws")
        mnd_done = sem("mnd_done")
        meb_copied = sem("meb_copied")
        mhn = sem("mhn")
        mh_sq = sem("mh_sq")
        mh_sum = sem("mh_sum")
        mh_rt = sem("mh_rt")
        mh_y = sem("mh_y")
        mh_part = sem("mh_part")
        mh_ready = sem("mh_ready")
        mg_in = sem("mg_in")
        mg_part = sem("mg_part")
        mg_ready = sem("mg_ready")
        f_out = sem("f_out")
        act_step = sem("act_step")
        dve_step = sem("dve_step")
        pool_step = sem("pool_step")

        steps = {"act": 0, "dve": 0}

        def act_link(eng, ins):
            steps["act"] += 1
            ins.then_inc(act_step, 1)
            eng.wait_ge(act_step, steps["act"])

        def dve_link(eng, ins):
            steps["dve"] += 1
            ins.then_inc(dve_step, 1)
            eng.wait_ge(dve_step, steps["dve"])

        class Att:
            def __init__(self, tag):
                self.s_done = sem(f"s_done_{tag}")
                self.m_done = sem(f"m_done_{tag}")
                self.e_done = sem(f"e_done_{tag}")
                self.p_done = sem(f"p_done_{tag}")
                self.t_done = sem(f"t_done_{tag}")
                self.t_copied = sem(f"t_copied_{tag}")
                self.pv_done = sem(f"pv_done_{tag}")
                self.o_part = sem(f"o_part_{tag}")
                self.o_ready = sem(f"o_ready_{tag}")

        att = [Att("n"), Att("w")]

        freed = [None] * GROUPS

        def frees(name, s, values):
            g = START[name][1]
            for i, v in enumerate(values):
                freed[g + i] = (s, v)

        frees("qkv", cv_done, [c + 1 for c in range(12)])
        frees("rows1", rows1_done, [3])
        for hd in range(GH):
            frees(f"z{hd}", z_silu, [hd + 1])
        frees("nq", nqk_done, [1, 2, 3, 4])
        frees("nk", nqk_done, [5, 6])
        frees("ncmp", z_ready, [2, 4, 6, 8])
        frees("nv", nv_done, [1, 2, 3, 4])
        frees("cmpk", hid_done, [1, 2])
        frees("cmpv", hid_done, [3, 4])
        for m in range(DC):
            frees(f"gate_a{m}", mixa_sig, [2 * m + 1])
            frees(f"a2d{m}", mix_a, [m + 1])
            frees(f"gate_b{m}", mixa_sig, [2 * m + 2])
            frees(f"b2d{m}", mix_b, [m + 1])
            frees(f"ple_gate{m}", ple_sig, [m + 1])
            frees(f"ple{m}", po_copy, [16 + m + 1])
            frees(f"gate_w{m}", sg_done, [m + 1])
            frees(f"proj_w{m}", ma_done, [m + 1])
            frees(f"gate_m{m}", sg_done, [8 + m + 1])
            frees(f"proj_m{m}", mg_in, [m + 1])
        frees("w_o", po_copy, [m + 1 for m in range(8)])
        frees("down", po_copy, [8 + m + 1 for m in range(8)])
        frees("up", up_conv, [c + 1 for c in range(2 * FC)])
        for n, name in ((0, "up1"), (1, "up2")):
            for c in range(FC):
                frees_at = START[name][1] + 2 * c
                freed[frees_at] = (up_act, FC * (n + 1) + c + 1)
                freed[frees_at + 1] = (a_raw, FC * (n + 1) + c + 1)
        frees("down1", h_ready, [24 + m + 1 for m in range(8)])
        frees("wq", wq_done, [m + 1 for m in range(8)])
        frees("wk", wk_done, [1, 2])
        frees("wv", wv_done, [1, 2, 3, 4])
        frees("mqk", mqk_lin, [m + 1 for m in range(8)])
        frees("rows2", r2_act, [1])
        frees("mv0", mv_done, [1, 2, 3, 4])
        frees("mv1", mv_done, [5, 6, 7, 8])
        frees("mo", so_done, [m + 1 for m in range(8)])
        frees("out", h_ready, [32 + m + 1 for m in range(8)])
        frees("down2", h_ready, [40 + m + 1 for m in range(8)])

        ends = {}
        done = 0
        for name, chunks, k, width in dense_layers():
            tile = START[name][0]
            if width:
                done += NT
                ends[tile + k * width - 1] = done
            else:
                for c in range(chunks):
                    done += 1
                    ends[tile + (c + 1) * k - 1] = done
        slab_used = []
        inside = 0
        for s in range(NSLABS):
            last = s * SLAB + SLAB - 1
            if last in ends or last >= TILES:
                slab_used.append((dense_done, ends.get(last, GROUPS)))
            else:
                inside += 1
                slab_used.append((w_used, inside))

        def group_of(name, m=0):
            return START[name][1] + m + 1

        def out_bank(name, m=0):
            return bank[(START[name][1] + m) % 4]

        block = ctx.enter_context(nc.Block())

        @block.sync
        def _(sp):
            sp.dma_start(h[:, 0:4, :], t["x"][:, 0:4, :]).then_inc(x_loaded, 16)
            sp.dma_start(h[:, 4:8, :], t["x"][:, 4:8, :]).then_inc(x_loaded, 16)
            for s in range(NSLABS):
                if s >= RAWS:
                    sp.wait_ge(w_split, s - RAWS + 1)
                sp.dma_start(raw[:, s % RAWS, :, :], t["weights"][s]).then_inc(w_loaded[s % RAWS], 16)
            for c in range(DC):
                sp.wait_ge(f_out, c + 1)
                sp.dma_start(t["out"][:, c, :], result[:, c, :]).then_inc(out_stored, 16)
            sp.wait_ge(out_stored, 16 * DC)

        @block.gpsimd
        def _(pool):
            for s in range(NSLABS):
                pool.wait_ge(w_loaded[s % RAWS], 16 * (s // RAWS + 1))
                if s >= SPLITS:
                    pool.wait_ge(*slab_used[s - SPLITS])
                nc.gpsimd.tensor_scalar(w_hi[:, s % SPLITS, :, :], raw[:, s % RAWS, :, :], 1.0, None,
                                        ALU.mult).then_inc(w_part, 1)
                pool.wait_ge(w_part, s + 1)
                nc.gpsimd.tensor_tensor(w_lo[:, s % SPLITS, :, :], raw[:, s % RAWS, :, :],
                                        w_hi[:, s % SPLITS, :, :].bitcast(F32),
                                        ALU.subtract).then_inc(w_split, 1)

        @block.tensor
        def _(pe):
            mm = nc.tensor.matmul
            tr = nc.tensor.transpose
            inner = [0]

            def weight(tile, n=1):
                s, j = divmod(tile, SLAB)
                if j == 0:
                    pe.wait_ge(w_split, s + 1)
                return (w_hi[:, s % SPLITS, j:j + n, :].rearrange("p a b -> p (a b)"),
                        w_lo[:, s % SPLITS, j:j + n, :].rearrange("p a b -> p (a b)"))

            def used(ins, tile):
                if tile % SLAB == SLAB - 1 and tile not in ends:
                    inner[0] += 1
                    assert slab_used[tile // SLAB] == (w_used, inner[0])
                    ins.then_inc(w_used, 1)

            def wait_bank(g):
                if g >= 4:
                    pe.wait_ge(*freed[g - 4])

            def dense(name, src_hi, src_lo, k_ready=None, chunks=None):
                tile, g0 = START[name]
                n, k = next((c, k) for nm, c, k, _ in dense_layers() if nm == name)
                for m in range(n):
                    g = g0 + m
                    wait_bank(g)
                    out = bank[g % 4][:, :]
                    for i in range(k):
                        hi, lo = weight(tile)
                        if k_ready and m == 0:
                            pe.wait_ge(k_ready[0], k_ready[1] + i + 1)
                        mm(out, hi, src_hi[:, i, :], start=(i == 0), stop=False)
                        mm(out, hi, src_lo[:, i, :], start=False, stop=False)
                        last = mm(out, lo, src_hi[:, i, :], start=False, stop=(i == k - 1))
                        used(last, tile)
                        tile += 1
                    last.then_inc(dense_done, 1)

            def dense_tokens(name, width):
                tile, g0 = START[name]
                for j in range(NT):
                    wait_bank(g0 + j)
                for i in range(DC):
                    hi, lo = weight(tile, width)
                    for j in range(NT):
                        out = bank[(g0 + j) % 4][:, 0:width * P]
                        a_h, a_l = u_hi[:, i, j * P:(j + 1) * P], u_lo[:, i, j * P:(j + 1) * P]
                        mm(out, a_h, hi, start=(i == 0), stop=False)
                        mm(out, a_h, lo, start=False, stop=False)
                        last = mm(out, a_l, hi, start=False, stop=(i == DC - 1))
                        if i == DC - 1:
                            last.then_inc(dense_done, 1)
                    tile += width
                    if i < DC - 1:
                        used(last, tile - 1)

            def norm_sum(n):
                if n > 0:
                    pe.wait_ge(rt_done, n)
                for c in range(DC):
                    pe.wait_ge(sq_done, DC * n + c + 1)
                    mm(misc[3][:, :], ones[:, :], slot[c % 2][:, :], start=(c == 0),
                       stop=(c == DC - 1)).then_inc(sq_used, 1)

            def post_sum(n):
                pe.wait_ge(po_acc, 7 * n + 7)
                mm(misc[2][:, :], ones[:, :], slot[2][:, :], start=True, stop=True).then_inc(po_sum, 1)

            def gdn():
                pe.wait_ge(g_done, 1)
                pe.wait_ge(rows1_done, 3)
                for j in range(NT):
                    tr(misc[0][:, 8 * j:8 * j + 4], g_sum[0:4, j * P:(j + 1) * P], ident[0:4, 0:4])
                    tr(misc[0][:, 8 * j + 4:8 * j + 8], b_gate[0:4, j * P:(j + 1) * P], ident[0:4, 0:4])
                for j in range(NT):
                    last = tr(misc[0][:, 64 + 24 * j:88 + 24 * j], n_gate[0:24, j * P:(j + 1) * P],
                              ident[0:24, 0:24])
                last.then_inc(tr1_done, 1)
                for i in range(8):
                    src = g_sum if i < 4 else b_gate
                    if i >= 2:
                        pe.wait_ge(bc_copied, i - 1)
                    mm(misc[1 + i % 2][:, :], ident[0:4, i % 4:i % 4 + 1].broadcast_to([4, P]), src[0:4, :],
                       start=True, stop=True).then_inc(bc_done, 1)
                for c in range(8):
                    pe.wait_ge(l2_sq, c + 1)
                    if c >= 2:
                        pe.wait_ge(l2_rt, c - 1)
                    elif c == 1:
                        pe.wait_ge(cols_done, 2)
                        pe.wait_ge(bc_copied, 8)
                    mm(misc[3 * (c % 2)][:, :], ones[:, :], slot[c % 2][:, :], start=True,
                       stop=True).then_inc(l2_sum, 1)
                for j in range(2 * NT):
                    tt = j // 2
                    if j == 0:
                        pe.wait_ge(l2_done, 8)
                        pe.wait_ge(cv_silu, 12)
                    if j >= 2:
                        pe.wait_ge(kv_done, 3 * ((j - 2) // 2) + (3 if j % 2 else 2))
                    for hd in range(GH):
                        last = tr(bank[j % 2][:, hd * P:(hd + 1) * P],
                                  qkv[:, (4 if j % 2 == 0 else 8) + hd, tt * P:(tt + 1) * P], ident[:, :])
                    last.then_inc(kv_tr, 1)
                for tt in range(NT):
                    if tt >= 1:
                        pe.wait_ge(at_done, 3 * tt)
                    for b, c0 in ((0, 4), (1, 0)):
                        for hd in range(GH):
                            ks = qkv[:, 4 + hd, tt * P:(tt + 1) * P]
                            last = mm(bank[2 + b][:, hd * P:(hd + 1) * P], ks,
                                      qkv[:, c0 + hd, tt * P:(tt + 1) * P], start=True, stop=True)
                        last.then_inc(kk_done, 1)
                n_all = LEVELS * NT

                def x_of(n):
                    tt = n % NT
                    pe.wait_ge(am_done, n + 1)
                    if n >= 2:
                        pe.wait_ge(xc_done, n - 1)
                    if n >= NT:
                        pe.wait_ge(t_upd, n - NT + 1)
                    for hd in range(GH):
                        last = mm(bank[n % 2][:, hd * P:(hd + 1) * P], am[:, n % 2, hd, :],
                                  t_inv[:, tt, hd, :], start=True, stop=True)
                    last.then_inc(x_done, 1)

                def tu_of(n):
                    tt, final = n % NT, n >= n_all - NT
                    pe.wait_ge(xc_done, n + 1)
                    if n >= NT:
                        pe.wait_ge(u_upd, n - NT + 1)
                    if n >= 2:
                        pe.wait_ge(u_upd, n - 1)
                    if not final:
                        for hd in range(GH):
                            last = mm(bank[2 + n % 2][:, hd * P:(hd + 1) * P], u_inv[:, tt, hd, :],
                                      xs[:, n % 2, hd, :], start=True, stop=True)
                        last.then_inc(txu_done, 1)
                    for hd in range(GH):
                        last = mm(misc[n % 2][:, hd * P:(hd + 1) * P], xs[:, n % 2, hd, :],
                                  u_inv[:, tt, hd, :], start=True, stop=True)
                    last.then_inc(txu_done, 1)

                x_of(0)
                for n in range(n_all):
                    if n + 1 < n_all:
                        x_of(n + 1)
                    tu_of(n)
                for tt in range(NT):
                    pe.wait_ge(u_upd, n_all - NT + tt + 1)
                    if tt >= 2:
                        pe.wait_ge(wt_copied, tt - 1)
                    for hd in range(GH):
                        last = mm(bank[tt % 2][:, hd * P:(hd + 1) * P], wk_t[:, tt, hd, :],
                                  u_inv[:, tt, hd, :], start=True, stop=True)
                    last.then_inc(wt_done, 1)
                pe.wait_ge(qd_done, 4)
                for tt in range(NT):
                    if tt > 0:
                        pe.wait_ge(s_upd, tt)
                        pe.wait_ge(wt_copied, tt + 1)
                        pe.wait_ge(og_copied, tt)
                    for hd in range(GH):
                        o = bank[2][:, hd * P:(hd + 1) * P]
                        last = mm(o, u_inv[:, tt, hd, :], vb_t[:, tt, hd, :], start=True, stop=(tt == 0))
                        if tt > 0:
                            last = mm(o, wt_t[:, tt, hd, :], state[:, (tt - 1) % 2, hd, :], start=False, stop=True)
                    last.then_inc(un_done, 1)
                    pe.wait_ge(un_copied, tt + 1)
                    if tt < NT - 1:
                        for hd in range(GH):
                            last = mm(bank[3][:, hd * P:(hd + 1) * P], kt_t[:, tt, hd, :],
                                      u_new[:, tt % 2, hd, :], start=True, stop=True)
                        last.then_inc(ds_done, 1)
                    for hd in range(GH):
                        o = misc[2][:, hd * P:(hd + 1) * P]
                        if tt > 0:
                            mm(o, state[:, (tt - 1) % 2, hd, :], qkv[:, hd, tt * P:(tt + 1) * P],
                               start=True, stop=False)
                        last = mm(o, u_new[:, tt % 2, hd, :], qk_t[:, tt, hd, :], start=(tt == 0), stop=True)
                    last.then_inc(og_done, 1)
                for hd in range(GH):
                    pe.wait_ge(on_sq, hd + 1)
                    if hd >= 2:
                        pe.wait_ge(on_rt, hd - 1)
                    mm(misc[hd % 2][:, :], ones[:, :], slot[hd % 2][:, :], start=True, stop=True)\
                        .then_inc(on_sum, 1)
                    dense(f"z{hd}", u_hi, u_lo)

            def compress():
                for b, name in ((0, "cmpk"), (1, "cmpv")):
                    tile, g0 = START[name]
                    pe.wait_ge(z_ready, 4 * b + 4)
                    for m in range(2):
                        g = g0 + m
                        wait_bank(g)
                        out = bank[g % 4][:, 0:64]
                        pout = misc[2 * b + m][:, 0:2]
                        if b == 0 and m == 0:
                            pe.wait_ge(pos_ready, 1)
                        for i in range(16):
                            hi, lo = weight(tile)
                            zh = z_hi[b][:, :, 2 * i:2 * i + 16 * 31 + 1:16]
                            zl = z_lo[b][:, :, 2 * i:2 * i + 16 * 31 + 1:16]
                            f, l = i == 0, i == 15
                            mm(pout, hi, pos_hi[:, b, i, :], start=f, stop=False)
                            mm(pout, hi, pos_lo[:, b, i, :], start=False, stop=False)
                            mm(pout, lo, pos_hi[:, b, i, :], start=False, stop=l)
                            mm(out, hi, zh, start=f, stop=False)
                            mm(out, hi, zl, start=False, stop=False)
                            last = mm(out, lo, zh, start=False, stop=l)
                            used(last, tile)
                            tile += 1
                        last.then_inc(dense_done, 1)
                pe.wait_ge(hid_done, 4)
                for gr in range(NG):
                    for m in range(2):
                        mm(misc[0][gr * ND:(gr + 1) * ND, 0:32], w2[:, 0, m, :], hid[:, 0, m, gr, :],
                           start=(m == 0), stop=(m == 1))
                for gr in range(NG):
                    for m in range(2):
                        last = mm(misc[1][0:32, gr * ND:(gr + 1) * ND], hid[:, 1, m, gr, :], w2[:, 1, m, :],
                                  start=(m == 0), stop=(m == 1))
                last.then_inc(kvc_done, 1)

            def nsa():
                a = att[0]
                items = [(qt, hd, b) for qt in range(NT) for hd in range(NH) for b in range(2)]

                def cmp_scores(qt):
                    if qt >= 1:
                        pe.wait_ge(cs_shift, qt)
                    for hd in range(NH):
                        gr, c = divmod(hd, 4)
                        last = mm(bank[2 + gr][:, c * NCMP:(c + 1) * NCMP],
                                  nq[gr * ND:(gr + 1) * ND, c, qt * P:(qt + 1) * P],
                                  kc[gr * ND:(gr + 1) * ND, 0:NCMP], start=True, stop=True)
                    last.then_inc(cs_done, 1)

                def scores(j):
                    qt, hd, b = items[j]
                    gr, c = divmod(hd, 4)
                    if j >= 2:
                        pe.wait_ge(a.m_done, j - 1)
                    mm(bank[j % 2][:, 0:(qt + 1) * P], nq[gr * ND:(gr + 1) * ND, c, qt * P:(qt + 1) * P],
                       nk[gr * ND:(gr + 1) * ND, b, 0:(qt + 1) * P], start=True, stop=True).then_inc(a.s_done, 1)

                def turn(j):
                    qt = items[j][0]
                    u = 18 * qt + 2 + j % 16
                    pe.wait_ge(a.p_done, j + 1)
                    pe.wait_ge(a.t_copied, u - 1)
                    for kt in range(qt + 1):
                        last = tr(misc[u % 2][:, kt * P:(kt + 1) * P], n_s[:, j % 3, kt * P:(kt + 1) * P], ident[:, :])
                    last.then_inc(a.t_done, 1)

                def cmp_turn(qt):
                    pe.wait_ge(cp_ready, qt + 1)
                    for b in range(2):
                        u = 18 * qt + b
                        if u >= 2:
                            pe.wait_ge(a.t_copied, u - 1)
                        for hd in range(4):
                            last = tr(misc[u % 2][0:NCMP, hd * P:(hd + 1) * P], c_s[:, 4 * b + hd, :], ident[:, :])
                        last.then_inc(a.t_done, 1)

                def values(j):
                    qt, hd, b = items[j]
                    gr, c = divmod(hd, 4)
                    o = misc[2 + qt % 2][gr * ND:(gr + 1) * ND, c * P:(c + 1) * P]
                    pe.wait_ge(a.t_copied, 18 * qt + 2 + j % 16 + 1)
                    if j % 16 == 0 and qt >= 2:
                        pe.wait_ge(a.o_ready, qt - 1)
                    if b == 0:
                        mm(o, vc[0:NCMP, gr, :], c_pt[0:NCMP, hd, :], start=True, stop=False)
                    for kt in range(qt + 1):
                        last = mm(o, nv[:, kt, b * P + gr * ND:b * P + (gr + 1) * ND], n_pt[:, j % 2, kt * P:(kt + 1) * P],
                                  start=False, stop=(b == 1 and kt == qt))
                    last.then_inc(a.pv_done, 1)

                pe.wait_ge(kvc_copied, 2)
                pe.wait_ge(nv_done, 4)
                cmp_scores(0)
                scores(0)
                scores(1)
                for j in range(len(items)):
                    if j + 2 < len(items):
                        scores(j + 2)
                    if j % 16 == 0:
                        if j >= 1:
                            values(j - 1)
                        cmp_turn(j // 16)
                    if j % 16 == 8 and j // 16 + 1 < NT:
                        cmp_scores(j // 16 + 1)
                    turn(j)
                    if j % 16:
                        values(j - 1)
                values(len(items) - 1)

            def window():
                a = att[1]
                items = [(qt, kv, r) for qt in range(NT) for kv in range(WKV) for r in range(4)]

                def scores(j):
                    qt, kv, r = items[j]
                    half, c = kv % 2, kv // 2
                    lo = max(qt - 1, 0) * P
                    if j >= 2:
                        pe.wait_ge(a.m_done, j - 1)
                    mm(bank[j % 2][:, 0:(qt + 1) * P - lo],
                       wq[half * ND:(half + 1) * ND, 4 * c + r, qt * P:(qt + 1) * P],
                       wk[half * ND:(half + 1) * ND, c, lo:(qt + 1) * P], start=True, stop=True).then_inc(a.s_done, 1)

                def turn(j):
                    qt = items[j][0]
                    pe.wait_ge(a.p_done, j + 1)
                    if j >= 2:
                        pe.wait_ge(a.t_copied, j - 1)
                    for kt in range(min(qt + 1, 2)):
                        last = tr(misc[j % 2][:, kt * P:(kt + 1) * P], w_s[:, j % 3, kt * P:(kt + 1) * P], ident[:, :])
                    last.then_inc(a.t_done, 1)

                def values(j):
                    qt, kv, r = items[j]
                    half, c = kv % 2, kv // 2
                    n = min(qt + 1, 2)
                    o = misc[2 + c][half * ND:(half + 1) * ND, r * P:(r + 1) * P]
                    pe.wait_ge(a.t_copied, j + 1)
                    if j % 8 == 0 and j >= 16:
                        pe.wait_ge(a.o_ready, j // 8 - 1)
                    for i in range(n):
                        kt = qt - n + 1 + i
                        last = mm(o, wv[:, kt, kv * ND:(kv + 1) * ND], w_pt[:, j % 2, i * P:(i + 1) * P],
                                  start=(i == 0), stop=(i == n - 1))
                    last.then_inc(a.pv_done, 1)

                pe.wait_ge(wq_done, 8)
                pe.wait_ge(wk_done, 2)
                pe.wait_ge(wv_done, 4)
                scores(0)
                scores(1)
                for j in range(len(items)):
                    if j + 2 < len(items):
                        scores(j + 2)
                    turn(j)
                    if j >= 1:
                        values(j - 1)
                values(len(items) - 1)
                pe.wait_ge(a.o_ready, 8)

            off = [(0, 512, 2, 0), (2, 896, 2, 384), (1, 1024, 3, 0)]

            def mlstm():
                pe.wait_ge(r2_dve, 3)
                for j in range(NT):
                    last = tr(misc[0][:, 8 * j:8 * j + 8], r_a[0:8, j * P:(j + 1) * P], ident[0:8, 0:8])
                last.then_inc(ac_tr, 1)
                pe.wait_ge(mqk_silu, 8)
                pe.wait_ge(mv_done, 8)
                pe.wait_ge(so_done, 8)
                pe.wait_ge(ac_done, 1)
                pe.wait_ge(r2_act, 7)

                def front(hd):
                    c, half = divmod(hd, 2)
                    sel = ident[0:8, hd:hd + 1].broadcast_to([8, P])
                    if hd >= 1:
                        pe.wait_ge(mw_exp, hd)
                        pe.wait_ge(mws, 3 * hd)
                    mm(bank[0][:, :], sel, mxr[0:8, :], start=True, stop=True).then_inc(mb_done, 1)
                    q = lambda a, b: mqk[half * ND:(half + 1) * ND, c, a * P:b * P]
                    k = lambda a: mqk[half * ND:(half + 1) * ND, 4 + c, a * P:(a + 1) * P]
                    for j in range(NT):
                        last = mm(bank[1][:, j * P:(j + 1) * P], k(j), q(j, j + 1), start=True, stop=True)
                    for j, _, b, at_col in off:
                        last = mm(bank[b][:, at_col:at_col + (3 - j) * P], k(j), q(j + 1, NT), start=True, stop=True)
                    last.then_inc(msc_done, 1)

                def back(hd):
                    if hd >= 1:
                        pe.wait_ge(mhn, 2 * hd)
                    mm(misc[2][:, :], ident[0:8, hd:hd + 1].broadcast_to([8, P]), emx[0:8, :],
                       start=True, stop=True).then_inc(mnd_done, 1)
                    pe.wait_ge(mws, 3 * hd + 3)
                    for dst, den in ((1, True), (0, False)):
                        w = lambda j: ones[:, :] if den else mv[:, j, hd * P:(hd + 1) * P]
                        for j in range(NT):
                            mm(misc[dst][:, j * P:(j + 1) * P], w(j), wsc[:, j * P:(j + 1) * P],
                               start=(j == 0), stop=False)
                        for n, (j, at_col, _, _) in enumerate(off):
                            last = mm(misc[dst][:, (j + 1) * P:S], w(j), wsc[:, at_col:at_col + (3 - j) * P],
                                      start=False, stop=(n == 2))
                        last.then_inc(mnd_done, 1)
                    pe.wait_ge(mh_sq, hd + 1)
                    if hd >= 1:
                        pe.wait_ge(mh_rt, hd)
                    mm(misc[3][:, :], ones[:, :], msq[:, :], start=True, stop=True).then_inc(mh_sum, 1)

                for hd in range(MH):
                    front(hd)
                    back(hd)
                pe.wait_ge(mh_ready, 8)

            def ffn(name_up, name_down, n):
                dense(name_up, u_hi, u_lo, (u_ready, DC * (n + 1)))
                dense(name_down, a_hi, a_lo, (a_ready, FC * n))

            pe.wait_ge(in_loaded, 48)
            norm_sum(0)
            dense("qkv", u_hi, u_lo, (u_ready, 0))
            dense("rows1", u_hi, u_lo)
            for g in range(START["qkv"][1] + 9, START["rows1"][1] + 1):
                pe.wait_ge(*freed[g])
            gdn()
            dense("nq", u_hi, u_lo)
            dense("nk", u_hi, u_lo)
            dense("ncmp", u_hi, u_lo)
            dense_tokens("nv", 2)
            pe.wait_ge(ya_ready, 4)
            compress()
            nsa()
            pe.wait_ge(att[0].o_ready, 4)
            for m in range(DC):
                dense(f"gate_a{m}", u_hi, u_lo)
                dense(f"a2d{m}", ya_hi, ya_lo)
                dense(f"gate_b{m}", u_hi, u_lo)
                dense(f"b2d{m}", yb_hi, yb_lo)
            dense("w_o", mx_hi, mx_lo, (mx_ready, 0))
            post_sum(0)
            norm_sum(1)
            ffn("up", "down", 0)
            post_sum(1)
            pe.wait_ge(ps_ready, 2)
            for m in range(DC):
                dense(f"ple{m}", p_hi, p_lo)
                dense(f"ple_gate{m}", u_hi, u_lo, (u_ready, 2 * DC) if m == 0 else None)
            post_sum(2)
            norm_sum(2)
            dense("up1", u_hi, u_lo, (u_ready, 3 * DC))
            dense("down1", a_hi, a_lo, (a_ready, FC))
            norm_sum(3)
            dense("wq", u_hi, u_lo, (u_ready, 4 * DC))
            dense("wk", u_hi, u_lo)
            dense_tokens("wv", 2)
            window()
            for m in range(DC):
                dense(f"gate_w{m}", u_hi, u_lo)
                dense(f"proj_w{m}", yw_hi, yw_lo)
            dense("mqk", u_hi, u_lo)
            dense("rows2", u_hi, u_lo)
            dense_tokens("mv0", 4)
            dense_tokens("mv1", 4)
            dense("mo", u_hi, u_lo)
            mlstm()
            for m in range(DC):
                dense(f"gate_m{m}", u_hi, u_lo)
                dense(f"proj_m{m}", m_hi, m_lo)
            dense("out", mg_hi, mg_lo, (mg_ready, 0))
            norm_sum(4)
            dense("up2", u_hi, u_lo, (u_ready, 5 * DC))
            dense("down2", a_hi, a_lo, (a_ready, 2 * FC))
            norm_sum(5)

        @block.scalar
        def _(act):
            f = nc.scalar.activation

            def norm_act(n, ready, gain_split=True, first=0):
                for c in range(DC):
                    act.wait_ge(ready[0], 32 if ready[0] is x_loaded else ready[1] + c + 1)
                    k = DC * n + c
                    if k >= 2:
                        act.wait_ge(sq_used, k - 1)
                    f(slot[c % 2][:, :], h[:, c, :], ACT.Square).then_inc(sq_done, 1)
                act.wait_ge(sq_used, DC * (n + 1))
                f(slot[3][:, :], misc[3][:, :], ACT.Sqrt, bias=eps_col, scale=1.0 / D).then_inc(rt_done, 1)

            def split_hi(k0):
                for c in range(DC):
                    act.wait_ge(ux_done, k0 + c + 1)
                    f(u_hi[:, c, :], slot[4 + c % 2][:, :], ACT.Copy).then_inc(u_part, 1)

            def post_act(n, name, mo):
                for c in range(DC):
                    if name:
                        act.wait_ge(dense_done, group_of(name, c))
                        f(mo[:, c, :], out_bank(name, c)[:, :], ACT.Copy).then_inc(po_copy, 1)
                        act.wait_ge(po_copy, DC * n + c + 1)
                    post_square(n, c, mo)
                post_root(n)

            def post_square(n, c, mo):
                if c >= 2:
                    act.wait_ge(po_acc, 7 * n + c - 1)
                f(slot[c % 2][:, :], mo[:, c, :], ACT.Square).then_inc(po_sq, 1)

            def post_root(n):
                act.wait_ge(po_sum, n + 1)
                f(slot[3][:, :], misc[2][:, :], ACT.Sqrt, bias=eps_col, scale=1.0 / D).then_inc(po_rt, 1)

            def attention(a, items, s_buf, pt_buf, st_buf, before, outs):
                for j in range(len(items) + 1):
                    if j < len(items):
                        nk_, sink, _ = items[j]
                        before(j)
                        act.wait_ge(a.m_done, j + 1)
                        if j >= 8:
                            act.wait_ge(a.p_done, j - 7)
                        if sink is None:
                            f(s_buf[:, j % 3, 0:nk_], s_buf[:, j % 3, 0:nk_], ACT.Exp, bias=st_buf[:, j % 8:j % 8 + 1],
                              scale=-1.0, accum_out=st_buf[:, 8 + j % 8:9 + j % 8]).then_inc(a.e_done, 1)
                        else:
                            f(st_buf[:, 24 + j % 8:25 + j % 8], sink, ACT.Exp, bias=st_buf[:, j % 8:j % 8 + 1])
                            f(s_buf[:, j % 3, 0:nk_], s_buf[:, j % 3, 0:nk_], ACT.Exp, bias=st_buf[:, j % 8:j % 8 + 1],
                              scale=-1.0, accum_out=st_buf[:, 8 + j % 8:9 + j % 8]).then_inc(a.e_done, 1)
                    if j >= 1:
                        i = j - 1
                        nk_, _, u = items[i]
                        act.wait_ge(a.t_done, u + 1)
                        if i >= 2:
                            act.wait_ge(a.pv_done, i - 1)
                        f(pt_buf[:, i % 2, 0:nk_], misc[u % 2][:, 0:nk_], ACT.Copy).then_inc(a.t_copied, 1)
                        outs(i - 1)
                outs(len(items) - 1)

            def ffn_swiglu(n, name):
                for c in range(FC + 1):
                    if c < FC:
                        k = FC * n + c
                        act.wait_ge(dense_done, group_of(name, 2 * c))
                        if c >= 2:
                            act.wait_ge(a_ready, k - 1)
                        f(slot[c % 2][:, :], out_bank(name, 2 * c)[:, :], ACT.Silu).then_inc(up_act, 1)
                    if c >= 1:
                        act.wait_ge(a_raw, FC * n + c)
                        f(a_hi[:, c - 1, :], slot[(c - 1) % 2][:, :], ACT.Copy).then_inc(a_part, 1)

            eps_col = small[:, 250:251]
            one_col = small[:, 251:252]
            act.dma_start(vec[:, 0:NVEC], t["vec"]).then_inc(in_loaded, 16)
            act.dma_start(ident[:, :], t["ident"]).then_inc(in_loaded, 16)
            act.dma_start(ones[:, :], t["ones"]).then_inc(in_loaded, 16)
            act.dma_start(masks_in[:, :, :], t["masks"]).then_inc(c1_loaded, 16)
            act.dma_start(rowmask[:, :], t["rowmask"]).then_inc(c1_loaded, 16)
            act.wait_ge(pool_step, 2)
            norm_act(0, (x_loaded, 0))
            split_hi(0)

            for c in range(13):
                if c < 12:
                    act.wait_ge(dense_done, group_of("qkv", c))
                    if c >= 2:
                        act.wait_ge(cv_silu, c - 1)
                    f(slot[c % 2][:, :], out_bank("qkv", c)[:, :], ACT.Copy,
                      scale=V("conv_qkv", 4 * c + 3)).then_inc(cv_lin, 1)
                if c >= 1:
                    act.wait_ge(cv_done, c)
                    f(qkv[:, c - 1, :], slot[(c - 1) % 2][:, :], ACT.Silu).then_inc(cv_silu, 1)
            act.wait_ge(dense_done, group_of("rows1"))
            rows = out_bank("rows1")
            f(b_gate[0:4, :], rows[0:4, :], ACT.Sigmoid).then_inc(rows1_done, 1)
            f(n_gate[0:24, :], rows[64:88, :], ACT.Sigmoid).then_inc(rows1_done, 1)
            f(a_gate[0:4, :], rows[32:36, :], ACT.Copy).then_inc(rows1_done, 1)
            act.wait_ge(sp_done, 1)
            act_link(act, f(sp2[0:4, :], sp1[0:4, :], ACT.Exp))
            f(na_col[0:4, :], V("a_log")[0:4, :], ACT.Exp)
            f(sp2[0:4, :], sp2[0:4, :], ACT.Ln, bias=one_col[0:4, :]).then_inc(sp_exp, 1)
            for i in range(8):
                act.wait_ge(bc_done, i + 1)
                dst = g_row if i < 4 else b_row
                f(dst[:, i % 4, :], misc[1 + i % 2][:, :], ACT.Copy).then_inc(bc_copied, 1)
            act.wait_ge(ecol_in, 1)
            f(e_col, cols1[:, :, 0:4], ACT.Exp).then_inc(ecol_done, 1)
            f(tail_col, tail_col, ACT.Exp).then_inc(ecol_done, 1)
            act.wait_ge(bc_copied, 8)
            f(gl_col, g_row[:, :, P - 1::P].rearrange("p h t -> p t h"), ACT.Exp).then_inc(ecol_done, 1)
            act.wait_ge(cv_silu, 12)
            for c in range(9):
                if c < 8:
                    if c >= 2:
                        act.wait_ge(l2_sum, c - 1)
                    f(slot[c % 2][:, :], qkv[:, c, :], ACT.Square).then_inc(l2_sq, 1)
                if c >= 1:
                    act.wait_ge(l2_sum, c)
                    if c >= 3:
                        act.wait_ge(l2_done, c - 2)
                    f(slot[2 + (c - 1) % 2][:, :], misc[3 * ((c - 1) % 2)][:, :], ACT.Sqrt,
                      bias=eps_col).then_inc(l2_rt, 1)
            for tt in range(NT):
                act.wait_ge(dc_in, tt + 1)
                f(dec[:, tt % 2, :, :], dec[:, tt % 2, :, :], ACT.Exp).then_inc(dc_exp, 1)
            act.wait_ge(dc_in, NT)
            act.wait_ge(kv_done, 12)
            for hd in range(GH):
                f(g_row[:, hd, :], g_row[:, hd, :], ACT.Exp).then_inc(eg_done, 1)
            for n in range(LEVELS * NT):
                act.wait_ge(x_done, n + 1)
                if n >= 2:
                    act.wait_ge(u_upd, n - 1)
                else:
                    act.wait_ge(at_done, 12)
                f(xs[:, n % 2, :, :], heads(bank[n % 2]), ACT.Copy).then_inc(xc_done, 1)
            for tt in range(NT):
                act.wait_ge(wt_done, tt + 1)
                f(wt_t[:, tt, :, :], heads(bank[tt % 2]), ACT.Copy, scale=-1.0).then_inc(wt_copied, 1)
            for tt in range(NT):
                act.wait_ge(un_done, tt + 1)
                f(u_new[:, tt % 2, :, :], heads(bank[2]), ACT.Copy).then_inc(un_copied, 1)
                act.wait_ge(og_done, tt + 1)
                f(o_t[:, :, tt * P:(tt + 1) * P], heads(misc[2]), ACT.Copy).then_inc(og_copied, 1)
            act.wait_ge(og_copied, NT)
            for hd in range(GH + 2):
                if hd < GH:
                    if hd >= 2:
                        act.wait_ge(on_sum, hd - 1)
                    f(slot[hd % 2][:, :], o_t[:, hd, :], ACT.Square).then_inc(on_sq, 1)
                i = hd - 1
                if 0 <= i < GH:
                    act.wait_ge(on_sum, i + 1)
                    if i >= 2:
                        act.wait_ge(y_done, i - 1)
                    f(slot[2 + i % 2][:, :], misc[i % 2][:, :], ACT.Sqrt, bias=eps_col, scale=1.0 / P).then_inc(on_rt, 1)
                    act.wait_ge(dense_done, group_of(f"z{i}"))
                    f(xs[:, i % 2, :, :].rearrange("p a b -> p (a b)"), out_bank(f"z{i}")[:, :],
                      ACT.Silu).then_inc(z_silu, 1)
                if i >= 1:
                    act.wait_ge(y_done, i)
                    f(ya_hi[:, i - 1, :], o_t[:, i - 1, :], ACT.Copy).then_inc(ya_part, 1)

            act.wait_ge(ya_ready, 4)
            act.dma_start(alibi[:, :, :], t["alibi"]).then_inc(c2_loaded, 16)
            act.dma_start(pos[:, :, :, :], t["pos"]).then_inc(c2_loaded, 16)
            act.dma_start(w2[:, :, :, :], t["w2"]).then_inc(c2_loaded, 16)
            act.dma_start(c_bias[:, :, :, :], t["c_bias"]).then_inc(c2_loaded, 16)
            act.dma_start(c_mask[:, :, :], t["c_mask"]).then_inc(c2_loaded, 16)
            for c in range(4):
                act.wait_ge(dense_done, group_of("nq", c))
                f(nq[:, c, :], out_bank("nq", c)[:, :], ACT.Copy, scale=ND ** -0.5).then_inc(nqk_done, 1)
            for c in range(2):
                act.wait_ge(dense_done, group_of("nk", c))
                f(nk[:, c, :], out_bank("nk", c)[:, :], ACT.Copy).then_inc(nqk_done, 1)
            act.wait_ge(zp_zero, 2)
            for c in range(4):
                b, gr = divmod(c, 2)
                act.wait_ge(dense_done, group_of("ncmp", c))
                ps = out_bank("ncmp", c)
                f(z_hi[b][0:ND, gr, 0:S], ps[0:ND, :], ACT.Copy).then_inc(z_part, 1)
                f(z_hi[b][ND:P, gr, 0:S - 1], ps[ND:P, 1:S], ACT.Copy).then_inc(z_part, 1)
            for j in range(NT):
                act.wait_ge(dense_done, group_of("nv", j))
                f(nv[:, j, :], out_bank("nv", j)[:, 0:256], ACT.Copy).then_inc(nv_done, 1)
            act.wait_ge(c2_loaded, 80)
            f(pos_hi[:, :, :, :], pos[:, :, :, :], ACT.Copy).then_inc(pos_part, 1)
            for i in range(4):
                b, m = divmod(i, 2)
                act.wait_ge(dense_done, group_of(("cmpk", "cmpv")[b], m))
                f(pbias[:, i:i + 1], misc[i][:, 0:1], ACT.Copy).then_inc(pb_copied, 1)
                act.wait_ge(pb_copied, i + 1)
                f(hid[:, b, m, :, :].rearrange("p a b -> p (a b)"), out_bank(("cmpk", "cmpv")[b], m)[:, 0:64],
                  ACT.Gelu_apprx_tanh, bias=pbias[:, i:i + 1]).then_inc(hid_done, 1)
            act.wait_ge(kvc_done, 1)
            f(kc[:, :], misc[0][:, 0:32], ACT.Copy).then_inc(kvc_copied, 1)
            f(vc[0:32, :, :].rearrange("p a b -> p (a b)"), misc[1][0:32, 0:P], ACT.Copy).then_inc(kvc_copied, 1)

            a0 = att[0]

            def nsa_before(j):
                if j % 16 == 0:
                    qt = j // 16
                    act.wait_ge(cs_shift, qt + 1)
                    f(c_s[:, :, :], c_s[:, :, :], ACT.Exp).then_inc(cs_exp, 1)

            def nsa_outs(i):
                if i >= 0 and i % 16 == 15:
                    qt = i // 16
                    act.wait_ge(a0.pv_done, i + 1)
                    f(yb_hi[:, :, qt * P:(qt + 1) * P], heads(misc[2 + qt % 2]), ACT.Copy).then_inc(a0.o_part, 1)

            def cmp_copy(qt):
                for b in range(2):
                    u = 18 * qt + b
                    act.wait_ge(a0.t_done, u + 1)
                    if qt >= 1:
                        act.wait_ge(a0.pv_done, 16 * qt)
                    f(c_pt[0:NCMP, 4 * b:4 * b + 4, :].rearrange("p a b -> p (a b)"), misc[u % 2][0:NCMP, :],
                      ACT.Copy).then_inc(a0.t_copied, 1)

            items = []
            for qt in range(NT):
                for n in range(16):
                    items.append(((qt + 1) * P, None, 18 * qt + 2 + n))
            for j in range(65):
                if j < 64:
                    nsa_before(j)
                    act.wait_ge(a0.m_done, j + 1)
                    f(n_s[:, j % 3, 0:items[j][0]], n_s[:, j % 3, 0:items[j][0]], ACT.Exp,
                      bias=st[:, j % 8:j % 8 + 1], scale=-1.0,
                      accum_out=st[:, 8 + j % 8:9 + j % 8]).then_inc(a0.e_done, 1)
                if j >= 1:
                    i = j - 1
                    nk_, _, u = items[i]
                    if i % 16 == 0:
                        if i >= 1:
                            nsa_outs(i - 1)
                        cmp_copy(i // 16)
                    act.wait_ge(a0.t_done, u + 1)
                    if i >= 2:
                        act.wait_ge(a0.pv_done, i - 1)
                    f(n_pt[:, i % 2, 0:nk_], misc[u % 2][:, 0:nk_], ACT.Copy).then_inc(a0.t_copied, 1)
            nsa_outs(63)

            for m in range(DC):
                for b, nm in ((0, "gate_a"), (1, "gate_b")):
                    act.wait_ge(dense_done, group_of(f"{nm}{m}"))
                    if m >= 1:
                        act.wait_ge((mix_a, mix_b)[b], m)
                    f(slot[b][:, :], out_bank(f"{nm}{m}")[:, :], ACT.Sigmoid).then_inc(mixa_sig, 1)
                act.wait_ge(mix_b, m + 1)
                f(mx_hi[:, m, :], slot[4 + m % 2][:, :], ACT.Copy).then_inc(mx_part, 1)
            act.wait_ge(mx_ready, 8)
            post_act(0, "w_o", mo_u)
            norm_act(1, (h_ready, 0))
            split_hi(8)

            act.wait_ge(u_ready, 16)
            for c in range(FC + 1):
                if c < FC:
                    for b in range(2):
                        g = b * FC + c
                        act.wait_ge(dense_done, group_of("up", 2 * c + b))
                        if c >= 2:
                            act.wait_ge(a_ready, c - 1)
                        f(slot[2 * b + c % 2][:, :], out_bank("up", 2 * c + b)[:, :], ACT.Identity,
                          bias=V("conv_ffn_b", g), scale=V("conv_ffn", 3 * g + 2)).then_inc(up_lin, 1)
                    act.wait_ge(up_conv, 2 * c + 1)
                    f(slot[c % 2][:, :], slot[c % 2][:, :], ACT.Gelu_apprx_tanh).then_inc(up_act, 1)
                if c >= 1:
                    act.wait_ge(a_raw, c)
                    f(a_hi[:, c - 1, :], slot[2 + (c - 1) % 2][:, :], ACT.Copy).then_inc(a_part, 1)
            act.wait_ge(a_ready, FC)
            post_act(1, "down", mo_u)
            act.dma_start(p_raw[:, :, :], t["p"]).then_inc(p_loaded, 16)
            act.wait_ge(p_loaded, 16)
            for c in range(2):
                f(p_hi[:, c, :], p_raw[:, c, :], ACT.Copy).then_inc(ps_part, 1)
            for c in range(DC):
                act.wait_ge(h_ready, 8 + c + 1)
                f(u_hi[:, c, :], h[:, c, :], ACT.Copy).then_inc(u_part, 1)
            for m in range(DC):
                act.wait_ge(dense_done, group_of(f"ple_gate{m}"))
                if m >= 2:
                    act.wait_ge(po_copy, 16 + m - 1)
                f(slot[4 + m % 2][:, :], out_bank(f"ple_gate{m}")[:, :], ACT.Sigmoid).then_inc(ple_sig, 1)
                act.wait_ge(po_copy, 16 + m + 1)
                post_square(2, m, mo_a)
            post_root(2)
            norm_act(2, (h_ready, 16))
            split_hi(16)
            act.wait_ge(u_ready, 32)
            ffn_swiglu(1, "up1")
            norm_act(3, (h_ready, 24))
            split_hi(24)
            act.dma_start(wvb[:, :], t["wvb"]).then_inc(c3_loaded, 16)
            act.dma_start(band[:, :], t["band"]).then_inc(c3_loaded, 16)
            for c in range(2):
                act.wait_ge(dense_done, group_of("wk", c))
                f(wk[:, c, :], out_bank("wk", c)[:, :], ACT.Identity, bias=V("b_wk", c)).then_inc(wk_done, 1)
            items2 = []
            for qt in range(NT):
                for kv in range(WKV):
                    for r in range(4):
                        items2.append((min(qt + 1, 2) * P, V("sinks", 4 * kv + r), len(items2)))

            def win_outs(i):
                if i >= 0 and i % 8 == 7:
                    qt, c = divmod(i // 8, 2)
                    act.wait_ge(att[1].pv_done, i + 1)
                    f(yw_hi[:, 4 * c:4 * c + 4, qt * P:(qt + 1) * P], heads(misc[2 + c]), ACT.Copy)\
                        .then_inc(att[1].o_part, 1)

            attention(att[1], items2, w_s, w_pt, st2, lambda j: None, win_outs)
            for m in range(DC):
                act.wait_ge(dense_done, group_of(f"gate_w{m}"))
                if m >= 2:
                    act.wait_ge(ma_done, m - 1)
                f(sg[:, m % 2, :], out_bank(f"gate_w{m}")[:, :], ACT.Sigmoid, bias=V("b_gate", m)).then_inc(sg_done, 1)
            act.wait_ge(ma_done, 8)
            act.dma_start(mvb[:, :], t["mvb"]).then_inc(c4_loaded, 16)
            act.dma_start(incl2, t["incl"]).then_inc(c4_loaded, 16)
            for c in range(9):
                if c < 8:
                    act.wait_ge(dense_done, group_of("mqk", c))
                    if c >= 2:
                        act.wait_ge(mqk_conv, c - 1)
                    f(slot[c % 2][:, :], out_bank("mqk", c)[:, :], ACT.Identity, bias=V("b_mqk", c)).then_inc(mqk_lin, 1)
                if c >= 1:
                    act.wait_ge(mqk_conv, c)
                    f(mqk[:, c - 1, :], cb2[:, (c - 1) % 2, :], ACT.Silu).then_inc(mqk_silu, 1)
            act.wait_ge(dense_done, group_of("rows2"))
            act.wait_ge(mqk_conv, 8)
            f(r_raw[0:40, :], out_bank("rows2")[0:40, :], ACT.Identity, bias=V("b_rows2")[0:40, :]).then_inc(r2_act, 1)
            act.wait_ge(r2_act, 1)
            f(r_i[0:8, :], r_raw[0:8, :], ACT.Tanh, scale=1.0 / 15.0).then_inc(r2_act, 1)
            f(r_f[0:8, :], r_raw[32:40, :], ACT.Tanh, scale=1.0 / 15.0).then_inc(r2_act, 1)
            act.wait_ge(r2_act, 3)
            f(r_f[0:8, :], r_f[0:8, :], ACT.Exp, scale=-15.0).then_inc(r2_act, 1)
            act.wait_ge(r2_act, 4)
            f(r_f[0:8, :], r_f[0:8, :], ACT.Ln, bias=one_col[0:8, :]).then_inc(r2_act, 1)
            for c in range(8):
                act.wait_ge(dense_done, group_of("mo", c))
                f(so[:, c, :], out_bank("mo", c)[:, :], ACT.Sigmoid, bias=V("b_mo", c)).then_inc(so_done, 1)
            act.wait_ge(r2_dve, 5)
            f(emx[0:8, :], r_raw[0:8, :], ACT.Exp, scale=-1.0).then_inc(r2_act, 1)
            act.wait_ge(mqk_silu, 8)
            f(mxr[0:8, :], r_f[0:8, :], ACT.Copy).then_inc(r2_act, 1)
            off = [(0, 512), (2, 896), (1, 1024)]
            for hd in range(MH):
                act.wait_ge(mb_done, hd + 1)
                act.wait_ge(ac_done, 1)
                if hd >= 1:
                    act.wait_ge(mnd_done, 3 * hd)
                else:
                    act.wait_ge(mv_done, 8)
                act.wait_ge(mdg_in, hd + 1)
                for j, at_col in off:
                    f(wsc[:, at_col:at_col + (3 - j) * P], bank[0][:, (j + 1) * P:S], ACT.Exp,
                      bias=acol[:, j, hd:hd + 1], scale=-1.0)
                f(wsc[:, 0:S], wsc[:, 0:S], ACT.Exp, scale=-1.0).then_inc(mw_exp, 1)
                act.wait_ge(mnd_done, 3 * hd + 1)
                f(em_b[:, :], misc[2][:, :], ACT.Copy).then_inc(meb_copied, 1)
                act.wait_ge(mhn, 2 * hd + 2)
                f(msq[:, :], hn[:, :], ACT.Square).then_inc(mh_sq, 1)
                act.wait_ge(mh_sum, hd + 1)
                f(mr[:, :], misc[3][:, :], ACT.Sqrt, bias=eps_col, scale=1.0 / P).then_inc(mh_rt, 1)
                act.wait_ge(mh_y, hd + 1)
                f(m_hi[:, hd, :], hn[:, :], ACT.Copy).then_inc(mh_part, 1)
            for m in range(DC):
                act.wait_ge(dense_done, group_of(f"gate_m{m}"))
                if m >= 1:
                    act.wait_ge(mg_in, m)
                else:
                    act.wait_ge(mh_ready, 8)
                f(slot[m % 2][:, :], out_bank(f"gate_m{m}")[:, :], ACT.Sigmoid, bias=V("b_gate", 8 + m)).then_inc(sg_done, 1)
                act.wait_ge(mg_in, m + 1)
                f(mg_hi[:, m, :], ma[:, m, :], ACT.Copy).then_inc(mg_part, 1)
            norm_act(4, (h_ready, 32))
            split_hi(32)
            act.wait_ge(u_ready, 48)
            ffn_swiglu(2, "up2")
            norm_act(5, (h_ready, 40))

        @block.vector
        def _(dve):
            v = nc.vector
            TT, TS, STT = v.tensor_tensor, v.tensor_scalar, v.scalar_tensor_tensor

            def norm_apply(n, gain, k0):
                dve.wait_ge(rt_done, n + 1)
                dve_link(dve, v.reciprocal(slot[3][:, :], slot[3][:, :]))
                for c in range(DC + 1):
                    if c < DC:
                        if c >= 2:
                            dve.wait_ge(u_ready, k0[1] + c - 1)
                        STT(slot[4 + c % 2][:, :], h[:, c, :], V(gain, c), slot[3][:, :], ALU.mult, ALU.mult)\
                            .then_inc(ux_done, 1)
                    if c >= 1:
                        dve.wait_ge(u_part, k0[1] + c)
                        TT(u_lo[:, c - 1, :], slot[4 + (c - 1) % 2][:, :], u_hi[:, c - 1, :].bitcast(F32),
                           ALU.subtract).then_inc(u_ready, 1)

            def post_add(n):
                dve.wait_ge(po_sq, DC * n + 2)
                TT(slot[2][:, :], slot[0][:, :], slot[1][:, :], ALU.add).then_inc(po_acc, 1)
                for c in range(2, DC):
                    post_add_one(n, c)

            def post_add_one(n, c):
                dve.wait_ge(po_sq, DC * n + c + 1)
                dve.wait_ge(po_acc, 7 * n + c - 1)
                TT(slot[2][:, :], slot[2][:, :], slot[c % 2][:, :], ALU.add).then_inc(po_acc, 1)

            def post_apply(n, gain, mo):
                dve.wait_ge(po_rt, n + 1)
                dve_link(dve, v.reciprocal(slot[3][:, :], slot[3][:, :]))
                for c in range(DC + 1):
                    if c < DC:
                        if c >= 2:
                            dve.wait_ge(h_ready, DC * n + c - 1)
                        STT(slot[4 + c % 2][:, :], mo[:, c, :], V(gain, c), slot[3][:, :], ALU.mult, ALU.mult)\
                            .then_inc(dve_step, 1)
                        steps["dve"] += 1
                    if c >= 1:
                        dve.wait_ge(dve_step, steps["dve"] - (1 if c < DC else 0))
                        TT(h[:, c - 1, :], h[:, c - 1, :], slot[4 + (c - 1) % 2][:, :], ALU.add).then_inc(h_ready, 1)

            def attention(a, items, s_buf, st_buf, between):
                def biased(j):
                    bias, init, _, nk_ = items[j]
                    dve.wait_ge(a.s_done, j + 1)
                    if j >= 3:
                        dve.wait_ge(a.t_done, between(j - 3))
                    v.tensor_tensor_reduce(s_buf[:, j % 3, 0:nk_], bank[j % 2][:, 0:nk_], bias, -1.0, init,
                                           ALU.add, ALU.min, st_buf[:, j % 8:j % 8 + 1]).then_inc(a.m_done, 1)

                def norm(j):
                    _, init, gate, nk_ = items[j]
                    dve.wait_ge(a.e_done, j + 1)
                    den = st_buf[:, 8 + j % 8:9 + j % 8]
                    if gate is None:
                        dve_link(dve, TT(den, den, st_buf[:, 24 + j % 8:25 + j % 8], ALU.add))
                    dve_link(dve, v.reciprocal(st_buf[:, 16 + j % 8:17 + j % 8], den))
                    r = st_buf[:, 16 + j % 8:17 + j % 8]
                    if gate is None:
                        ins = TS(s_buf[:, j % 3, 0:nk_], s_buf[:, j % 3, 0:nk_], r, None, ALU.mult)
                    else:
                        ins = TS(s_buf[:, j % 3, 0:nk_], s_buf[:, j % 3, 0:nk_], r, gate, ALU.mult, ALU.mult)
                    ins.then_inc(a.p_done, 1)
                return biased, norm

            def ffn_gate(n, name):
                for c in range(FC + 1):
                    if c < FC:
                        dve.wait_ge(dense_done, group_of(name, 2 * c + 1))
                        dve.wait_ge(up_act, FC * n + c + 1)
                        TT(slot[c % 2][:, :], slot[c % 2][:, :], out_bank(name, 2 * c + 1)[:, :], ALU.mult)\
                            .then_inc(a_raw, 1)
                    if c >= 1:
                        dve.wait_ge(a_part, FC * n + c)
                        TT(a_lo[:, c - 1, :], slot[(c - 1) % 2][:, :], a_hi[:, c - 1, :].bitcast(F32),
                           ALU.subtract).then_inc(a_ready, 1)

            def add_half(name, scale):
                for c in range(DC):
                    dve.wait_ge(dense_done, group_of(name, c))
                    STT(h[:, c, :], out_bank(name, c)[:, :], scale, h[:, c, :], ALU.mult, ALU.add).then_inc(h_ready, 1)

            v.memset(small[:, 250:251], EPS).then_inc(pool_step, 1)
            v.memset(small[:, 251:252], 1.0).then_inc(pool_step, 1)
            dve.wait_ge(in_loaded, 48)
            dve.wait_ge(x_loaded, 32)
            norm_apply(0, "mix_pre", (0, 0))
            for c in range(12):
                dve.wait_ge(cv_lin, c + 1)
                src, dst = out_bank("qkv", c), slot[c % 2]
                for n, tap in ((1, 2), (2, 1), (3, 0)):
                    ins = STT(dst[:, n:S], src[:, 0:S - n], V("conv_qkv", 4 * c + tap), dst[:, n:S], ALU.mult, ALU.add)
                    if n < 3:
                        dve_link(dve, ins)
                ins.then_inc(cv_done, 1)
            dve.wait_ge(c1_loaded, 32)
            dve.wait_ge(u_ready, 8)
            dve_link(dve, v.tensor_copy(masks[:, :, :], masks_in[:, :, :]))
            dve.wait_ge(rows1_done, 3)
            dve_link(dve, TS(a_gate[0:4, :], a_gate[0:4, :], V("dt_bias")[0:4, :], None, ALU.add))
            STT(sp1[0:4, :], a_gate[0:4, :], -1.0, a_gate[0:4, :], ALU.mult, ALU.min).then_inc(sp_done, 1)
            dve.wait_ge(sp_exp, 1)
            dve_link(dve, STT(sp2[0:4, :], a_gate[0:4, :], 0.0, sp2[0:4, :], ALU.max, ALU.add))
            dve_link(dve, TS(sp2[0:4, :], sp2[0:4, :], na_col[0:4, :], -1.0, ALU.mult, ALU.mult))
            dve.wait_ge(c1_loaded, 32)
            v.tensor_tensor_scan(g_sum[0:4, :], rowmask[0:4, :], sp2[0:4, :], 0.0, ALU.mult, ALU.add)\
                .then_inc(g_done, 1)
            dve.wait_ge(tr1_done, 1)
            v.tensor_copy(small[:, 0:32], misc[0][:, 0:32]).then_inc(cols_done, 1)
            v.tensor_copy(small[:, 96:192], misc[0][:, 64:160]).then_inc(cols_done, 1)
            dve.wait_ge(bc_copied, 4)
            dve.wait_ge(cols_done, 2)
            TT(tail_col, g_row[:, :, P - 1::P].rearrange("p h t -> p t h"), cols1[:, :, 0:4], ALU.subtract)\
                .then_inc(ecol_in, 1)
            dve.wait_ge(ecol_done, 3)
            dve_link(dve, TT(bg_col, e_col, cols1[:, :, 4:8], ALU.mult))
            for c in range(8):
                dve.wait_ge(l2_rt, c + 1)
                dve_link(dve, v.reciprocal(slot[2 + c % 2][:, :], slot[2 + c % 2][:, :]))
                STT(qkv[:, c, :], qkv[:, c, :], P ** -0.5 if c < 4 else 1.0, slot[2 + c % 2][:, :], ALU.mult,
                    ALU.mult).then_inc(l2_done, 1)

            def wide(col, tt):
                return col[:, tt, :].unsqueeze(2).broadcast_to([P, GH, P])

            for tt in range(NT):
                dve.wait_ge(kv_tr, 2 * tt + 1)
                TT(wk_t[:, tt, :, :], heads(bank[0]), wide(bg_col, tt), ALU.mult).then_inc(kv_done, 1)
                TT(kt_t[:, tt, :, :], heads(bank[0]), wide(tail_col, tt), ALU.mult).then_inc(kv_done, 1)
                dve.wait_ge(kv_tr, 2 * tt + 2)
                TT(vb_t[:, tt, :, :], heads(bank[1]), wide(cols1[:, :, 4:8], tt), ALU.mult).then_inc(kv_done, 1)

            def head_mask(i):
                return masks[:, i, :].unsqueeze(1).broadcast_to([P, GH, P])

            for tt in range(NT):
                cut = slice(tt * P, (tt + 1) * P)
                for hd in range(GH):
                    ins = TS(dec[:, tt % 2, hd, :], g_row[:, hd, cut], cols1[:, tt, hd:hd + 1], 0.0, ALU.subtract, ALU.min)
                ins.then_inc(dc_in, 1)
                dve.wait_ge(dc_exp, tt + 1)
                dve_link(dve, TT(dmask[:, tt % 2, :, :], dec[:, tt % 2, :, :], head_mask(7), ALU.mult))
                dve.wait_ge(kk_done, 2 * tt + 1)
                TT(at_t[:, tt, :, :], heads(bank[2]), dmask[:, tt % 2, :, :], ALU.mult).then_inc(at_done, 1)
                dve.wait_ge(kk_done, 2 * tt + 2)
                TT(qk_t[:, tt, :, :], heads(bank[3]), dmask[:, tt % 2, :, :], ALU.mult).then_inc(at_done, 1)
                dve.wait_ge(at_done, 3 * tt + 1)
                TT(at_t[:, tt, :, :], at_t[:, tt, :, :], b_row[:, :, cut], ALU.mult).then_inc(at_done, 1)
            dve.wait_ge(at_done, 12)
            eye = ident[:, :].unsqueeze(1).broadcast_to([P, GH, P])
            for tt in range(NT):
                v.tensor_copy(t_inv[:, tt, :, :], eye)
                dve_link(dve, v.tensor_copy(u_inv[:, tt, :, :], eye))
            for hd in range(GH):
                dve.wait_ge(eg_done, hd + 1)
                TT(qkv[:, hd, :], qkv[:, hd, :], g_row[:, hd, :], ALU.mult).then_inc(qd_done, 1)

            def level_cut(n):
                if n >= 2:
                    dve.wait_ge(x_done, n - 1)
                TT(am[:, n % 2, :, :], at_t[:, n % NT, :, :], head_mask(n // NT), ALU.mult).then_inc(am_done, 1)

            n_all = LEVELS * NT
            level_cut(0)
            for n in range(n_all):
                tt, final = n % NT, n >= n_all - NT
                if n + 1 < n_all:
                    level_cut(n + 1)
                k = 2 * n if not final else 2 * (n_all - NT) + (n - (n_all - NT))
                if not final:
                    dve.wait_ge(txu_done, k + 1)
                    TT(t_inv[:, tt, :, :], t_inv[:, tt, :, :], heads(bank[2 + n % 2]), ALU.subtract).then_inc(t_upd, 1)
                    dve.wait_ge(txu_done, k + 2)
                else:
                    dve.wait_ge(txu_done, k + 1)
                TT(u_inv[:, tt, :, :], u_inv[:, tt, :, :], heads(misc[n % 2]), ALU.subtract).then_inc(u_upd, 1)
            for tt in range(NT - 1):
                dve.wait_ge(ds_done, tt + 1)
                if tt == 0:
                    v.tensor_copy(state[:, 0, :, :], heads(bank[3])).then_inc(s_upd, 1)
                else:
                    dve.wait_ge(s_upd, tt)
                    for hd in range(GH):
                        ins = STT(state[:, tt % 2, hd, :], state[:, (tt - 1) % 2, hd, :], gl_col[:, tt, hd:hd + 1],
                                  bank[3][:, hd * P:(hd + 1) * P], ALU.mult, ALU.add)
                    ins.then_inc(s_upd, 1)
            for hd in range(GH):
                dve.wait_ge(on_rt, hd + 1)
                r = slot[2 + hd % 2]
                dve_link(dve, v.reciprocal(r[:, :], r[:, :]))
                dve_link(dve, STT(o_t[:, hd, :], o_t[:, hd, :], V("gdn_norm"), r[:, :], ALU.mult, ALU.mult))
                dve.wait_ge(z_silu, hd + 1)
                TT(o_t[:, hd, :], o_t[:, hd, :], xs[:, hd % 2, :, :].rearrange("p a b -> p (a b)"), ALU.mult)\
                    .then_inc(y_done, 1)
                dve.wait_ge(ya_part, hd + 1)
                TT(ya_lo[:, hd, :], o_t[:, hd, :], ya_hi[:, hd, :].bitcast(F32), ALU.subtract).then_inc(ya_ready, 1)

            for b in range(2):
                v.memset(z_hi[b][:, :, S - 1:528].bitcast(F32), 0.0)
                v.memset(z_lo[b][:, :, S - 1:528].bitcast(F32), 0.0).then_inc(zp_zero, 1)
            for c in range(4):
                b, gr = divmod(c, 2)
                ps = out_bank("ncmp", c)
                for half in range(2):
                    dve.wait_ge(z_part, 2 * c + half + 1)
                    q, n = slice(half * ND, (half + 1) * ND), S - half
                    TT(z_lo[b][q, gr, 0:n], ps[q, half:S], z_hi[b][q, gr, 0:n].bitcast(F32), ALU.subtract)\
                        .then_inc(z_ready, 1)
            dve.wait_ge(pos_part, 1)
            TT(pos_lo[:, :, :, :], pos[:, :, :, :], pos_hi[:, :, :, :].bitcast(F32), ALU.subtract).then_inc(pos_ready, 1)
            a0 = att[0]
            c_m, c_r = st[:, 32:40], st[:, 40:48]

            def cmp_front(qt):
                dve.wait_ge(cs_done, qt + 1)
                if qt >= 1:
                    dve.wait_ge(a0.t_done, 18 * qt - 16)
                for gr in range(NG):
                    ins = TT(c_s[:, 4 * gr:4 * gr + 4, :], bank[2 + gr][:, 0:4 * NCMP].rearrange("p (h n) -> p h n", h=4),
                             c_bias[:, qt, 4 * gr:4 * gr + 4, :], ALU.add)
                dve_link(dve, ins)
                dve_link(dve, v.tensor_reduce(c_m, c_s[:, :, :], AX.X, ALU.max))
                TT(c_s[:, :, :], c_s[:, :, :], c_m.unsqueeze(2).broadcast_to([P, NH, NCMP]), ALU.subtract)\
                    .then_inc(cs_shift, 1)

            def cmp_back(qt):
                dve.wait_ge(cs_exp, qt + 1)
                dve_link(dve, v.tensor_reduce(c_r, c_s[:, :, :], AX.X, ALU.add))
                dve_link(dve, v.reciprocal(c_r, c_r))
                dve_link(dve, TT(c_r, c_r, gate_col[:, qt, 0:24:3], ALU.mult))
                dve_link(dve, TT(c_s[:, :, :], c_s[:, :, :],
                                 c_mask[:, qt, :].unsqueeze(1).broadcast_to([P, NH, NCMP]), ALU.mult))
                TT(c_s[:, :, :], c_s[:, :, :], c_r.unsqueeze(2).broadcast_to([P, NH, NCMP]), ALU.mult)\
                    .then_inc(cp_ready, 1)

            items = []
            for qt in range(NT):
                for hd in range(NH):
                    for b in range(2):
                        items.append((alibi[:, hd, (3 - qt) * P:S], BIG,
                                      gate_col[:, qt, 3 * hd + 1 + b:3 * hd + 2 + b], (qt + 1) * P))
            biased, norm = attention(a0, items, n_s, st, lambda i: 18 * (i // 16) + 2 + i % 16 + 1)
            dve.wait_ge(c2_loaded, 80)
            dve.wait_ge(hid_done, 4)
            cmp_front(0)
            biased(0)
            for j in range(64):
                if j % 16 == 0:
                    if j > 0:
                        cmp_front(j // 16)
                    cmp_back(j // 16)
                if j + 1 < 64:
                    biased(j + 1)
                norm(j)
                if j % 16 == 3 and j > 16:
                    nsa_lo(dve, TT, j // 16 - 1, a0, yb_lo, yb_hi, misc, heads)
            nsa_lo(dve, TT, 3, a0, yb_lo, yb_hi, misc, heads)

            for m in range(DC):
                dve.wait_ge(dense_done, group_of(f"a2d{m}"))
                dve.wait_ge(mixa_sig, 2 * m + 1)
                if m >= 2:
                    dve.wait_ge(mx_ready, m - 1)
                TT(slot[4 + m % 2][:, :], slot[0][:, :], out_bank(f"a2d{m}")[:, :], ALU.mult).then_inc(mix_a, 1)
                dve.wait_ge(dense_done, group_of(f"b2d{m}"))
                dve.wait_ge(mixa_sig, 2 * m + 2)
                dve.wait_ge(mix_a, m + 1)
                if m >= 1:
                    dve.wait_ge(mix_b, m)
                dve_link(dve, TT(slot[2][:, :], slot[1][:, :], out_bank(f"b2d{m}")[:, :], ALU.mult))
                TT(slot[4 + m % 2][:, :], slot[4 + m % 2][:, :], slot[2][:, :], ALU.add).then_inc(mix_b, 1)
                dve.wait_ge(mx_part, m + 1)
                TT(mx_lo[:, m, :], slot[4 + m % 2][:, :], mx_hi[:, m, :].bitcast(F32), ALU.subtract)\
                    .then_inc(mx_ready, 1)
            post_add(0)
            post_apply(0, "mix_post", mo_u)
            norm_apply(1, "ffn_pre", (0, 8))
            for c in range(FC + 1):
                if c < FC:
                    for b in range(2):
                        g = b * FC + c
                        dve.wait_ge(up_lin, 2 * c + b + 1)
                        src, dst = out_bank("up", 2 * c + b), slot[2 * b + c % 2]
                        dve_link(dve, STT(dst[:, 1:S], src[:, 0:S - 1], V("conv_ffn", 3 * g + 1), dst[:, 1:S], ALU.mult, ALU.add))
                        STT(dst[:, 2:S], src[:, 0:S - 2], V("conv_ffn", 3 * g), dst[:, 2:S], ALU.mult, ALU.add)\
                            .then_inc(up_conv, 1)
                if c >= 1:
                    dve.wait_ge(a_part, c)
                    TT(a_lo[:, c - 1, :], slot[2 + (c - 1) % 2][:, :], a_hi[:, c - 1, :].bitcast(F32),
                       ALU.subtract).then_inc(a_ready, 1)
                if c < FC:
                    dve.wait_ge(up_act, c + 1)
                    dve.wait_ge(up_conv, 2 * c + 2)
                    TT(slot[2 + c % 2][:, :], slot[2 + c % 2][:, :], slot[c % 2][:, :], ALU.mult).then_inc(a_raw, 1)
            post_add(1)
            post_apply(1, "ffn_post", mo_u)
            for c in range(2):
                dve.wait_ge(ps_part, c + 1)
                TT(p_lo[:, c, :], p_raw[:, c, :], p_hi[:, c, :].bitcast(F32), ALU.subtract).then_inc(ps_ready, 1)
            for c in range(DC):
                dve.wait_ge(u_part, 16 + c + 1)
                TT(u_lo[:, c, :], h[:, c, :], u_hi[:, c, :].bitcast(F32), ALU.subtract).then_inc(u_ready, 1)
            for m in range(DC):
                dve.wait_ge(ple_sig, m + 1)
                TT(mo_a[:, m, :], slot[4 + m % 2][:, :], out_bank(f"ple{m}")[:, :], ALU.mult).then_inc(po_copy, 1)
                if m == 1:
                    dve.wait_ge(po_sq, 16 + 2)
                    TT(slot[2][:, :], slot[0][:, :], slot[1][:, :], ALU.add).then_inc(po_acc, 1)
                elif m >= 2:
                    post_add_one(2, m)
            post_apply(2, "ple_post", mo_a)
            norm_apply(2, "ffn1", (0, 24))
            ffn_gate(1, "up1")
            add_half("down1", 0.5)
            norm_apply(3, "mix2", (0, 32))
            for c in range(8):
                dve.wait_ge(dense_done, group_of("wq", c))
                TS(wq[:, c, :], out_bank("wq", c)[:, :], V("b_wq", c), ND ** -0.5, ALU.add, ALU.mult).then_inc(wq_done, 1)
            dve.wait_ge(c3_loaded, 32)
            for j in range(NT):
                dve.wait_ge(dense_done, group_of("wv", j))
                TT(wv[:, j, :], out_bank("wv", j)[:, 0:256], wvb[:, :], ALU.add).then_inc(wv_done, 1)
            nsink = st2[:, 64:80]
            dve_link(dve, TS(nsink, V("sinks", 0, 16), -1.0, None, ALU.mult))
            items = []
            for qt in range(NT):
                for hd in range(WH):
                    items.append((band[:, P:256] if qt == 0 else band[:, :], nsink[:, hd:hd + 1], None,
                                  min(qt + 1, 2) * P))
            a1 = att[1]
            biased, norm = attention(a1, items, w_s, st2, lambda i: i + 1)

            def win_lo(n):
                qt, c = divmod(n, 2)
                dve.wait_ge(a1.o_part, n + 1)
                cut = slice(qt * P, (qt + 1) * P)
                TT(yw_lo[:, 4 * c:4 * c + 4, cut], heads(misc[2 + c]), yw_hi[:, 4 * c:4 * c + 4, cut].bitcast(F32),
                   ALU.subtract).then_inc(a1.o_ready, 1)

            biased(0)
            for j in range(64):
                if j + 1 < 64:
                    biased(j + 1)
                norm(j)
                if j % 8 == 3 and j > 8:
                    win_lo(j // 8 - 1)
            win_lo(7)
            for m in range(DC):
                dve.wait_ge(dense_done, group_of(f"proj_w{m}"))
                dve.wait_ge(sg_done, m + 1)
                STT(ma[:, m, :], out_bank(f"proj_w{m}")[:, :], 1.0, sg[:, m % 2, :], ALU.mult, ALU.mult)\
                    .then_inc(ma_done, 1)
            for c in range(8):
                dve.wait_ge(mqk_lin, c + 1)
                if c >= 2:
                    dve.wait_ge(mqk_silu, c - 1)
                src, dst = slot[c % 2], cb2[:, c % 2, :]
                dve_link(dve, TS(dst, src[:, :], V("mconv", 4 * c + 3), None, ALU.mult))
                for n, tap in ((1, 2), (2, 1), (3, 0)):
                    ins = STT(dst[:, n:S], src[:, 0:S - n], V("mconv", 4 * c + tap), dst[:, n:S], ALU.mult, ALU.add)
                    if n < 3:
                        dve_link(dve, ins)
                ins.then_inc(mqk_conv, 1)
            dve_link(dve, v.memset(r_one[0:8, :], 1.0))
            dve.wait_ge(r2_act, 5)
            v.tensor_tensor_scan(r_raw[0:8, :], r_one[0:8, :], r_f[0:8, :], 0.0, ALU.mult, ALU.subtract)\
                .then_inc(r2_dve, 1)
            dve.wait_ge(r2_dve, 1)
            STT(r_a[0:8, :], r_i[0:8, :], 15.0, r_raw[0:8, :], ALU.mult, ALU.subtract).then_inc(r2_dve, 1)
            dve.wait_ge(r2_dve, 2)
            v.tensor_tensor_scan(r_f[0:8, :], r_one[0:8, :], r_a[0:8, :], 0.0, ALU.mult, ALU.max).then_inc(r2_dve, 1)
            dve.wait_ge(r2_dve, 3)
            TT(r_raw[0:8, :], r_raw[0:8, :], r_f[0:8, :], ALU.add).then_inc(r2_dve, 1)
            dve.wait_ge(c4_loaded, 32)
            for hf in range(2):
                for j in range(NT):
                    dve.wait_ge(dense_done, group_of(f"mv{hf}", j))
                    TT(mv[:, j, hf * S:(hf + 1) * S], out_bank(f"mv{hf}", j)[:, :], mvb[:, hf * S:(hf + 1) * S], ALU.add)\
                        .then_inc(mv_done, 1)
            dve.wait_ge(ac_tr, 1)
            v.tensor_copy(small[:, 0:32], misc[0][:, 0:32]).then_inc(ac_done, 1)
            dve.wait_ge(mqk_silu, 8)
            v.memset(small[:, 252:253], 0.0).then_inc(r2_dve, 1)
            for hd in range(MH):
                dve.wait_ge(mb_done, hd + 1)
                if hd >= 1:
                    dve.wait_ge(mnd_done, 3 * hd)
                else:
                    dve.wait_ge(ac_done, 1)
                for j in range(NT):
                    ins = TS(wsc[:, j * P:(j + 1) * P], bank[0][:, j * P:(j + 1) * P], acol[:, j, hd:hd + 1], 0.0,
                             ALU.subtract, ALU.max)
                ins.then_inc(mdg_in, 1)
                dve.wait_ge(mw_exp, hd + 1)
                w4 = wsc[:, 0:S].rearrange("p (h c) -> p h c", h=NT)
                dve_link(dve, TT(w4, w4, incl2.unsqueeze(1).broadcast_to([P, NT, P]), ALU.mult))
                dve.wait_ge(msc_done, hd + 1)
                for lo, n, b in ((0, 512, 1), (512, 512, 2), (1024, 256, 3)):
                    STT(wsc[:, lo:lo + n], bank[b][:, 0:n], ND ** -0.5, wsc[:, lo:lo + n], ALU.mult, ALU.mult)\
                        .then_inc(mws, 1)
                dve.wait_ge(mnd_done, 3 * hd + 2)
                dve.wait_ge(meb_copied, hd + 1)
                if hd >= 1:
                    dve.wait_ge(mh_ready, hd)
                dve_link(dve, STT(em_b[:, :], misc[1][:, :], -1.0, em_b[:, :], ALU.mult, ALU.max))
                dve_link(dve, TT(em_b[:, :], misc[1][:, :], em_b[:, :], ALU.max))
                v.reciprocal(em_b[:, :], em_b[:, :]).then_inc(mhn, 1)
                dve.wait_ge(mnd_done, 3 * hd + 3)
                dve.wait_ge(mhn, 2 * hd + 1)
                TT(hn[:, :], misc[0][:, :], em_b[:, :], ALU.mult).then_inc(mhn, 1)
                dve.wait_ge(mh_rt, hd + 1)
                dve_link(dve, v.reciprocal(mr[:, :], mr[:, :]))
                dve_link(dve, STT(hn[:, :], hn[:, :], V("head_norm", hd), mr[:, :], ALU.mult, ALU.mult))
                TT(hn[:, :], hn[:, :], so[:, hd, :], ALU.mult).then_inc(mh_y, 1)
                dve.wait_ge(mh_part, hd + 1)
                TT(m_lo[:, hd, :], hn[:, :], m_hi[:, hd, :].bitcast(F32), ALU.subtract).then_inc(mh_ready, 1)
            for m in range(DC):
                dve.wait_ge(dense_done, group_of(f"proj_m{m}"))
                dve.wait_ge(sg_done, 8 + m + 1)
                if m >= 2:
                    dve.wait_ge(mg_in, m - 1)
                dve_link(dve, TT(slot[2 + m % 2][:, :], slot[m % 2][:, :], out_bank(f"proj_m{m}")[:, :], ALU.mult))
                TT(ma[:, m, :], ma[:, m, :], slot[2 + m % 2][:, :], ALU.add).then_inc(mg_in, 1)
                dve.wait_ge(mg_part, m + 1)
                TT(mg_lo[:, m, :], ma[:, m, :], mg_hi[:, m, :].bitcast(F32), ALU.subtract).then_inc(mg_ready, 1)
            add_half("out", 1.0)
            norm_apply(4, "ffn2", (0, 40))
            ffn_gate(2, "up2")
            add_half("down2", 0.5)
            dve.wait_ge(rt_done, 6)
            dve_link(dve, v.reciprocal(hn[:, :], slot[3][:, :]))
            for c in range(DC):
                STT(result[:, c, :], h[:, c, :], V("final", c), hn[:, :], ALU.mult, ALU.mult).then_inc(f_out, 1)


def nsa_lo(dve, TT, qt, a, yb_lo, yb_hi, misc, heads):
    dve.wait_ge(a.o_part, qt + 1)
    cut = slice(qt * P, (qt + 1) * P)
    TT(yb_lo[:, :, cut], heads(misc[2 + qt % 2]), yb_hi[:, :, cut].bitcast(F32), ALU.subtract).then_inc(a.o_ready, 1)


def layout(x, inp):
    I = {k: np.asarray(v) for k, v in inp.items()}
    one = lambda n: I[n][0]
    win = one("w_in")
    o = np.cumsum([0, 512, 512, 512, 512, 4, 4, 512, 128, 128, 128, 128, 128, 128, 24, 2048])
    (qa, ka, va, za, ba, aa, qb, kcm, vcm, ksl, vsl, kwi, vwi, gn, gm) = [win[:, a:b] for a, b in zip(o[:-1], o[1:])]
    zero = lambda n: np.zeros((D, n), np.float32)
    rows1 = np.concatenate([ba, zero(28), aa, zero(28), gn, zero(40)], 1)
    order = [g * 4 + c for c in range(4) for g in range(2)]
    pick = lambda w, heads_: np.concatenate([w[:, 64 * i:64 * i + 64] for i in heads_], 1)
    twice = lambda w: np.concatenate([w, w], 1)
    w2i = one("w_in_2")
    o2 = np.cumsum([0, 1024, 256, 256, 512, 512, 1024, 1024, 8, 8, 2048])
    cut2 = [slice(a, b) for a, b in zip(o2[:-1], o2[1:])]
    worder = [(2 * p_ + s) * 4 + r for p_ in range(2) for r in range(4) for s in range(2)]
    rows2 = np.concatenate([w2i[:, cut2[7]], zero(24), w2i[:, cut2[8]], zero(88)], 1)
    rowpick = lambda w, heads_: np.concatenate([w[64 * i:64 * i + 64] for i in heads_], 0)
    w_b2d = rowpick(one("w_b2d"), order)
    w_pa = rowpick(one("w_proj_attn_2"), worder)
    up = one("w_up")

    def pairs(a, b):
        a, b = a.reshape(D, FC, 1, P), b.reshape(D, FC, 1, P)
        return np.concatenate([a, b], 2).reshape(D, 2 * FF)

    mats = {
        "qkv": np.concatenate([qa, ka, va], 1), "rows1": rows1,  "nq": pick(qb, order),
        "nk": np.concatenate([ksl, kwi], 1),
        "ncmp": np.concatenate([twice(kcm[:, :64]), twice(kcm[:, 64:]), twice(vcm[:, :64]), twice(vcm[:, 64:])], 1),
        "nv": np.concatenate([vsl, vwi], 1), "cmpk": one("cmp_w1_k"), "cmpv": one("cmp_w1_v"),
        "w_o": one("w_o"), "up": pairs(up[:, :FF], up[:, FF:]), "down": one("w_down"),
        "up1": pairs(one("ffn1_w_gate_2"), one("ffn1_w_up_2")), "down1": one("ffn1_w_down_2"),
        "up2": pairs(one("ffn2_w_gate_2"), one("ffn2_w_up_2")), "down2": one("ffn2_w_down_2"),
        "wq": pick(w2i[:, cut2[0]], worder), "wk": w2i[:, cut2[1]], "wv": w2i[:, cut2[2]],
        "mqk": np.concatenate([w2i[:, cut2[3]], w2i[:, cut2[4]]], 1), "rows2": rows2,
        "mv0": w2i[:, cut2[5]][:, :512], "mv1": w2i[:, cut2[5]][:, 512:], "mo": w2i[:, cut2[6]],
        "out": one("w_out_2"),
    }
    g2 = w2i[:, cut2[9]]
    mats.update({f"z{i}": za[:, i * P:(i + 1) * P] for i in range(GH)})
    for m in range(DC):
        c = slice(m * P, (m + 1) * P)
        mats[f"gate_a{m}"], mats[f"gate_b{m}"] = gm[:, :D][:, c], gm[:, D:][:, c]
        mats[f"a2d{m}"], mats[f"b2d{m}"] = one("w_a2d")[:, c], w_b2d[:, c]
        mats[f"ple{m}"], mats[f"ple_gate{m}"] = one("w_ple")[:, c], one("w_ple_gate")[:, c]
        mats[f"gate_w{m}"], mats[f"gate_m{m}"] = g2[:, :D][:, c], g2[:, D:][:, c]
        mats[f"proj_w{m}"], mats[f"proj_m{m}"] = w_pa[:, c], one("w_proj_mlstm_2")[:, c]
    stream = np.zeros((NSLABS * SLAB, P, P), np.float32)
    for name, chunks, k, width in dense_layers():
        at = START[name][0]
        w = mats[name]
        b = w.reshape(k, P, w.shape[1] // P, P)
        b = b.transpose(0, 2, 1, 3) if width else b.transpose(2, 0, 1, 3)
        n = b.shape[0] * b.shape[1]
        stream[at:at + n] = b.reshape(n, P, P)
    weights = np.ascontiguousarray(stream.reshape(NSLABS, SLAB, P, P).transpose(0, 2, 1, 3))

    vec = np.zeros((P, NVEC), np.float32)

    def put(name, a):
        a = np.asarray(a)
        vec[:a.shape[0], VECS[name]:VECS[name] + a.shape[1]] = a

    cols = lambda a: a.reshape(-1, P).T
    taps = lambda w: w.T.reshape(-1, P, w.shape[0]).transpose(1, 0, 2).reshape(P, -1)
    put("mix_pre", cols(one("norm_mix_pre")))
    put("conv_qkv", taps(one("conv_qkv")))
    put("gdn_norm", one("gdn_norm")[:, None])
    put("mix_post", cols(one("norm_mix_post")))
    put("ffn_pre", cols(one("norm_ffn_pre")))
    put("conv_ffn", taps(one("conv_ffn")))
    put("conv_ffn_b", cols(one("conv_ffn_b")))
    put("ffn_post", cols(one("norm_ffn_post")))
    put("ple_post", cols(one("norm_ple_post")))
    put("ffn1", cols(one("ffn1_norm_2")))
    put("mix2", cols(one("mix_norm_2")))
    bi = one("b_in_2")
    put("b_wq", cols(pick(bi[None, cut2[0]], worder)[0]))
    put("b_wk", cols(bi[cut2[1]]))
    put("b_mqk", cols(np.concatenate([bi[cut2[3]], bi[cut2[4]]])))
    put("b_mo", cols(bi[cut2[6]]))
    put("b_rows2", np.concatenate([bi[cut2[7]], np.zeros(24, np.float32), bi[cut2[8]]])[:, None])
    put("b_gate", cols(bi[cut2[9]]))
    put("mconv", taps(one("mlstm_conv_2")))
    put("head_norm", one("mlstm_head_norm_2").T)
    put("ffn2", cols(one("ffn2_norm_2")))
    put("final", cols(I["final_norm_2"]))
    put("a_log", one("a_log")[:, None])
    put("dt_bias", one("dt_bias")[:, None])
    put("sinks", np.broadcast_to(one("attn_sinks_2")[None], (P, WH)))

    j, i = np.arange(P)[:, None], np.arange(P)[None, :]
    masks = np.zeros((P, 8, P), np.float32)
    for lv in range(LEVELS):
        m = 1 << lv
        masks[:, lv] = (j // (2 * m) == i // (2 * m)) & ((i // m) % 2 == 1) & ((j // m) % 2 == 0)
    masks[:, 7] = i >= j
    rowmask = np.broadcast_to((np.arange(S) % P != 0).astype(np.float32), (P, S))
    q, xk = np.arange(P)[:, None], np.arange(S)[None, :] - 384
    slope = 2.0 ** (-8.0 * np.arange(1, NH + 1) / NH)
    alibi = np.where(xk <= q, 0, 1)[:, None, :] * -1e30 + np.where(xk <= q, xk - q, 0)[:, None, :] * slope[None, :, None]
    tq = np.arange(NT)[None, :] * P + np.arange(P)[:, None]
    dist = tq[:, :, None] - (np.arange(NCMP) * CS + CL - 1)[None, None, :]
    c_mask = (dist >= 0).astype(np.float32)
    c_bias = np.where(dist[:, :, None, :] >= 0, -slope[None, None, :, None] * dist[:, :, None, :], -1e30)
    kj, qi = np.arange(2 * P)[None, :], np.arange(P)[:, None]
    band = np.where((kj > qi) & (kj <= qi + P), 0.0, -1e30)
    pos = np.stack([one(n).reshape(16, P).T for n in ("cmp_pos_k", "cmp_pos_v")], 1)
    pos = np.repeat(pos[:, :, :, None], 2, 3)
    w2 = np.stack([one(n).reshape(2, P, ND).transpose(1, 0, 2) for n in ("cmp_w2_k", "cmp_w2_v")], 1)
    f = lambda a: np.ascontiguousarray(a, dtype=np.float32)
    fm = lambda a: f(a.T.reshape(-1, P, S).transpose(1, 0, 2))
    return {
        "weights": weights, "x": fm(x[0]), "p": fm(I["p"][0, 0]), "vec": vec,
        "ident": f(np.eye(P)), "ones": f(np.ones((P, P))), "masks": f(masks),
        "incl": f(masks[:, 7]), "rowmask": f(rowmask),
        "alibi": f(alibi), "c_bias": f(c_bias), "c_mask": f(c_mask), "band": f(band), "pos": f(pos), "w2": f(w2),
        "wvb": f(np.broadcast_to(bi[cut2[2]], (P, 256))), "mvb": f(np.broadcast_to(bi[cut2[5]], (P, 1024))),
    }


def kernel(**inputs):
    import concourse.bacc as bacc
    from concourse.bass_utils import run_bass_kernel_spmd

    x = np.asarray(inputs.pop("x"))
    arrays = layout(x, inputs)
    nc = bacc.Bacc("TRN2", target_bir_lowering=False, num_devices=1)
    t = {n: nc.dram_tensor(f"in_{n}", a.shape, mybir.dt.from_np(a.dtype), kind="ExternalInput").ap()
         for n, a in arrays.items()}
    t["out"] = nc.dram_tensor("out", (P, DC, S), F32, kind="ExternalOutput").ap()
    build(nc, t)
    r = run_bass_kernel_spmd(nc, [{f"in_{n}": a for n, a in arrays.items()}], core_ids=[0])
    out = r.results[0]["out"]
    return np.ascontiguousarray(out.transpose(1, 0, 2).reshape(D, S).T)[None]
```

```python
from contextlib import ExitStack

import numpy as np

import concourse.bass as bass
from concourse import mybir

F32 = mybir.dt.float32
F32R = mybir.dt.float32r
BF16 = mybir.dt.bfloat16
ALU = mybir.AluOpType
ACT = mybir.ActivationFunctionType
AX = mybir.AxisListType

P = 128
S = 512
NT = S // P
D = 1024
DC = D // P
KB = 1024

SLAB = 8
RAWS = 4
SPLITS = 5
LEAD = 3

GH = 4
LEVELS = 7
NH, NG, ND = 8, 2, 64
CL, CS, NCMP = 32, 16, 31
WH, WKV = 16, 4
MH = 8
FF = 2816
FC = FF // P
EPS = 1e-6
BIG = 3.0e38


def dense_layers():
    a = [("qkv", 12, 8, 0), ("rows1", 1, 8, 0), ("nq", 4, 8, 0), ("nk", 2, 8, 0),
         ("z0", 1, 8, 0), ("z1", 1, 8, 0), ("z2", 1, 8, 0), ("z3", 1, 8, 0), ("ncmp", 4, 8, 0), ("nv", NT, 8, 2),
         ("cmpk", 1, 16, 2), ("cmpv", 1, 16, 2)]
    for m in range(DC):
        a += [(f"gate_a{m}", 1, 8, 0), (f"a2d{m}", 1, 4, 0), (f"gate_b{m}", 1, 8, 0), (f"b2d{m}", 1, 4, 0)]
    a += [("w_o", 8, 8, 0), ("up", 2 * FC, 8, 0), ("down", 8, FC, 0)]
    for m in range(DC):
        a += [(f"ple{m}", 1, 2, 0), (f"ple_gate{m}", 1, 8, 0)]
    a += [("up1", 2 * FC, 8, 0), ("down1", 8, FC, 0),
          ("wq", 8, 8, 0), ("wk", 2, 8, 0), ("wv", NT, 8, 2)]
    for m in range(DC):
        a += [(f"gate_w{m}", 1, 8, 0), (f"proj_w{m}", 1, 8, 0)]
    a += [("mqk", 8, 8, 0), ("rows2", 1, 8, 0), ("mv0", NT, 8, 4), ("mv1", NT, 8, 4), ("mo", 8, 8, 0)]
    for m in range(DC):
        a += [(f"gate_m{m}", 1, 8, 0), (f"proj_m{m}", 1, 8, 0)]
    a += [("out", 8, 8, 0), ("up2", 2 * FC, 8, 0), ("down2", 8, FC, 0)]
    return a


def dense_plan():
    tile = group = 0
    start = {}
    for name, chunks, k, width in dense_layers():
        start[name] = (tile, group)
        tile += k * (width or chunks)
        group += chunks
    return start, tile, group


START, TILES, GROUPS = dense_plan()
NSLABS = -(-TILES // SLAB)

VECS = {}


def _vec_layout():
    at = 0
    for name, n in (("mix_pre", 8), ("conv_qkv", 48), ("gdn_norm", 1), ("mix_post", 8), ("ffn_pre", 8),
                    ("conv_ffn", 132), ("conv_ffn_b", 44), ("ffn_post", 8), ("ple_post", 8),
                    ("ffn1", 8), ("mix2", 8), ("b_wq", 8), ("b_wk", 2), ("b_mqk", 8), ("b_mo", 8),
                    ("b_rows2", 1), ("b_gate", 16), ("mconv", 32), ("head_norm", 8), ("ffn2", 8),
                    ("final", 8), ("a_log", 1), ("dt_bias", 1), ("sinks", 16)):
        VECS[name] = at
        at += n
    return at


NVEC = _vec_layout()


def build(nc, t):
    ctx = ExitStack()
    with ctx:
        base = 16512

        def at(name, offset, shape, dt=F32):
            return nc.alloc_sbuf_tensor_at(name, [P] + shape, dt, offset=base + offset)

        def sem(name):
            return ctx.enter_context(nc.semaphore(name))

        raw = at("raw", 0, [RAWS, SLAB, P])
        w_hi = at("w_hi", 16 * KB, [SPLITS, SLAB, P], F32R)
        w_lo = at("w_lo", 36 * KB, [SPLITS, SLAB, P], F32R)
        h = at("h", 56 * KB, [DC, S])
        u_hi = at("u_hi", 72 * KB, [DC, S], F32R)
        u_lo = at("u_lo", 88 * KB, [DC, S], F32R)
        mo_u = at("mo_u", 72 * KB, [DC, S])
        vec = at("vec", 104 * KB, [448])
        ident = at("ident", 104 * KB + 1792, [P])
        ones = at("ones", 104 * KB + 2304, [P])
        small = at("small", 104 * KB + 2816, [256])
        A = 104 * KB + 3840
        assert NVEC <= 448

        def arena(name, kb, shape, dt=F32):
            return at(name, A + int(kb * KB), shape, dt)

        slot = [arena(f"slot{i}", 88 + 2 * i, [S]) for i in range(6)]

        qkv = arena("qkv", 0, [12, S])
        wk_t = arena("wk_t", 24, [NT, GH, P])
        kt_t = arena("kt_t", 32, [NT, GH, P])
        vb_t = arena("vb_t", 40, [NT, GH, P])
        g_row = arena("g_row", 48, [GH, S])
        b_row = arena("b_row", 56, [GH, S])
        t_inv = arena("t_inv", 56, [NT, GH, P])
        u_inv = arena("u_inv", 16, [NT, GH, P])
        o_t = arena("o_t", 56, [GH, S])
        qk_t = arena("qk_t", 64, [NT, GH, P])
        at_t = arena("at_t", 72, [NT, GH, P])
        wt_t = arena("wt_t", 72, [NT, GH, P])
        am = arena("am", 88, [4, GH, P])
        xs = arena("xs", 80, [4, GH, P])
        dec = arena("dec", 80, [2, GH, P])
        dmask = arena("dmask", 84, [2, GH, P])
        state = arena("state", 80, [2, GH, P])
        u_new = arena("u_new", 84, [2, GH, P])
        a_gate = arena("a_gate", 24, [S])
        b_gate = arena("b_gate", 26, [S])
        sp1 = arena("sp1", 28, [S])
        n_gate = arena("n_gate", 30, [S])
        sp2 = arena("sp2", 32, [S])
        g_sum = arena("g_sum", 34, [S])
        rowmask = arena("rowmask", 40, [S])
        masks = arena("masks", 98, [8, P], BF16)
        masks_in = arena("masks_in", 64, [8, P])
        lens = arena("lens", 72, [8, S])
        ya_hi = arena("ya_hi", 0, [4, S], F32R)
        ya_lo = arena("ya_lo", 8, [4, S], F32R)
        cols1 = small[:, 0:32].rearrange("p (t c) -> p t c", t=NT)
        e_col = small[:, 32:48].rearrange("p (t c) -> p t c", t=NT)
        bg_col = small[:, 48:64].rearrange("p (t c) -> p t c", t=NT)
        tail_col = small[:, 64:80].rearrange("p (t c) -> p t c", t=NT)
        gl_col = small[:, 80:96].rearrange("p (t c) -> p t c", t=NT)
        gate_col = small[:, 96:192].rearrange("p (t c) -> p t c", t=NT)
        na_col = small[:, 192:193]

        nq = at("nq", 56 * KB, [4, S])
        nk = at("nk", 64 * KB, [2, S])
        nv = arena("nv", 28, [NT, 256])
        yb_hi = arena("yb_hi", 32, [4, S], F32R)
        yb_lo = arena("yb_lo", 40, [4, S], F32R)
        alibi = arena("alibi", 48, [NH, S])
        z_raw = [arena(f"z_raw{i}", 64 + 4.25 * i, [NG, 528]) for i in range(2)]
        zc = arena("zc", 40, [2, 16, NG, 32])
        zc_hi = arena("zc_hi", 32, [2, 16, NG, 32], F32R)
        zc_lo = arena("zc_lo", 40, [2, 16, NG, 32], F32R)
        pos = arena("pos", 81, [2, 16])
        hid_t = arena("hid_t", 85, [2, 256])
        w2 = arena("w2", 82, [2, 2, ND])
        hid = arena("hid", 83, [2, 2, NG, 32])
        kc = arena("kc", 84, [32])
        vc = arena("vc", 84.25, [NG, ND])
        n_s = arena("n_s", 64, [3, S])
        n_pt = arena("n_pt", 70, [2, S])
        c_s = arena("c_s", 74, [NH, NCMP])
        c_pt = arena("c_pt", 76, [NH, P])
        c_bias = arena("c_bias", 88, [NT, NH, NCMP])
        c_mask = arena("c_mask", 92, [NT, NCMP])
        st = arena("st", 93, [64])
        mx_hi = arena("mx_hi", 48, [DC, S], F32R)
        mx_lo = arena("mx_lo", 64, [DC, S], F32R)

        a_hi = arena("a_hi", 0, [FC, S], F32R)
        a_lo = arena("a_lo", 44, [FC, S], F32R)
        p_raw = arena("p_raw", 0, [2, S])
        p_hi = arena("p_hi", 4, [2, S], F32R)
        p_lo = arena("p_lo", 8, [2, S], F32R)
        mo_a = arena("mo_a", 16, [DC, S])

        wq = arena("wq", 0, [8, S])
        wk = arena("wk", 16, [2, S])
        wv = arena("wv", 20, [NT, 256])
        wvb = arena("wvb", 24, [256])
        band = arena("band", 25, [256])
        yw_hi = arena("yw_hi", 26, [8, S], F32R)
        yw_lo = arena("yw_lo", 42, [8, S], F32R)
        w_s = arena("w_s", 58, [3, S])
        w_pt = arena("w_pt", 64, [2, S])
        st2 = arena("st2", 68, [96])
        ma = arena("ma", 0, [DC, S])
        sg = arena("sg", 70, [2, S])
        mqk = arena("mqk", 16, [8, S])
        mv = arena("mv", 32, [NT, 1024])
        mvb = arena("mvb", 80, [1024])
        m_hi = arena("m_hi", 48, [MH, S], F32R)
        m_lo = arena("m_lo", 64, [MH, S], F32R)
        so = arena("so", 64, [MH, S])
        cb2 = arena("cb2", 84, [2, S])
        wsc = arena("wsc", 80, [1280])
        emx = arena("emx", 90, [S])
        em_b = arena("em_b", 92, [S])
        hn = arena("hn", 94, [S])
        msq = arena("msq", 96, [S])
        mr = arena("mr", 98, [S])
        mxr = arena("mxr", 86, [S])
        acol = small[:, 0:32].rearrange("p (t c) -> p t c", t=NT)
        incl2 = small[:, 96:224]
        r_raw = arena("r_raw", 88, [S])
        r_i = arena("r_i", 92, [S])
        r_f = arena("r_f", 94, [S])
        r_one = arena("r_one", 96, [S])
        r_a = arena("r_a", 98, [S])
        mg_hi = arena("mg_hi", 16, [DC, S], F32R)
        mg_lo = arena("mg_lo", 32, [DC, S], F32R)

        result = arena("result", 0, [DC, S])

        bank = [ctx.enter_context(nc.psum_tensor(f"dense{i}", [P, S], F32)) for i in range(4)]
        misc = [ctx.enter_context(nc.psum_tensor(f"misc{i}", [P, S], F32)) for i in range(4)]

        def heads(ps):
            return ps[:, :].rearrange("p (h c) -> p h c", h=GH)

        def V(name, i=0, n=1):
            return vec[:, VECS[name] + i:VECS[name] + i + n]

        w_loaded = [sem(f"w_loaded{i}") for i in range(RAWS)]
        w_part = sem("w_part")
        w_split = sem("w_split")
        w_used = sem("w_used")
        dense_done = sem("dense_done")
        in_loaded = sem("in_loaded")
        x_loaded = sem("x_loaded")
        c1_loaded = sem("c1_loaded")
        c2_loaded = sem("c2_loaded")
        c3_loaded = sem("c3_loaded")
        c4_loaded = sem("c4_loaded")
        p_loaded = sem("p_loaded")
        out_stored = sem("out_stored")
        h_ready = sem("h_ready")
        sq_done = sem("sq_done")
        sq_used = sem("sq_used")
        rt_done = sem("rt_done")
        ux_done = sem("ux_done")
        u_part = sem("u_part")
        u_ready = sem("u_ready")
        po_copy = sem("po_copy")
        po_sq = sem("po_sq")
        po_acc = sem("po_acc")
        po_sum = sem("po_sum")
        po_rt = sem("po_rt")
        cv_lin = sem("cv_lin")
        cv_done = sem("cv_done")
        cv_silu = sem("cv_silu")
        rows1_done = sem("rows1_done")
        sp_done = sem("sp_done")
        sp_exp = sem("sp_exp")
        g_done = sem("g_done")
        tr1_done = sem("tr1_done")
        cols_done = sem("cols_done")
        bc_done = sem("bc_done")
        bc_copied = sem("bc_copied")
        ecol_in = sem("ecol_in")
        ecol_done = sem("ecol_done")
        head_sq = sem("head_sq")
        head_sum = sem("head_sum")
        head_rt = sem("head_rt")
        l2_done = sem("l2_done")
        kv_tr = sem("kv_tr")
        kv_done = sem("kv_done")
        dc_in = sem("dc_in")
        dc_exp = sem("dc_exp")
        kk_done = sem("kk_done")
        at_done = sem("at_done")
        eg_done = sem("eg_done")
        qd_done = sem("qd_done")
        at_beta = sem("at_beta")
        len_done = sem("len_done")
        am_done = sem("am_done")
        x_done = sem("x_done")
        xc_done = sem("xc_done")
        txu_done = sem("txu_done")
        t_upd = sem("t_upd")
        u_upd = sem("u_upd")
        wt_done = sem("wt_done")
        wt_copied = sem("wt_copied")
        un_done = sem("un_done")
        un_copied = sem("un_copied")
        og_done = sem("og_done")
        og_copied = sem("og_copied")
        ds_done = sem("ds_done")
        s_upd = sem("s_upd")
        z_silu = sem("z_silu")
        y_done = sem("y_done")
        ya_part = sem("ya_part")
        ya_ready = sem("ya_ready")
        nqk_done = sem("nqk_done")
        nv_done = sem("nv_done")
        zp_zero = sem("zp_zero")
        z_copied = sem("z_copied")
        zc_sum = sem("zc_sum")
        zc_part = sem("zc_part")
        zc_ready = sem("zc_ready")
        hid_act = sem("hid_act")
        hid_tr = sem("hid_tr")
        hid_done = sem("hid_done")
        kvc_done = sem("kvc_done")
        kvc_copied = sem("kvc_copied")
        cs_done = sem("cs_done")
        cs_shift = sem("cs_shift")
        cs_exp = sem("cs_exp")
        cp_ready = sem("cp_ready")
        mixa_sig = sem("mixa_sig")
        mix_a = sem("mix_a")
        mix_b = sem("mix_b")
        mx_part = sem("mx_part")
        mx_ready = sem("mx_ready")
        up_lin = sem("up_lin")
        up_conv = sem("up_conv")
        up_act = sem("up_act")
        a_raw = sem("a_raw")
        a_part = sem("a_part")
        a_ready = sem("a_ready")
        ps_part = sem("ps_part")
        ps_ready = sem("ps_ready")
        ple_sig = sem("ple_sig")
        wq_done = sem("wq_done")
        wk_done = sem("wk_done")
        wv_done = sem("wv_done")
        sg_done = sem("sg_done")
        ma_done = sem("ma_done")
        mqk_lin = sem("mqk_lin")
        mqk_b = sem("mqk_b")
        mqk_conv = sem("mqk_conv")
        mqk_silu = sem("mqk_silu")
        mv_done = sem("mv_done")
        so_done = sem("so_done")
        r2_act = sem("r2_act")
        r2_dve = sem("r2_dve")
        ac_tr = sem("ac_tr")
        ac_done = sem("ac_done")
        mb_done = sem("mb_done")
        mdg_in = sem("mdg_in")
        mw_exp = sem("mw_exp")
        msc_done = sem("msc_done")
        mws = sem("mws")
        mnd_done = sem("mnd_done")
        meb_copied = sem("meb_copied")
        mhn = sem("mhn")
        mh_y = sem("mh_y")
        mh_part = sem("mh_part")
        mh_ready = sem("mh_ready")
        mg_in = sem("mg_in")
        mg_part = sem("mg_part")
        mg_ready = sem("mg_ready")
        f_out = sem("f_out")
        act_step = sem("act_step")
        dve_step = sem("dve_step")
        pool_step = sem("pool_step")

        steps = {"act": 0, "dve": 0}

        def act_link(eng, ins):
            steps["act"] += 1
            ins.then_inc(act_step, 1)
            eng.wait_ge(act_step, steps["act"])

        def dve_link(eng, ins):
            steps["dve"] += 1
            ins.then_inc(dve_step, 1)
            eng.wait_ge(dve_step, steps["dve"])

        class Att:
            def __init__(self, tag):
                self.s_done = sem(f"s_done_{tag}")
                self.m_done = sem(f"m_done_{tag}")
                self.e_done = sem(f"e_done_{tag}")
                self.p_done = sem(f"p_done_{tag}")
                self.t_done = sem(f"t_done_{tag}")
                self.t_copied = sem(f"t_copied_{tag}")
                self.pv_done = sem(f"pv_done_{tag}")
                self.o_part = sem(f"o_part_{tag}")
                self.o_ready = sem(f"o_ready_{tag}")

        att = [Att("n"), Att("w")]

        freed = [None] * GROUPS

        def frees(name, s, values):
            g = START[name][1]
            for i, v in enumerate(values):
                freed[g + i] = (s, v)

        frees("qkv", cv_done, [c + 1 for c in range(12)])
        frees("rows1", rows1_done, [3])
        for hd in range(GH):
            frees(f"z{hd}", z_silu, [hd + 1])
        frees("nq", nqk_done, [1, 2, 3, 4])
        frees("nk", nqk_done, [5, 6])
        frees("ncmp", z_copied, [2, 4, 6, 8])
        frees("nv", nv_done, [1, 2, 3, 4])
        frees("cmpk", hid_act, [1])
        frees("cmpv", hid_act, [2])
        for m in range(DC):
            frees(f"gate_a{m}", mixa_sig, [2 * m + 1])
            frees(f"a2d{m}", mix_a, [m + 1])
            frees(f"gate_b{m}", mixa_sig, [2 * m + 2])
            frees(f"b2d{m}", mix_b, [m + 1])
            frees(f"ple_gate{m}", ple_sig, [m + 1])
            frees(f"ple{m}", po_copy, [16 + m + 1])
            frees(f"gate_w{m}", sg_done, [m + 1])
            frees(f"proj_w{m}", ma_done, [m + 1])
            frees(f"gate_m{m}", sg_done, [8 + m + 1])
            frees(f"proj_m{m}", mg_in, [m + 1])
        frees("w_o", po_copy, [m + 1 for m in range(8)])
        frees("down", po_copy, [8 + m + 1 for m in range(8)])
        frees("up", up_conv, [c + 1 for c in range(2 * FC)])
        for n, name in ((0, "up1"), (1, "up2")):
            for c in range(FC):
                frees_at = START[name][1] + 2 * c
                freed[frees_at] = (up_act, FC * (n + 1) + c + 1)
                freed[frees_at + 1] = (a_raw, FC * (n + 1) + c + 1)
        frees("down1", h_ready, [24 + m + 1 for m in range(8)])
        frees("wq", wq_done, [m + 1 for m in range(8)])
        frees("wk", wk_done, [1, 2])
        frees("wv", wv_done, [1, 2, 3, 4])
        frees("mqk", mqk_lin, [m + 1 for m in range(8)])
        frees("rows2", r2_act, [1])
        frees("mv0", mv_done, [1, 2, 3, 4])
        frees("mv1", mv_done, [5, 6, 7, 8])
        frees("mo", so_done, [m + 1 for m in range(8)])
        frees("out", h_ready, [32 + m + 1 for m in range(8)])
        frees("down2", h_ready, [40 + m + 1 for m in range(8)])

        ends = {}
        last_slab = []
        done = 0
        for name, chunks, k, width in dense_layers():
            tile = START[name][0]
            for c in range(chunks):
                last_slab.append((tile + (k * width if width else (c + 1) * k) - 1) // SLAB)
            if width:
                done += chunks
                ends[tile + k * width - 1] = done
            else:
                for c in range(chunks):
                    done += 1
                    ends[tile + (c + 1) * k - 1] = done
        slab_used = []
        inside = 0
        for s in range(NSLABS):
            last = s * SLAB + SLAB - 1
            if last in ends or last >= TILES:
                slab_used.append((dense_done, ends.get(last, GROUPS)))
            else:
                inside += 1
                slab_used.append((w_used, inside))

        def group_of(name, m=0):
            return START[name][1] + m + 1

        def out_bank(name, m=0):
            return bank[(START[name][1] + m) % 4]

        block = ctx.enter_context(nc.Block())

        @block.sync
        def _(sp):
            sp.dma_start(h[:, 0:4, :], t["x"][:, 0:4, :]).then_inc(x_loaded, 16)
            sp.dma_start(h[:, 4:8, :], t["x"][:, 4:8, :]).then_inc(x_loaded, 16)
            for s in range(NSLABS):
                if s >= RAWS:
                    sp.wait_ge(w_split, s - RAWS + 1)
                sp.dma_start(raw[:, s % RAWS, :, :], t["weights"][s]).then_inc(w_loaded[s % RAWS], 16)
            for c in range(DC):
                sp.wait_ge(f_out, c + 1)
                sp.dma_start(t["out"][:, c, :], result[:, c, :]).then_inc(out_stored, 16)
            sp.wait_ge(out_stored, 16 * DC)

        @block.gpsimd
        def _(pool):
            for s in range(NSLABS):
                if s == last_slab[START["nk"][1] + 1] + 1:
                    for tt in range(NT):
                        pool.wait_ge(at_done, 2 * tt + 1)
                        nc.gpsimd.tensor_tensor(at_t[:, tt, :, :], at_t[:, tt, :, :],
                                                b_row[:, :, tt * P:(tt + 1) * P], ALU.mult).then_inc(at_beta, 1)
                pool.wait_ge(w_part, s + 1)
                nc.gpsimd.tensor_tensor(w_lo[:, s % SPLITS, :, :], raw[:, s % RAWS, :, :],
                                        w_hi[:, s % SPLITS, :, :].bitcast(F32),
                                        ALU.subtract).then_inc(w_split, 1)

        @block.tensor
        def _(pe):
            mm = nc.tensor.matmul
            tr = nc.tensor.transpose
            inner = [0]

            def weight(tile, n=1):
                s, j = divmod(tile, SLAB)
                if j == 0:
                    pe.wait_ge(w_split, s + 1)
                return (w_hi[:, s % SPLITS, j:j + n, :].rearrange("p a b -> p (a b)"),
                        w_lo[:, s % SPLITS, j:j + n, :].rearrange("p a b -> p (a b)"))

            def used(ins, tile):
                if tile % SLAB == SLAB - 1 and tile not in ends:
                    inner[0] += 1
                    assert slab_used[tile // SLAB] == (w_used, inner[0])
                    ins.then_inc(w_used, 1)

            def wait_bank(g):
                if g >= 4:
                    pe.wait_ge(*freed[g - 4])

            def dense_part(name, m, i, src_hi, src_lo):
                tile, g = START[name][0] + DC * m + i, START[name][1] + m
                if i == 0:
                    wait_bank(g)
                out = bank[g % 4][:, :]
                hi, lo = weight(tile)
                mm(out, hi, src_hi[:, i, :], start=(i == 0), stop=False)
                mm(out, hi, src_lo[:, i, :], start=False, stop=False)
                last = mm(out, lo, src_hi[:, i, :], start=False, stop=(i == DC - 1))
                used(last, tile)
                if i == DC - 1:
                    last.then_inc(dense_done, 1)

            def dense(name, src_hi, src_lo, k_ready=None, after=None):
                tile, g0 = START[name]
                n, k = next((c, k) for nm, c, k, _ in dense_layers() if nm == name)
                for m in range(n):
                    g = g0 + m
                    wait_bank(g)
                    out = bank[g % 4][:, :]
                    for i in range(k):
                        hi, lo = weight(tile)
                        if k_ready and m == 0:
                            pe.wait_ge(k_ready[0], k_ready[1] + i + 1)
                        mm(out, hi, src_hi[:, i, :], start=(i == 0), stop=False)
                        mm(out, hi, src_lo[:, i, :], start=False, stop=False)
                        last = mm(out, lo, src_hi[:, i, :], start=False, stop=(i == k - 1))
                        used(last, tile)
                        tile += 1
                    last.then_inc(dense_done, 1)
                    if after:
                        after(m)

            def dense_tokens(name, width):
                tile, g0 = START[name]
                for j in range(NT):
                    wait_bank(g0 + j)
                for i in range(DC):
                    hi, lo = weight(tile, width)
                    for j in range(NT):
                        out = bank[(g0 + j) % 4][:, 0:width * P]
                        a_h, a_l = u_hi[:, i, j * P:(j + 1) * P], u_lo[:, i, j * P:(j + 1) * P]
                        mm(out, a_h, hi, start=(i == 0), stop=False)
                        mm(out, a_h, lo, start=False, stop=False)
                        last = mm(out, a_l, hi, start=False, stop=(i == DC - 1))
                        if i == DC - 1:
                            last.then_inc(dense_done, 1)
                    tile += width
                    if i < DC - 1:
                        used(last, tile - 1)

            def norm_sum(n):
                if n > 0:
                    pe.wait_ge(rt_done, n)
                for c in range(DC):
                    pe.wait_ge(sq_done, DC * n + c + 1)
                    mm(misc[3][:, :], ones[:, :], slot[c % 2][:, :], start=(c == 0),
                       stop=(c == DC - 1)).then_inc(sq_used, 1)

            def post_sum(n):
                pe.wait_ge(po_acc, 7 * n + 7)
                mm(misc[2][:, :], ones[:, :], slot[2][:, :], start=True, stop=True).then_inc(po_sum, 1)

            def gdn():
                for m in range(2):
                    for i in range(DC):
                        dense_part("nq", m, i, u_hi, u_lo)
                pe.wait_ge(g_done, 1)
                pe.wait_ge(rows1_done, 3)
                pe.wait_ge(head_rt, 8)
                for j in range(NT):
                    tr(misc[0][:, 8 * j:8 * j + 4], g_sum[0:4, j * P:(j + 1) * P], ident[0:4, 0:4])
                    tr(misc[0][:, 8 * j + 4:8 * j + 8], b_gate[0:4, j * P:(j + 1) * P], ident[0:4, 0:4])
                for j in range(NT):
                    last = tr(misc[0][:, 64 + 24 * j:88 + 24 * j], n_gate[0:24, j * P:(j + 1) * P],
                              ident[0:24, 0:24])
                last.then_inc(tr1_done, 1)
                for i in range(8):
                    src = g_sum if i < 4 else b_gate
                    if i >= 2:
                        pe.wait_ge(bc_copied, i - 1)
                    mm(misc[1 + i % 2][:, :], ident[0:4, i % 4:i % 4 + 1].broadcast_to([4, P]), src[0:4, :],
                       start=True, stop=True).then_inc(bc_done, 1)
                    dense_part("nq", 2, i, u_hi, u_lo)
                for j in range(2 * NT):
                    tt = j // 2
                    if j == 0:
                        pe.wait_ge(l2_done, 8)
                        pe.wait_ge(cols_done, 2)
                    if j >= 2:
                        pe.wait_ge(kv_done, 3 * ((j - 2) // 2) + (3 if j % 2 else 2))
                    for hd in range(GH):
                        last = tr(misc[3 * (j % 2)][:, hd * P:(hd + 1) * P],
                                  qkv[:, (4 if j % 2 == 0 else 8) + hd, tt * P:(tt + 1) * P], ident[:, :])
                    last.then_inc(kv_tr, 1)
                    dense_part("nq", 3, j, u_hi, u_lo)
                pe.wait_ge(bc_copied, 8)
                for tt in range(NT):
                    if tt >= 1:
                        pe.wait_ge(at_done, 2 * tt)
                    for b, c0 in ((0, 4), (1, 0)):
                        for hd in range(GH):
                            ks = qkv[:, 4 + hd, tt * P:(tt + 1) * P]
                            last = mm(misc[1 + b][:, hd * P:(hd + 1) * P], ks,
                                      qkv[:, c0 + hd, tt * P:(tt + 1) * P], start=True, stop=True)
                        last.then_inc(kk_done, 1)
                    for i in range(4 * tt, 4 * tt + 4):
                        dense_part("nk", i // DC, i % DC, u_hi, u_lo)
                pe.wait_ge(nqk_done, 6)
                n_all = LEVELS * NT

                def x_of(n):
                    tt = n % NT
                    pe.wait_ge(am_done, n + 1)
                    if n >= NT + 2:
                        pe.wait_ge(xc_done, n - NT - 1)
                    elif n >= 2:
                        pe.wait_ge(t_upd, n - 1)
                    if n >= NT:
                        pe.wait_ge(t_upd, n - NT + 1)
                    for hd in range(GH):
                        last = mm(bank[n % 2][:, hd * P:(hd + 1) * P], am[:, n % 4, hd, :],
                                  t_inv[:, tt, hd, :] if n >= NT else ident[:, :], start=True, stop=True)
                    last.then_inc(x_done, 1)

                def tu_of(n):
                    tt, final = n % NT, n >= n_all - NT
                    pe.wait_ge(xc_done, n - NT + 1)
                    pe.wait_ge(u_upd, max(n - NT + 1, n - 1))
                    if not final:
                        for hd in range(GH):
                            last = mm(bank[2 + n % 2][:, hd * P:(hd + 1) * P], u_inv[:, tt, hd, :],
                                      xs[:, n % 4, hd, :], start=True, stop=True)
                        last.then_inc(txu_done, 1)
                    for hd in range(GH):
                        last = mm(misc[n % 2][:, hd * P:(hd + 1) * P], xs[:, n % 4, hd, :],
                                  u_inv[:, tt, hd, :], start=True, stop=True)
                    last.then_inc(txu_done, 1)

                for n in range(NT + 2):
                    x_of(n)
                for n in range(NT, n_all):
                    if n + 2 < n_all:
                        x_of(n + 2)
                    tu_of(n)
                for tt in range(NT):
                    pe.wait_ge(u_upd, n_all - NT + tt + 1)
                    if tt >= 2:
                        pe.wait_ge(wt_copied, tt - 1)
                    for hd in range(GH):
                        last = mm(bank[tt % 2][:, hd * P:(hd + 1) * P], wk_t[:, tt, hd, :],
                                  u_inv[:, tt, hd, :], start=True, stop=True)
                    last.then_inc(wt_done, 1)
                pe.wait_ge(qd_done, 4)
                for tt in range(NT):
                    if tt > 0:
                        pe.wait_ge(s_upd, tt)
                        pe.wait_ge(wt_copied, tt + 1)
                        pe.wait_ge(og_copied, tt)
                    for hd in range(GH):
                        o = bank[2][:, hd * P:(hd + 1) * P]
                        last = mm(o, u_inv[:, tt, hd, :], vb_t[:, tt, hd, :], start=True, stop=(tt == 0))
                        if tt > 0:
                            last = mm(o, wt_t[:, tt, hd, :], state[:, (tt - 1) % 2, hd, :], start=False, stop=True)
                    last.then_inc(un_done, 1)
                    pe.wait_ge(un_copied, tt + 1)
                    if tt < NT - 1:
                        for hd in range(GH):
                            last = mm(bank[3][:, hd * P:(hd + 1) * P], kt_t[:, tt, hd, :],
                                      u_new[:, tt % 2, hd, :], start=True, stop=True)
                        last.then_inc(ds_done, 1)
                    for hd in range(GH):
                        o = misc[2][:, hd * P:(hd + 1) * P]
                        if tt > 0:
                            mm(o, state[:, (tt - 1) % 2, hd, :], qkv[:, hd, tt * P:(tt + 1) * P],
                               start=True, stop=False)
                        last = mm(o, u_new[:, tt % 2, hd, :], qk_t[:, tt, hd, :], start=(tt == 0), stop=True)
                    last.then_inc(og_done, 1)
                for hd in range(GH):
                    pe.wait_ge(head_sq, 8 + hd + 1)
                    if hd >= 2:
                        pe.wait_ge(head_rt, 8 + hd - 1)
                    mm(misc[hd % 2][:, :], ones[:, :], slot[hd % 2][:, :], start=True, stop=True)\
                        .then_inc(head_sum, 1)
                    dense(f"z{hd}", u_hi, u_lo)

            def compress():
                for b, name in ((0, "cmpk"), (1, "cmpv")):
                    tile, g = START[name]
                    pe.wait_ge(zc_ready, b + 1)
                    wait_bank(g)
                    out = bank[g % 4][0:64, 0:256]
                    for i in range(16):
                        hi, lo = weight(tile, 2)
                        zh = zc_hi[:, b, i, :, :].rearrange("p a b -> p (a b)")
                        zl = zc_lo[:, b, i, :, :].rearrange("p a b -> p (a b)")
                        mm(out, zh, hi, start=(i == 0), stop=False)
                        mm(out, zh, lo, start=False, stop=False)
                        last = mm(out, zl, hi, start=False, stop=(i == 15))
                        tile += 2
                        if i < 15:
                            used(last, tile - 1)
                    last.then_inc(dense_done, 1)
                for b in range(2):
                    pe.wait_ge(hid_act, b + 1)
                    for m in range(2):
                        last = tr(misc[b][:, m * 64:(m + 1) * 64], hid_t[0:64, b, m * P:(m + 1) * P],
                                  ident[0:64, 0:64])
                    last.then_inc(hid_tr, 1)
                pe.wait_ge(hid_done, 2)
                for gr in range(NG):
                    for m in range(2):
                        mm(misc[0][gr * ND:(gr + 1) * ND, 0:32], w2[:, 0, m, :], hid[:, 0, m, gr, :],
                           start=(m == 0), stop=(m == 1))
                for gr in range(NG):
                    for m in range(2):
                        last = mm(misc[1][0:32, gr * ND:(gr + 1) * ND], hid[:, 1, m, gr, :], w2[:, 1, m, :],
                                  start=(m == 0), stop=(m == 1))
                last.then_inc(kvc_done, 1)

            def nsa():
                a = att[0]
                items = [(qt, hd, b) for qt in range(NT) for hd in range(NH) for b in range(2)]

                def cmp_scores(qt):
                    if qt >= 1:
                        pe.wait_ge(cs_shift, qt)
                    for hd in range(NH):
                        gr, c = divmod(hd, 4)
                        last = mm(bank[2 + gr][:, c * NCMP:(c + 1) * NCMP],
                                  nq[gr * ND:(gr + 1) * ND, c, qt * P:(qt + 1) * P],
                                  kc[gr * ND:(gr + 1) * ND, 0:NCMP], start=True, stop=True)
                    last.then_inc(cs_done, 1)

                def scores(j):
                    qt, hd, b = items[j]
                    gr, c = divmod(hd, 4)
                    if j >= 2:
                        pe.wait_ge(a.m_done, j - 1)
                    mm(bank[j % 2][:, 0:(qt + 1) * P], nq[gr * ND:(gr + 1) * ND, c, qt * P:(qt + 1) * P],
                       nk[gr * ND:(gr + 1) * ND, b, 0:(qt + 1) * P], start=True, stop=True).then_inc(a.s_done, 1)

                def turn(j):
                    qt = items[j][0]
                    u = 18 * qt + 2 + j % 16
                    pe.wait_ge(a.p_done, j + 1)
                    pe.wait_ge(a.t_copied, u - 1)
                    for kt in range(qt + 1):
                        last = tr(misc[u % 2][:, kt * P:(kt + 1) * P], n_s[:, j % 3, kt * P:(kt + 1) * P], ident[:, :])
                    last.then_inc(a.t_done, 1)

                def cmp_turn(qt):
                    pe.wait_ge(cp_ready, qt + 1)
                    for b in range(2):
                        u = 18 * qt + b
                        if u >= 2:
                            pe.wait_ge(a.t_copied, u - 1)
                        for hd in range(4):
                            last = tr(misc[u % 2][0:NCMP, hd * P:(hd + 1) * P], c_s[:, 4 * b + hd, :], ident[:, :])
                        last.then_inc(a.t_done, 1)

                def values(j):
                    qt, hd, b = items[j]
                    gr, c = divmod(hd, 4)
                    o = misc[2 + qt % 2][gr * ND:(gr + 1) * ND, c * P:(c + 1) * P]
                    pe.wait_ge(a.t_copied, 18 * qt + 2 + j % 16 + 1)
                    if j % 16 == 0 and qt >= 2:
                        pe.wait_ge(a.o_ready, qt - 1)
                    if b == 0:
                        mm(o, vc[0:NCMP, gr, :], c_pt[0:NCMP, hd, :], start=True, stop=False)
                    for kt in range(qt + 1):
                        last = mm(o, nv[:, kt, b * P + gr * ND:b * P + (gr + 1) * ND], n_pt[:, j % 2, kt * P:(kt + 1) * P],
                                  start=False, stop=(b == 1 and kt == qt))
                    last.then_inc(a.pv_done, 1)

                pe.wait_ge(kvc_copied, 2)
                pe.wait_ge(nv_done, 4)
                cmp_scores(0)
                scores(0)
                scores(1)
                for j in range(len(items)):
                    if j + 2 < len(items):
                        scores(j + 2)
                    if j % 16 == 0:
                        if j >= 1:
                            values(j - 1)
                        cmp_turn(j // 16)
                    if j % 16 == 8 and j // 16 + 1 < NT:
                        cmp_scores(j // 16 + 1)
                    turn(j)
                    if j % 16:
                        values(j - 1)
                values(len(items) - 1)

            def window():
                a = att[1]
                items = [(qt, kv, r) for qt in range(NT) for kv in range(WKV) for r in range(4)]

                def scores(j):
                    qt, kv, r = items[j]
                    half, c = kv % 2, kv // 2
                    lo = max(qt - 1, 0) * P
                    if j >= 2:
                        pe.wait_ge(a.m_done, j - 1)
                    mm(bank[j % 2][:, 0:(qt + 1) * P - lo],
                       wq[half * ND:(half + 1) * ND, 4 * c + r, qt * P:(qt + 1) * P],
                       wk[half * ND:(half + 1) * ND, c, lo:(qt + 1) * P], start=True, stop=True).then_inc(a.s_done, 1)

                def turn(j):
                    qt = items[j][0]
                    pe.wait_ge(a.p_done, j + 1)
                    if j >= 2:
                        pe.wait_ge(a.t_copied, j - 1)
                    for kt in range(min(qt + 1, 2)):
                        last = tr(misc[j % 2][:, kt * P:(kt + 1) * P], w_s[:, j % 3, kt * P:(kt + 1) * P], ident[:, :])
                    last.then_inc(a.t_done, 1)

                def values(j):
                    qt, kv, r = items[j]
                    half, c = kv % 2, kv // 2
                    n = min(qt + 1, 2)
                    o = misc[2 + c][half * ND:(half + 1) * ND, r * P:(r + 1) * P]
                    pe.wait_ge(a.t_copied, j + 1)
                    if j % 8 == 0 and j >= 16:
                        pe.wait_ge(a.o_ready, j // 8 - 1)
                    for i in range(n):
                        kt = qt - n + 1 + i
                        last = mm(o, wv[:, kt, kv * ND:(kv + 1) * ND], w_pt[:, j % 2, i * P:(i + 1) * P],
                                  start=(i == 0), stop=(i == n - 1))
                    last.then_inc(a.pv_done, 1)

                pe.wait_ge(wq_done, 8)
                pe.wait_ge(wk_done, 2)
                pe.wait_ge(wv_done, 4)
                scores(0)
                scores(1)
                for j in range(len(items)):
                    if j + 2 < len(items):
                        scores(j + 2)
                    turn(j)
                    if j >= 1:
                        values(j - 1)
                values(len(items) - 1)
                pe.wait_ge(a.o_ready, 8)

            off = [(0, 512, 2, 0), (2, 896, 2, 384), (1, 1024, 3, 0)]

            def mlstm():
                pe.wait_ge(r2_dve, 3)
                for j in range(NT):
                    last = tr(misc[0][:, 8 * j:8 * j + 8], r_a[0:8, j * P:(j + 1) * P], ident[0:8, 0:8])
                last.then_inc(ac_tr, 1)
                pe.wait_ge(mqk_silu, 8)
                pe.wait_ge(mv_done, 8)
                pe.wait_ge(so_done, 8)
                pe.wait_ge(ac_done, 1)
                pe.wait_ge(r2_act, 7)

                def front(hd):
                    c, half = divmod(hd, 2)
                    sel = ident[0:8, hd:hd + 1].broadcast_to([8, P])
                    if hd >= 1:
                        pe.wait_ge(mw_exp, hd)
                        pe.wait_ge(mws, 3 * hd)
                    mm(bank[0][:, :], sel, mxr[0:8, :], start=True, stop=True).then_inc(mb_done, 1)
                    q = lambda a, b: mqk[half * ND:(half + 1) * ND, c, a * P:b * P]
                    k = lambda a: mqk[half * ND:(half + 1) * ND, 4 + c, a * P:(a + 1) * P]
                    for j in range(NT):
                        last = mm(bank[1][:, j * P:(j + 1) * P], k(j), q(j, j + 1), start=True, stop=True)
                    for j, _, b, at_col in off:
                        last = mm(bank[b][:, at_col:at_col + (3 - j) * P], k(j), q(j + 1, NT), start=True, stop=True)
                    last.then_inc(msc_done, 1)

                def back(hd):
                    if hd >= 1:
                        pe.wait_ge(mhn, 2 * hd)
                    mm(misc[2][:, :], ident[0:8, hd:hd + 1].broadcast_to([8, P]), emx[0:8, :],
                       start=True, stop=True).then_inc(mnd_done, 1)
                    pe.wait_ge(mws, 3 * hd + 3)
                    for dst, den in ((1, True), (0, False)):
                        w = lambda j: ones[:, :] if den else mv[:, j, hd * P:(hd + 1) * P]
                        for j in range(NT):
                            mm(misc[dst][:, j * P:(j + 1) * P], w(j), wsc[:, j * P:(j + 1) * P],
                               start=(j == 0), stop=False)
                        for n, (j, at_col, _, _) in enumerate(off):
                            last = mm(misc[dst][:, (j + 1) * P:S], w(j), wsc[:, at_col:at_col + (3 - j) * P],
                                      start=False, stop=(n == 2))
                        last.then_inc(mnd_done, 1)
                    pe.wait_ge(head_sq, 12 + hd + 1)
                    if hd >= 1:
                        pe.wait_ge(head_rt, 12 + hd)
                    mm(misc[3][:, :], ones[:, :], msq[:, :], start=True, stop=True).then_inc(head_sum, 1)

                for hd in range(MH):
                    front(hd)
                    back(hd)
                pe.wait_ge(mh_ready, 8)

            def ffn(name_up, name_down, n):
                dense(name_up, u_hi, u_lo, (u_ready, DC * (n + 1)))
                dense(name_down, a_hi, a_lo, (a_ready, FC * n))

            pe.wait_ge(in_loaded, 48)
            norm_sum(0)

            def length_sum(m):
                c = m - 2
                if 0 <= c < 8:
                    pe.wait_ge(head_sq, c + 1)
                    if c >= 2:
                        pe.wait_ge(head_rt, c - 1)
                    mm(misc[c % 2][:, :], ones[:, :], slot[2 + c % 2][:, :], start=True,
                       stop=True).then_inc(head_sum, 1)

            dense("qkv", u_hi, u_lo, (u_ready, 0), length_sum)
            dense("rows1", u_hi, u_lo)
            for g in range(START["qkv"][1] + 9, START["rows1"][1] + 1):
                pe.wait_ge(*freed[g])
            gdn()
            dense("ncmp", u_hi, u_lo)
            dense_tokens("nv", 2)
            pe.wait_ge(ya_ready, 4)
            compress()
            nsa()
            pe.wait_ge(att[0].o_ready, 4)
            for m in range(DC):
                dense(f"gate_a{m}", u_hi, u_lo)
                dense(f"a2d{m}", ya_hi, ya_lo)
                dense(f"gate_b{m}", u_hi, u_lo)
                dense(f"b2d{m}", yb_hi, yb_lo)
            dense("w_o", mx_hi, mx_lo, (mx_ready, 0))
            post_sum(0)
            norm_sum(1)
            ffn("up", "down", 0)
            post_sum(1)
            pe.wait_ge(ps_ready, 2)
            for m in range(DC):
                dense(f"ple{m}", p_hi, p_lo)
                dense(f"ple_gate{m}", u_hi, u_lo, (u_ready, 2 * DC) if m == 0 else None)
            post_sum(2)
            norm_sum(2)
            dense("up1", u_hi, u_lo, (u_ready, 3 * DC))
            dense("down1", a_hi, a_lo, (a_ready, FC))
            norm_sum(3)
            dense("wq", u_hi, u_lo, (u_ready, 4 * DC))
            dense("wk", u_hi, u_lo)
            dense_tokens("wv", 2)
            window()
            for m in range(DC):
                dense(f"gate_w{m}", u_hi, u_lo)
                dense(f"proj_w{m}", yw_hi, yw_lo)
            dense("mqk", u_hi, u_lo)
            dense("rows2", u_hi, u_lo)
            dense_tokens("mv0", 4)
            dense_tokens("mv1", 4)
            dense("mo", u_hi, u_lo)
            mlstm()
            for m in range(DC):
                dense(f"gate_m{m}", u_hi, u_lo)
                dense(f"proj_m{m}", m_hi, m_lo)
            dense("out", mg_hi, mg_lo, (mg_ready, 0))
            norm_sum(4)
            dense("up2", u_hi, u_lo, (u_ready, 5 * DC))
            dense("down2", a_hi, a_lo, (a_ready, 2 * FC))
            norm_sum(5)

        @block.scalar
        def _(act):
            f = nc.scalar.activation
            rounded = [0]

            def feed(name, m=0):
                upto = min(last_slab[START[name][1] + m] + LEAD + 1, NSLABS)
                while rounded[0] < upto:
                    s = rounded[0]
                    act.wait_ge(w_loaded[s % RAWS], 16 * (s // RAWS + 1))
                    if s >= SPLITS:
                        act.wait_ge(*slab_used[s - SPLITS])
                    f(w_hi[:, s % SPLITS, :, :], raw[:, s % RAWS, :, :], ACT.Copy).then_inc(w_part, 1)
                    rounded[0] += 1

            def after_group(name, m=0):
                feed(name, m)
                act.wait_ge(dense_done, group_of(name, m))

            def norm_act(n, ready, layer=None):
                for c in range(DC):
                    if layer:
                        feed(layer, c if c < 2 else DC - 1)
                    act.wait_ge(ready[0], 32 if ready[0] is x_loaded else ready[1] + c + 1)
                    k = DC * n + c
                    if k >= 2:
                        act.wait_ge(sq_used, k - 1)
                    f(slot[c % 2][:, :], h[:, c, :], ACT.Square).then_inc(sq_done, 1)
                act.wait_ge(sq_used, DC * (n + 1))
                f(slot[3][:, :], misc[3][:, :], ACT.Sqrt, bias=eps_col, scale=1.0 / D).then_inc(rt_done, 1)

            def split_hi(k0):
                for c in range(DC):
                    act.wait_ge(ux_done, k0 + c + 1)
                    f(u_hi[:, c, :], slot[4 + c % 2][:, :], ACT.Copy).then_inc(u_part, 1)

            def post_act(n, name, mo):
                for c in range(DC):
                    if name:
                        after_group(name, c)
                        f(mo[:, c, :], out_bank(name, c)[:, :], ACT.Copy).then_inc(po_copy, 1)
                        act.wait_ge(po_copy, DC * n + c + 1)
                    post_square(n, c, mo)
                post_root(n)

            def post_square(n, c, mo):
                if c >= 2:
                    act.wait_ge(po_acc, 7 * n + c - 1)
                f(slot[c % 2][:, :], mo[:, c, :], ACT.Square).then_inc(po_sq, 1)

            def post_root(n):
                act.wait_ge(po_sum, n + 1)
                f(slot[3][:, :], misc[2][:, :], ACT.Sqrt, bias=eps_col, scale=1.0 / D).then_inc(po_rt, 1)

            def attention(a, items, s_buf, pt_buf, st_buf, before, outs):
                for j in range(len(items) + 1):
                    if j < len(items):
                        nk_, sink, _ = items[j]
                        before(j)
                        act.wait_ge(a.m_done, j + 1)
                        if j >= 8:
                            act.wait_ge(a.p_done, j - 7)
                        if sink is None:
                            f(s_buf[:, j % 3, 0:nk_], s_buf[:, j % 3, 0:nk_], ACT.Exp, bias=st_buf[:, j % 8:j % 8 + 1],
                              scale=-1.0, accum_out=st_buf[:, 8 + j % 8:9 + j % 8]).then_inc(a.e_done, 1)
                        else:
                            f(st_buf[:, 24 + j % 8:25 + j % 8], sink, ACT.Exp, bias=st_buf[:, j % 8:j % 8 + 1])
                            f(s_buf[:, j % 3, 0:nk_], s_buf[:, j % 3, 0:nk_], ACT.Exp, bias=st_buf[:, j % 8:j % 8 + 1],
                              scale=-1.0, accum_out=st_buf[:, 8 + j % 8:9 + j % 8]).then_inc(a.e_done, 1)
                    if j >= 1:
                        i = j - 1
                        nk_, _, u = items[i]
                        act.wait_ge(a.t_done, u + 1)
                        if i >= 2:
                            act.wait_ge(a.pv_done, i - 1)
                        f(pt_buf[:, i % 2, 0:nk_], misc[u % 2][:, 0:nk_], ACT.Copy).then_inc(a.t_copied, 1)
                        outs(i - 1)
                outs(len(items) - 1)

            def ffn_swiglu(n, name):
                for c in range(FC + 1):
                    if c < FC:
                        k = FC * n + c
                        after_group(name, 2 * c)
                        if c >= 2:
                            act.wait_ge(a_ready, k - 1)
                        f(slot[c % 2][:, :], out_bank(name, 2 * c)[:, :], ACT.Silu).then_inc(up_act, 1)
                    if c >= 1:
                        act.wait_ge(a_raw, FC * n + c)
                        f(a_hi[:, c - 1, :], slot[(c - 1) % 2][:, :], ACT.Copy).then_inc(a_part, 1)

            eps_col = small[:, 250:251]
            one_col = small[:, 251:252]
            act.dma_start(vec[:, 0:NVEC], t["vec"]).then_inc(in_loaded, 16)
            act.dma_start(ident[:, :], t["ident"]).then_inc(in_loaded, 16)
            act.dma_start(ones[:, :], t["ones"]).then_inc(in_loaded, 16)
            act.dma_start(masks_in[:, :, :], t["masks"]).then_inc(c1_loaded, 16)
            act.dma_start(rowmask[:, :], t["rowmask"]).then_inc(c1_loaded, 16)
            act.wait_ge(pool_step, 2)
            feed("qkv")
            norm_act(0, (x_loaded, 0))
            split_hi(0)

            for c in range(13):
                if c < 12:
                    after_group("qkv", c)
                    if c >= 2:
                        act.wait_ge(cv_silu, c - 1)
                    f(slot[c % 2][:, :], out_bank("qkv", c)[:, :], ACT.Copy,
                      scale=V("conv_qkv", 4 * c + 3)).then_inc(cv_lin, 1)
                if c >= 1:
                    act.wait_ge(cv_done, c)
                    f(qkv[:, c - 1, :], slot[(c - 1) % 2][:, :], ACT.Silu).then_inc(cv_silu, 1)
                i = c - 1
                if 0 <= i < 8:
                    act.wait_ge(cv_silu, i + 1)
                    if i == 0:
                        act.wait_ge(u_ready, 8)
                    if i >= 2:
                        act.wait_ge(head_sum, i - 1)
                    f(slot[2 + i % 2][:, :], qkv[:, i, :], ACT.Square).then_inc(head_sq, 1)
                i = c - 3
                if 0 <= i < 8:
                    act.wait_ge(head_sum, i + 1)
                    f(lens[:, i, :], misc[i % 2][:, :], ACT.Copy).then_inc(head_rt, 1)
            after_group("rows1")
            rows = out_bank("rows1")
            f(b_gate[0:4, :], rows[0:4, :], ACT.Sigmoid).then_inc(rows1_done, 1)
            f(n_gate[0:24, :], rows[64:88, :], ACT.Sigmoid).then_inc(rows1_done, 1)
            f(a_gate[0:4, :], rows[32:36, :], ACT.Copy).then_inc(rows1_done, 1)
            act.wait_ge(sp_done, 1)
            act_link(act, f(sp2[0:4, :], sp1[0:4, :], ACT.Exp))
            f(na_col[0:4, :], V("a_log")[0:4, :], ACT.Exp)
            f(sp2[0:4, :], sp2[0:4, :], ACT.Ln, bias=one_col[0:4, :]).then_inc(sp_exp, 1)
            act.wait_ge(head_rt, 8)
            act_link(act, f(lens[:, :, :], lens[:, :, :], ACT.Ln, bias=eps_col))
            f(lens[:, :, :], lens[:, :, :], ACT.Exp, scale=-0.5).then_inc(len_done, 1)

            def project(name, dst, c, scale):
                after_group(name, c)
                f(dst[:, c, :], out_bank(name, c)[:, :], ACT.Copy, scale=scale).then_inc(nqk_done, 1)

            project("nq", nq, 0, ND ** -0.5)
            project("nq", nq, 1, ND ** -0.5)
            for i in range(8):
                act.wait_ge(bc_done, i + 1)
                dst = g_row if i < 4 else b_row
                f(dst[:, i % 4, :], misc[1 + i % 2][:, :], ACT.Copy).then_inc(bc_copied, 1)
            act.wait_ge(ecol_in, 1)
            f(e_col, cols1[:, :, 0:4], ACT.Exp).then_inc(ecol_done, 1)
            f(tail_col, tail_col, ACT.Exp).then_inc(ecol_done, 1)
            act.wait_ge(bc_copied, 8)
            f(gl_col, g_row[:, :, P - 1::P].rearrange("p h t -> p t h"), ACT.Exp).then_inc(ecol_done, 1)
            project("nq", nq, 2, ND ** -0.5)
            project("nq", nq, 3, ND ** -0.5)
            for tt in range(NT):
                act.wait_ge(dc_in, tt + 1)
                f(dec[:, tt % 2, :, :], dec[:, tt % 2, :, :], ACT.Exp).then_inc(dc_exp, 1)
            project("nk", nk, 0, 1.0)
            project("nk", nk, 1, 1.0)
            act.wait_ge(kv_done, 12)
            for hd in range(GH):
                f(g_row[:, hd, :], g_row[:, hd, :], ACT.Exp).then_inc(eg_done, 1)
            act.wait_ge(at_done, 2 * NT)
            for n in range(NT, LEVELS * NT):
                act.wait_ge(x_done, n + 1)
                if n >= NT + 4:
                    act.wait_ge(u_upd, n - 3)
                f(xs[:, n % 4, :, :], heads(bank[n % 2]), ACT.Copy).then_inc(xc_done, 1)
            for tt in range(NT):
                act.wait_ge(wt_done, tt + 1)
                f(wt_t[:, tt, :, :], heads(bank[tt % 2]), ACT.Copy, scale=-1.0).then_inc(wt_copied, 1)
            for tt in range(NT):
                act.wait_ge(un_done, tt + 1)
                f(u_new[:, tt % 2, :, :], heads(bank[2]), ACT.Copy).then_inc(un_copied, 1)
                act.wait_ge(og_done, tt + 1)
                f(o_t[:, :, tt * P:(tt + 1) * P], heads(misc[2]), ACT.Copy).then_inc(og_copied, 1)
            act.wait_ge(og_copied, NT)
            for hd in range(GH + 2):
                if hd < GH:
                    if hd >= 2:
                        act.wait_ge(head_sum, 8 + hd - 1)
                    f(slot[hd % 2][:, :], o_t[:, hd, :], ACT.Square).then_inc(head_sq, 1)
                i = hd - 1
                if 0 <= i < GH:
                    act.wait_ge(head_sum, 8 + i + 1)
                    if i >= 2:
                        act.wait_ge(y_done, i - 1)
                    f(slot[2 + i % 2][:, :], misc[i % 2][:, :], ACT.Sqrt, bias=eps_col, scale=1.0 / P).then_inc(head_rt, 1)
                    after_group(f"z{i}")
                    f(xs[:, i % 2, :, :].rearrange("p a b -> p (a b)"), out_bank(f"z{i}")[:, :],
                      ACT.Silu).then_inc(z_silu, 1)
                if i >= 1:
                    act.wait_ge(y_done, i)
                    f(ya_hi[:, i - 1, :], o_t[:, i - 1, :], ACT.Copy).then_inc(ya_part, 1)

            act.wait_ge(ya_ready, 4)
            act.dma_start(alibi[:, :, :], t["alibi"]).then_inc(c2_loaded, 16)
            act.dma_start(pos[:, :, :], t["pos"]).then_inc(c2_loaded, 16)
            act.dma_start(w2[:, :, :, :], t["w2"]).then_inc(c2_loaded, 16)
            act.dma_start(c_bias[:, :, :, :], t["c_bias"]).then_inc(c2_loaded, 16)
            act.dma_start(c_mask[:, :, :], t["c_mask"]).then_inc(c2_loaded, 16)
            act.wait_ge(zp_zero, 2)
            for c in range(4):
                b, gr = divmod(c, 2)
                after_group("ncmp", c)
                ps = out_bank("ncmp", c)
                f(z_raw[b][0:ND, gr, 0:S], ps[0:ND, :], ACT.Copy).then_inc(z_copied, 1)
                f(z_raw[b][ND:P, gr, 0:S - 1], ps[ND:P, 1:S], ACT.Copy).then_inc(z_copied, 1)
            for j in range(NT):
                after_group("nv", j)
                f(nv[:, j, :], out_bank("nv", j)[:, 0:256], ACT.Copy).then_inc(nv_done, 1)
            for b in range(2):
                act.wait_ge(zc_sum, 2 * b + 2)
                f(zc_hi[:, b, :, :, :], zc[:, b, :, :, :], ACT.Copy).then_inc(zc_part, 1)
            for b in range(2):
                after_group(("cmpk", "cmpv")[b])
                f(hid_t[0:64, b, :], out_bank(("cmpk", "cmpv")[b])[0:64, 0:256],
                  ACT.Gelu_apprx_tanh).then_inc(hid_act, 1)
            for b in range(2):
                act.wait_ge(hid_tr, b + 1)
                f(hid[:, b, :, :, :].rearrange("p a b c -> p (a b c)"), misc[b][:, 0:P],
                  ACT.Copy).then_inc(hid_done, 1)
            act.wait_ge(kvc_done, 1)
            f(kc[:, :], misc[0][:, 0:32], ACT.Copy).then_inc(kvc_copied, 1)
            f(vc[0:32, :, :].rearrange("p a b -> p (a b)"), misc[1][0:32, 0:P], ACT.Copy).then_inc(kvc_copied, 1)

            a0 = att[0]

            def nsa_before(j):
                if j % 16 == 0:
                    qt = j // 16
                    act.wait_ge(cs_shift, qt + 1)
                    f(c_s[:, :, :], c_s[:, :, :], ACT.Exp).then_inc(cs_exp, 1)

            def nsa_outs(i):
                if i >= 0 and i % 16 == 15:
                    qt = i // 16
                    act.wait_ge(a0.pv_done, i + 1)
                    f(yb_hi[:, :, qt * P:(qt + 1) * P], heads(misc[2 + qt % 2]), ACT.Copy).then_inc(a0.o_part, 1)

            def cmp_copy(qt):
                for b in range(2):
                    u = 18 * qt + b
                    act.wait_ge(a0.t_done, u + 1)
                    if qt >= 1:
                        act.wait_ge(a0.pv_done, 16 * qt)
                    f(c_pt[0:NCMP, 4 * b:4 * b + 4, :].rearrange("p a b -> p (a b)"), misc[u % 2][0:NCMP, :],
                      ACT.Copy).then_inc(a0.t_copied, 1)

            items = []
            for qt in range(NT):
                for n in range(16):
                    items.append(((qt + 1) * P, None, 18 * qt + 2 + n))
            for j in range(65):
                if j < 64:
                    nsa_before(j)
                    act.wait_ge(a0.m_done, j + 1)
                    f(n_s[:, j % 3, 0:items[j][0]], n_s[:, j % 3, 0:items[j][0]], ACT.Exp,
                      bias=st[:, j % 8:j % 8 + 1], scale=-1.0,
                      accum_out=st[:, 8 + j % 8:9 + j % 8]).then_inc(a0.e_done, 1)
                if j >= 1:
                    i = j - 1
                    nk_, _, u = items[i]
                    if i % 16 == 0:
                        if i >= 1:
                            nsa_outs(i - 1)
                        cmp_copy(i // 16)
                    act.wait_ge(a0.t_done, u + 1)
                    if i >= 2:
                        act.wait_ge(a0.pv_done, i - 1)
                    f(n_pt[:, i % 2, 0:nk_], misc[u % 2][:, 0:nk_], ACT.Copy).then_inc(a0.t_copied, 1)
            nsa_outs(63)

            act.dma_start(h[:, 0:4, :], t["x"][:, 0:4, :]).then_inc(x_loaded, 16)
            act.dma_start(h[:, 4:8, :], t["x"][:, 4:8, :]).then_inc(x_loaded, 16)
            for m in range(DC):
                for b, nm in ((0, "gate_a"), (1, "gate_b")):
                    after_group(f"{nm}{m}")
                    if m >= 1:
                        act.wait_ge((mix_a, mix_b)[b], m)
                    f(slot[b][:, :], out_bank(f"{nm}{m}")[:, :], ACT.Sigmoid).then_inc(mixa_sig, 1)
                act.wait_ge(mix_b, m + 1)
                f(mx_hi[:, m, :], slot[4 + m % 2][:, :], ACT.Copy).then_inc(mx_part, 1)
            act.wait_ge(mx_ready, 8)
            post_act(0, "w_o", mo_u)
            norm_act(1, (h_ready, 0))
            split_hi(8)

            act.wait_ge(u_ready, 16)
            for c in range(FC + 1):
                if c < FC:
                    for b in range(2):
                        g = b * FC + c
                        after_group("up", 2 * c + b)
                        if c >= 2:
                            act.wait_ge(a_ready, c - 1)
                        f(slot[2 * b + c % 2][:, :], out_bank("up", 2 * c + b)[:, :], ACT.Identity,
                          bias=V("conv_ffn_b", g), scale=V("conv_ffn", 3 * g + 2)).then_inc(up_lin, 1)
                    act.wait_ge(up_conv, 2 * c + 1)
                    f(slot[c % 2][:, :], slot[c % 2][:, :], ACT.Gelu_apprx_tanh).then_inc(up_act, 1)
                if c >= 1:
                    act.wait_ge(a_raw, c)
                    f(a_hi[:, c - 1, :], slot[2 + (c - 1) % 2][:, :], ACT.Copy).then_inc(a_part, 1)
            act.wait_ge(a_ready, FC)
            post_act(1, "down", mo_u)
            act.dma_start(p_raw[:, :, :], t["p"]).then_inc(p_loaded, 16)
            act.wait_ge(p_loaded, 16)
            for c in range(2):
                f(p_hi[:, c, :], p_raw[:, c, :], ACT.Copy).then_inc(ps_part, 1)
            for c in range(DC):
                act.wait_ge(h_ready, 8 + c + 1)
                f(u_hi[:, c, :], h[:, c, :], ACT.Copy).then_inc(u_part, 1)
            for m in range(DC):
                after_group(f"ple_gate{m}")
                if m >= 2:
                    act.wait_ge(po_copy, 16 + m - 1)
                f(slot[4 + m % 2][:, :], out_bank(f"ple_gate{m}")[:, :], ACT.Sigmoid).then_inc(ple_sig, 1)
                act.wait_ge(po_copy, 16 + m + 1)
                post_square(2, m, mo_a)
            post_root(2)
            norm_act(2, (h_ready, 16))
            split_hi(16)
            act.wait_ge(u_ready, 32)
            ffn_swiglu(1, "up1")
            norm_act(3, (h_ready, 24), "down1")
            split_hi(24)
            act.dma_start(wvb[:, :], t["wvb"]).then_inc(c3_loaded, 16)
            act.dma_start(band[:, :], t["band"]).then_inc(c3_loaded, 16)
            for c in range(8):
                feed("wq", c)
            for c in range(2):
                after_group("wk", c)
                f(wk[:, c, :], out_bank("wk", c)[:, :], ACT.Identity, bias=V("b_wk", c)).then_inc(wk_done, 1)
            feed("wv")
            items2 = []
            for qt in range(NT):
                for kv in range(WKV):
                    for r in range(4):
                        items2.append((min(qt + 1, 2) * P, V("sinks", 4 * kv + r), len(items2)))

            def win_outs(i):
                if i >= 0 and i % 8 == 7:
                    qt, c = divmod(i // 8, 2)
                    act.wait_ge(att[1].pv_done, i + 1)
                    f(yw_hi[:, 4 * c:4 * c + 4, qt * P:(qt + 1) * P], heads(misc[2 + c]), ACT.Copy)\
                        .then_inc(att[1].o_part, 1)

            attention(att[1], items2, w_s, w_pt, st2, lambda j: None, win_outs)
            for m in range(DC):
                after_group(f"gate_w{m}")
                if m >= 2:
                    act.wait_ge(ma_done, m - 1)
                f(sg[:, m % 2, :], out_bank(f"gate_w{m}")[:, :], ACT.Sigmoid, bias=V("b_gate", m)).then_inc(sg_done, 1)
            act.wait_ge(ma_done, 8)
            act.dma_start(mvb[:, :], t["mvb"]).then_inc(c4_loaded, 16)
            act.dma_start(incl2, t["incl"]).then_inc(c4_loaded, 16)
            for c in range(9):
                if c < 8:
                    after_group("mqk", c)
                    if c >= 2:
                        act.wait_ge(mqk_conv, c - 1)
                    f(slot[c % 2][:, :], out_bank("mqk", c)[:, :], ACT.Identity, bias=V("b_mqk", c)).then_inc(mqk_lin, 1)
                if c >= 1:
                    act.wait_ge(mqk_conv, c)
                    f(mqk[:, c - 1, :], cb2[:, (c - 1) % 2, :], ACT.Silu).then_inc(mqk_silu, 1)
            after_group("rows2")
            act.wait_ge(mqk_conv, 8)
            f(r_raw[0:40, :], out_bank("rows2")[0:40, :], ACT.Identity, bias=V("b_rows2")[0:40, :]).then_inc(r2_act, 1)
            act.wait_ge(r2_act, 1)
            f(r_i[0:8, :], r_raw[0:8, :], ACT.Tanh, scale=1.0 / 15.0).then_inc(r2_act, 1)
            f(r_f[0:8, :], r_raw[32:40, :], ACT.Tanh, scale=1.0 / 15.0).then_inc(r2_act, 1)
            act.wait_ge(r2_act, 3)
            f(r_f[0:8, :], r_f[0:8, :], ACT.Exp, scale=-15.0).then_inc(r2_act, 1)
            act.wait_ge(r2_act, 4)
            f(r_f[0:8, :], r_f[0:8, :], ACT.Ln, bias=one_col[0:8, :]).then_inc(r2_act, 1)
            feed("mv0")
            feed("mv1")
            for c in range(8):
                after_group("mo", c)
                f(so[:, c, :], out_bank("mo", c)[:, :], ACT.Sigmoid, bias=V("b_mo", c)).then_inc(so_done, 1)
            act.wait_ge(r2_dve, 5)
            f(emx[0:8, :], r_raw[0:8, :], ACT.Exp, scale=-1.0).then_inc(r2_act, 1)
            act.wait_ge(mqk_silu, 8)
            f(mxr[0:8, :], r_f[0:8, :], ACT.Copy).then_inc(r2_act, 1)
            off = [(0, 512), (2, 896), (1, 1024)]
            for hd in range(MH):
                act.wait_ge(mb_done, hd + 1)
                act.wait_ge(ac_done, 1)
                if hd >= 1:
                    act.wait_ge(mnd_done, 3 * hd)
                else:
                    act.wait_ge(mv_done, 8)
                act.wait_ge(mdg_in, hd + 1)
                for j, at_col in off:
                    f(wsc[:, at_col:at_col + (3 - j) * P], bank[0][:, (j + 1) * P:S], ACT.Exp,
                      bias=acol[:, j, hd:hd + 1], scale=-1.0)
                f(wsc[:, 0:S], wsc[:, 0:S], ACT.Exp, scale=-1.0).then_inc(mw_exp, 1)
                act.wait_ge(mnd_done, 3 * hd + 1)
                f(em_b[:, :], misc[2][:, :], ACT.Copy).then_inc(meb_copied, 1)
                act.wait_ge(mhn, 2 * hd + 2)
                f(msq[:, :], hn[:, :], ACT.Square).then_inc(head_sq, 1)
                act.wait_ge(head_sum, 12 + hd + 1)
                f(mr[:, :], misc[3][:, :], ACT.Sqrt, bias=eps_col, scale=1.0 / P).then_inc(head_rt, 1)
                act.wait_ge(mh_y, hd + 1)
                f(m_hi[:, hd, :], hn[:, :], ACT.Copy).then_inc(mh_part, 1)
            for m in range(DC):
                after_group(f"gate_m{m}")
                if m >= 1:
                    act.wait_ge(mg_in, m)
                else:
                    act.wait_ge(mh_ready, 8)
                f(slot[m % 2][:, :], out_bank(f"gate_m{m}")[:, :], ACT.Sigmoid, bias=V("b_gate", 8 + m)).then_inc(sg_done, 1)
                act.wait_ge(mg_in, m + 1)
                f(mg_hi[:, m, :], ma[:, m, :], ACT.Copy).then_inc(mg_part, 1)
            norm_act(4, (h_ready, 32), "out")
            split_hi(32)
            act.wait_ge(u_ready, 48)
            ffn_swiglu(2, "up2")
            norm_act(5, (h_ready, 40), "down2")

        @block.vector
        def _(dve):
            v = nc.vector
            TT, TS, STT = v.tensor_tensor, v.tensor_scalar, v.scalar_tensor_tensor

            def norm_apply(n, gain, k0):
                dve.wait_ge(rt_done, n + 1)
                dve_link(dve, v.reciprocal(slot[3][:, :], slot[3][:, :]))
                for c in range(DC + 1):
                    if c < DC:
                        if c >= 2:
                            dve.wait_ge(u_ready, k0[1] + c - 1)
                        STT(slot[4 + c % 2][:, :], h[:, c, :], V(gain, c), slot[3][:, :], ALU.mult, ALU.mult)\
                            .then_inc(ux_done, 1)
                    if c >= 1:
                        dve.wait_ge(u_part, k0[1] + c)
                        TT(u_lo[:, c - 1, :], slot[4 + (c - 1) % 2][:, :], u_hi[:, c - 1, :].bitcast(F32),
                           ALU.subtract).then_inc(u_ready, 1)

            def post_add(n):
                dve.wait_ge(po_sq, DC * n + 2)
                TT(slot[2][:, :], slot[0][:, :], slot[1][:, :], ALU.add).then_inc(po_acc, 1)
                for c in range(2, DC):
                    post_add_one(n, c)

            def post_add_one(n, c):
                dve.wait_ge(po_sq, DC * n + c + 1)
                dve.wait_ge(po_acc, 7 * n + c - 1)
                TT(slot[2][:, :], slot[2][:, :], slot[c % 2][:, :], ALU.add).then_inc(po_acc, 1)

            def post_apply(n, gain, mo):
                dve.wait_ge(po_rt, n + 1)
                dve_link(dve, v.reciprocal(slot[3][:, :], slot[3][:, :]))
                for c in range(DC + 1):
                    if c < DC:
                        if c >= 2:
                            dve.wait_ge(h_ready, DC * n + c - 1)
                        STT(slot[4 + c % 2][:, :], mo[:, c, :], V(gain, c), slot[3][:, :], ALU.mult, ALU.mult)\
                            .then_inc(dve_step, 1)
                        steps["dve"] += 1
                    if c >= 1:
                        dve.wait_ge(dve_step, steps["dve"] - (1 if c < DC else 0))
                        TT(h[:, c - 1, :], h[:, c - 1, :], slot[4 + (c - 1) % 2][:, :], ALU.add).then_inc(h_ready, 1)

            def attention(a, items, s_buf, st_buf, between):
                def biased(j):
                    bias, init, _, nk_ = items[j]
                    dve.wait_ge(a.s_done, j + 1)
                    if j >= 3:
                        dve.wait_ge(a.t_done, between(j - 3))
                    v.tensor_tensor_reduce(s_buf[:, j % 3, 0:nk_], bank[j % 2][:, 0:nk_], bias, -1.0, init,
                                           ALU.add, ALU.min, st_buf[:, j % 8:j % 8 + 1]).then_inc(a.m_done, 1)

                def norm(j):
                    _, init, gate, nk_ = items[j]
                    dve.wait_ge(a.e_done, j + 1)
                    den = st_buf[:, 8 + j % 8:9 + j % 8]
                    if gate is None:
                        dve_link(dve, TT(den, den, st_buf[:, 24 + j % 8:25 + j % 8], ALU.add))
                    dve_link(dve, v.reciprocal(st_buf[:, 16 + j % 8:17 + j % 8], den))
                    r = st_buf[:, 16 + j % 8:17 + j % 8]
                    if gate is None:
                        ins = TS(s_buf[:, j % 3, 0:nk_], s_buf[:, j % 3, 0:nk_], r, None, ALU.mult)
                    else:
                        ins = TS(s_buf[:, j % 3, 0:nk_], s_buf[:, j % 3, 0:nk_], r, gate, ALU.mult, ALU.mult)
                    ins.then_inc(a.p_done, 1)
                return biased, norm

            def ffn_gate(n, name):
                for c in range(FC + 1):
                    if c < FC:
                        dve.wait_ge(dense_done, group_of(name, 2 * c + 1))
                        dve.wait_ge(up_act, FC * n + c + 1)
                        TT(slot[c % 2][:, :], slot[c % 2][:, :], out_bank(name, 2 * c + 1)[:, :], ALU.mult)\
                            .then_inc(a_raw, 1)
                    if c >= 1:
                        dve.wait_ge(a_part, FC * n + c)
                        TT(a_lo[:, c - 1, :], slot[(c - 1) % 2][:, :], a_hi[:, c - 1, :].bitcast(F32),
                           ALU.subtract).then_inc(a_ready, 1)

            def add_half(name, scale):
                for c in range(DC):
                    dve.wait_ge(dense_done, group_of(name, c))
                    STT(h[:, c, :], out_bank(name, c)[:, :], scale, h[:, c, :], ALU.mult, ALU.add).then_inc(h_ready, 1)

            v.memset(small[:, 250:251], EPS).then_inc(pool_step, 1)
            v.memset(small[:, 251:252], 1.0).then_inc(pool_step, 1)
            dve.wait_ge(in_loaded, 48)
            dve.wait_ge(x_loaded, 32)
            norm_apply(0, "mix_pre", (0, 0))
            for c in range(12):
                dve.wait_ge(cv_lin, c + 1)
                src, dst = out_bank("qkv", c), slot[c % 2]
                for n, tap in ((1, 2), (2, 1), (3, 0)):
                    ins = STT(dst[:, n:S], src[:, 0:S - n], V("conv_qkv", 4 * c + tap), dst[:, n:S], ALU.mult, ALU.add)
                    if n < 3:
                        dve_link(dve, ins)
                ins.then_inc(cv_done, 1)
            dve.wait_ge(c1_loaded, 32)
            dve.wait_ge(u_ready, 8)
            dve_link(dve, v.tensor_copy(masks[:, :, :], masks_in[:, :, :]))
            dve.wait_ge(rows1_done, 3)
            dve_link(dve, TS(a_gate[0:4, :], a_gate[0:4, :], V("dt_bias")[0:4, :], None, ALU.add))
            STT(sp1[0:4, :], a_gate[0:4, :], -1.0, a_gate[0:4, :], ALU.mult, ALU.min).then_inc(sp_done, 1)
            dve.wait_ge(sp_exp, 1)
            dve_link(dve, STT(sp2[0:4, :], a_gate[0:4, :], 0.0, sp2[0:4, :], ALU.max, ALU.add))
            dve_link(dve, TS(sp2[0:4, :], sp2[0:4, :], na_col[0:4, :], -1.0, ALU.mult, ALU.mult))
            dve.wait_ge(c1_loaded, 32)
            v.tensor_tensor_scan(g_sum[0:4, :], rowmask[0:4, :], sp2[0:4, :], 0.0, ALU.mult, ALU.add)\
                .then_inc(g_done, 1)
            for c in range(8):
                if c == 0:
                    dve.wait_ge(len_done, 1)
                STT(qkv[:, c, :], qkv[:, c, :], P ** -0.5 if c < 4 else 1.0, lens[:, c, :], ALU.mult,
                    ALU.mult).then_inc(l2_done, 1)
            dve.wait_ge(tr1_done, 1)
            v.tensor_copy(small[:, 0:32], misc[0][:, 0:32]).then_inc(cols_done, 1)
            v.tensor_copy(small[:, 96:192], misc[0][:, 64:160]).then_inc(cols_done, 1)
            dve.wait_ge(bc_copied, 4)
            dve.wait_ge(cols_done, 2)
            TT(tail_col, g_row[:, :, P - 1::P].rearrange("p h t -> p t h"), cols1[:, :, 0:4], ALU.subtract)\
                .then_inc(ecol_in, 1)
            dve.wait_ge(ecol_done, 3)
            dve_link(dve, TT(bg_col, e_col, cols1[:, :, 4:8], ALU.mult))

            def wide(col, tt):
                return col[:, tt, :].unsqueeze(2).broadcast_to([P, GH, P])

            for tt in range(NT):
                dve.wait_ge(kv_tr, 2 * tt + 1)
                TT(wk_t[:, tt, :, :], heads(misc[0]), wide(bg_col, tt), ALU.mult).then_inc(kv_done, 1)
                TT(kt_t[:, tt, :, :], heads(misc[0]), wide(tail_col, tt), ALU.mult).then_inc(kv_done, 1)
                dve.wait_ge(kv_tr, 2 * tt + 2)
                TT(vb_t[:, tt, :, :], heads(misc[3]), wide(cols1[:, :, 4:8], tt), ALU.mult).then_inc(kv_done, 1)

            def head_mask(i):
                return masks[:, i, :].unsqueeze(1).broadcast_to([P, GH, P])

            dve.wait_ge(l2_done, 8)
            for tt in range(NT):
                cut = slice(tt * P, (tt + 1) * P)
                for hd in range(GH):
                    ins = TS(dec[:, tt % 2, hd, :], g_row[:, hd, cut], cols1[:, tt, hd:hd + 1], 0.0, ALU.subtract, ALU.min)
                ins.then_inc(dc_in, 1)
                dve.wait_ge(dc_exp, tt + 1)
                dve_link(dve, TT(dmask[:, tt % 2, :, :], dec[:, tt % 2, :, :], head_mask(7), ALU.mult))
                dve.wait_ge(kk_done, 2 * tt + 1)
                TT(at_t[:, tt, :, :], heads(misc[1]), dmask[:, tt % 2, :, :], ALU.mult).then_inc(at_done, 1)
                dve.wait_ge(kk_done, 2 * tt + 2)
                TT(qk_t[:, tt, :, :], heads(misc[2]), dmask[:, tt % 2, :, :], ALU.mult).then_inc(at_done, 1)
            eye = ident[:, :].unsqueeze(1).broadcast_to([P, GH, P])

            def level_cut(n):
                if n < NT:
                    dve.wait_ge(at_beta, n + 1)
                else:
                    dve.wait_ge(x_done, n - 3)
                    if n < 2 * NT:
                        dve.wait_ge(u_upd, n - 3)
                TT(am[:, n % 4, :, :], at_t[:, n % NT, :, :], head_mask(n // NT), ALU.mult).then_inc(am_done, 1)

            n_all = LEVELS * NT
            for n in range(3):
                level_cut(n)
            for n in range(n_all):
                tt, final = n % NT, n >= n_all - NT
                if n + 3 < n_all:
                    level_cut(n + 3)
                if n < NT:
                    dve.wait_ge(at_beta, NT)
                    dve.wait_ge(am_done, n + 1)
                    TT(u_inv[:, tt, :, :], eye, am[:, n % 4, :, :], ALU.subtract).then_inc(u_upd, 1)
                    dve.wait_ge(x_done, n + 1)
                    TT(t_inv[:, tt, :, :], eye, heads(bank[n % 2]), ALU.subtract).then_inc(t_upd, 1)
                    dve.wait_ge(eg_done, n + 1)
                    TT(qkv[:, n, :], qkv[:, n, :], g_row[:, n, :], ALU.mult).then_inc(qd_done, 1)
                    continue
                k = 2 * (n - NT) if not final else 2 * (n_all - 2 * NT) + (n - (n_all - NT))
                if not final:
                    dve.wait_ge(txu_done, k + 1)
                    TT(t_inv[:, tt, :, :], t_inv[:, tt, :, :], heads(bank[2 + n % 2]), ALU.subtract).then_inc(t_upd, 1)
                    dve.wait_ge(txu_done, k + 2)
                else:
                    dve.wait_ge(txu_done, k + 1)
                TT(u_inv[:, tt, :, :], u_inv[:, tt, :, :], heads(misc[n % 2]), ALU.subtract).then_inc(u_upd, 1)
            for tt in range(NT - 1):
                dve.wait_ge(ds_done, tt + 1)
                if tt == 0:
                    v.tensor_copy(state[:, 0, :, :], heads(bank[3])).then_inc(s_upd, 1)
                else:
                    dve.wait_ge(s_upd, tt)
                    for hd in range(GH):
                        ins = STT(state[:, tt % 2, hd, :], state[:, (tt - 1) % 2, hd, :], gl_col[:, tt, hd:hd + 1],
                                  bank[3][:, hd * P:(hd + 1) * P], ALU.mult, ALU.add)
                    ins.then_inc(s_upd, 1)
            for hd in range(GH):
                dve.wait_ge(head_rt, 8 + hd + 1)
                r = slot[2 + hd % 2]
                dve_link(dve, v.reciprocal(r[:, :], r[:, :]))
                dve_link(dve, STT(o_t[:, hd, :], o_t[:, hd, :], V("gdn_norm"), r[:, :], ALU.mult, ALU.mult))
                dve.wait_ge(z_silu, hd + 1)
                TT(o_t[:, hd, :], o_t[:, hd, :], xs[:, hd % 2, :, :].rearrange("p a b -> p (a b)"), ALU.mult)\
                    .then_inc(y_done, 1)
                dve.wait_ge(ya_part, hd + 1)
                TT(ya_lo[:, hd, :], o_t[:, hd, :], ya_hi[:, hd, :].bitcast(F32), ALU.subtract).then_inc(ya_ready, 1)

            for b in range(2):
                v.memset(z_raw[b][:, :, S - 1:528], 0.0).then_inc(zp_zero, 1)
            dve.wait_ge(c2_loaded, 80)
            for b in range(2):
                dve.wait_ge(z_copied, 4 * b + 4)
                for half in range(2):
                    src = z_raw[b][:, :, 16 * half:16 * half + S].rearrange("p g (w i two) -> p g w i two", i=8, two=2)
                    i8 = slice(8 * half, 8 * half + 8)
                    dst = zc[:, b, i8, :, :].rearrange("p i g w -> p g w i")
                    for gr in range(NG):
                        add = pos[:, b, i8].unsqueeze(1).broadcast_to([P, 32, 8])
                        ins = TT(dst[:, gr, :, :], src[:, gr, :, :, 0], add, ALU.add)
                    ins.then_inc(zc_sum, 1)
            for b in range(2):
                dve.wait_ge(zc_part, b + 1)
                TT(zc_lo[:, b, :, :, :], zc[:, b, :, :, :], zc_hi[:, b, :, :, :].bitcast(F32), ALU.subtract)\
                    .then_inc(zc_ready, 1)
            a0 = att[0]
            c_m, c_r = st[:, 32:40], st[:, 40:48]

            def cmp_front(qt):
                dve.wait_ge(cs_done, qt + 1)
                if qt >= 1:
                    dve.wait_ge(a0.t_done, 18 * qt - 16)
                for gr in range(NG):
                    ins = TT(c_s[:, 4 * gr:4 * gr + 4, :], bank[2 + gr][:, 0:4 * NCMP].rearrange("p (h n) -> p h n", h=4),
                             c_bias[:, qt, 4 * gr:4 * gr + 4, :], ALU.add)
                dve_link(dve, ins)
                dve_link(dve, v.tensor_reduce(c_m, c_s[:, :, :], AX.X, ALU.max))
                TT(c_s[:, :, :], c_s[:, :, :], c_m.unsqueeze(2).broadcast_to([P, NH, NCMP]), ALU.subtract)\
                    .then_inc(cs_shift, 1)

            def cmp_back(qt):
                dve.wait_ge(cs_exp, qt + 1)
                dve_link(dve, v.tensor_reduce(c_r, c_s[:, :, :], AX.X, ALU.add))
                dve_link(dve, v.reciprocal(c_r, c_r))
                dve_link(dve, TT(c_r, c_r, gate_col[:, qt, 0:24:3], ALU.mult))
                dve_link(dve, TT(c_s[:, :, :], c_s[:, :, :],
                                 c_mask[:, qt, :].unsqueeze(1).broadcast_to([P, NH, NCMP]), ALU.mult))
                TT(c_s[:, :, :], c_s[:, :, :], c_r.unsqueeze(2).broadcast_to([P, NH, NCMP]), ALU.mult)\
                    .then_inc(cp_ready, 1)

            items = []
            for qt in range(NT):
                for hd in range(NH):
                    for b in range(2):
                        items.append((alibi[:, hd, (3 - qt) * P:S], BIG,
                                      gate_col[:, qt, 3 * hd + 1 + b:3 * hd + 2 + b], (qt + 1) * P))
            biased, norm = attention(a0, items, n_s, st, lambda i: 18 * (i // 16) + 2 + i % 16 + 1)
            dve.wait_ge(c2_loaded, 80)
            dve.wait_ge(hid_done, 2)
            cmp_front(0)
            biased(0)
            for j in range(64):
                if j % 16 == 0:
                    if j > 0:
                        cmp_front(j // 16)
                    cmp_back(j // 16)
                if j + 1 < 64:
                    biased(j + 1)
                norm(j)
                if j % 16 == 3 and j > 16:
                    nsa_lo(dve, TT, j // 16 - 1, a0, yb_lo, yb_hi, misc, heads)
            nsa_lo(dve, TT, 3, a0, yb_lo, yb_hi, misc, heads)

            for m in range(DC):
                dve.wait_ge(dense_done, group_of(f"a2d{m}"))
                dve.wait_ge(mixa_sig, 2 * m + 1)
                if m >= 2:
                    dve.wait_ge(mx_ready, m - 1)
                TT(slot[4 + m % 2][:, :], slot[0][:, :], out_bank(f"a2d{m}")[:, :], ALU.mult).then_inc(mix_a, 1)
                dve.wait_ge(dense_done, group_of(f"b2d{m}"))
                dve.wait_ge(mixa_sig, 2 * m + 2)
                dve.wait_ge(mix_a, m + 1)
                if m >= 1:
                    dve.wait_ge(mix_b, m)
                dve_link(dve, TT(slot[2][:, :], slot[1][:, :], out_bank(f"b2d{m}")[:, :], ALU.mult))
                TT(slot[4 + m % 2][:, :], slot[4 + m % 2][:, :], slot[2][:, :], ALU.add).then_inc(mix_b, 1)
                dve.wait_ge(mx_part, m + 1)
                TT(mx_lo[:, m, :], slot[4 + m % 2][:, :], mx_hi[:, m, :].bitcast(F32), ALU.subtract)\
                    .then_inc(mx_ready, 1)
            post_add(0)
            dve.wait_ge(x_loaded, 64)
            post_apply(0, "mix_post", mo_u)
            norm_apply(1, "ffn_pre", (0, 8))
            for c in range(FC + 1):
                if c < FC:
                    for b in range(2):
                        g = b * FC + c
                        dve.wait_ge(up_lin, 2 * c + b + 1)
                        src, dst = out_bank("up", 2 * c + b), slot[2 * b + c % 2]
                        dve_link(dve, STT(dst[:, 1:S], src[:, 0:S - 1], V("conv_ffn", 3 * g + 1), dst[:, 1:S], ALU.mult, ALU.add))
                        STT(dst[:, 2:S], src[:, 0:S - 2], V("conv_ffn", 3 * g), dst[:, 2:S], ALU.mult, ALU.add)\
                            .then_inc(up_conv, 1)
                if c >= 1:
                    dve.wait_ge(a_part, c)
                    TT(a_lo[:, c - 1, :], slot[2 + (c - 1) % 2][:, :], a_hi[:, c - 1, :].bitcast(F32),
                       ALU.subtract).then_inc(a_ready, 1)
                if c < FC:
                    dve.wait_ge(up_act, c + 1)
                    dve.wait_ge(up_conv, 2 * c + 2)
                    TT(slot[2 + c % 2][:, :], slot[2 + c % 2][:, :], slot[c % 2][:, :], ALU.mult).then_inc(a_raw, 1)
            post_add(1)
            post_apply(1, "ffn_post", mo_u)
            for c in range(2):
                dve.wait_ge(ps_part, c + 1)
                TT(p_lo[:, c, :], p_raw[:, c, :], p_hi[:, c, :].bitcast(F32), ALU.subtract).then_inc(ps_ready, 1)
            for c in range(DC):
                dve.wait_ge(u_part, 16 + c + 1)
                TT(u_lo[:, c, :], h[:, c, :], u_hi[:, c, :].bitcast(F32), ALU.subtract).then_inc(u_ready, 1)
            for m in range(DC):
                dve.wait_ge(ple_sig, m + 1)
                TT(mo_a[:, m, :], slot[4 + m % 2][:, :], out_bank(f"ple{m}")[:, :], ALU.mult).then_inc(po_copy, 1)
                if m == 1:
                    dve.wait_ge(po_sq, 16 + 2)
                    TT(slot[2][:, :], slot[0][:, :], slot[1][:, :], ALU.add).then_inc(po_acc, 1)
                elif m >= 2:
                    post_add_one(2, m)
            post_apply(2, "ple_post", mo_a)
            norm_apply(2, "ffn1", (0, 24))
            ffn_gate(1, "up1")
            add_half("down1", 0.5)
            norm_apply(3, "mix2", (0, 32))
            for c in range(8):
                dve.wait_ge(dense_done, group_of("wq", c))
                TS(wq[:, c, :], out_bank("wq", c)[:, :], V("b_wq", c), ND ** -0.5, ALU.add, ALU.mult).then_inc(wq_done, 1)
            dve.wait_ge(c3_loaded, 32)
            for j in range(NT):
                dve.wait_ge(dense_done, group_of("wv", j))
                TT(wv[:, j, :], out_bank("wv", j)[:, 0:256], wvb[:, :], ALU.add).then_inc(wv_done, 1)
            nsink = st2[:, 64:80]
            dve_link(dve, TS(nsink, V("sinks", 0, 16), -1.0, None, ALU.mult))
            items = []
            for qt in range(NT):
                for hd in range(WH):
                    items.append((band[:, P:256] if qt == 0 else band[:, :], nsink[:, hd:hd + 1], None,
                                  min(qt + 1, 2) * P))
            a1 = att[1]
            biased, norm = attention(a1, items, w_s, st2, lambda i: i + 1)

            def win_lo(n):
                qt, c = divmod(n, 2)
                dve.wait_ge(a1.o_part, n + 1)
                cut = slice(qt * P, (qt + 1) * P)
                TT(yw_lo[:, 4 * c:4 * c + 4, cut], heads(misc[2 + c]), yw_hi[:, 4 * c:4 * c + 4, cut].bitcast(F32),
                   ALU.subtract).then_inc(a1.o_ready, 1)

            biased(0)
            for j in range(64):
                if j + 1 < 64:
                    biased(j + 1)
                norm(j)
                if j % 8 == 3 and j > 8:
                    win_lo(j // 8 - 1)
            win_lo(7)
            for m in range(DC):
                dve.wait_ge(dense_done, group_of(f"proj_w{m}"))
                dve.wait_ge(sg_done, m + 1)
                STT(ma[:, m, :], out_bank(f"proj_w{m}")[:, :], 1.0, sg[:, m % 2, :], ALU.mult, ALU.mult)\
                    .then_inc(ma_done, 1)
            for c in range(8):
                dve.wait_ge(mqk_lin, c + 1)
                if c >= 2:
                    dve.wait_ge(mqk_silu, c - 1)
                src, dst = slot[c % 2], cb2[:, c % 2, :]
                dve_link(dve, TS(dst, src[:, :], V("mconv", 4 * c + 3), None, ALU.mult))
                for n, tap in ((1, 2), (2, 1), (3, 0)):
                    ins = STT(dst[:, n:S], src[:, 0:S - n], V("mconv", 4 * c + tap), dst[:, n:S], ALU.mult, ALU.add)
                    if n < 3:
                        dve_link(dve, ins)
                ins.then_inc(mqk_conv, 1)
            dve_link(dve, v.memset(r_one[0:8, :], 1.0))
            dve.wait_ge(r2_act, 5)
            v.tensor_tensor_scan(r_raw[0:8, :], r_one[0:8, :], r_f[0:8, :], 0.0, ALU.mult, ALU.subtract)\
                .then_inc(r2_dve, 1)
            dve.wait_ge(r2_dve, 1)
            STT(r_a[0:8, :], r_i[0:8, :], 15.0, r_raw[0:8, :], ALU.mult, ALU.subtract).then_inc(r2_dve, 1)
            dve.wait_ge(r2_dve, 2)
            v.tensor_tensor_scan(r_f[0:8, :], r_one[0:8, :], r_a[0:8, :], 0.0, ALU.mult, ALU.max).then_inc(r2_dve, 1)
            dve.wait_ge(r2_dve, 3)
            TT(r_raw[0:8, :], r_raw[0:8, :], r_f[0:8, :], ALU.add).then_inc(r2_dve, 1)
            dve.wait_ge(c4_loaded, 32)
            for hf in range(2):
                for j in range(NT):
                    dve.wait_ge(dense_done, group_of(f"mv{hf}", j))
                    TT(mv[:, j, hf * S:(hf + 1) * S], out_bank(f"mv{hf}", j)[:, :], mvb[:, hf * S:(hf + 1) * S], ALU.add)\
                        .then_inc(mv_done, 1)
            dve.wait_ge(ac_tr, 1)
            v.tensor_copy(small[:, 0:32], misc[0][:, 0:32]).then_inc(ac_done, 1)
            dve.wait_ge(mqk_silu, 8)
            v.memset(small[:, 252:253], 0.0).then_inc(r2_dve, 1)
            for hd in range(MH):
                dve.wait_ge(mb_done, hd + 1)
                if hd >= 1:
                    dve.wait_ge(mnd_done, 3 * hd)
                else:
                    dve.wait_ge(ac_done, 1)
                for j in range(NT):
                    ins = TS(wsc[:, j * P:(j + 1) * P], bank[0][:, j * P:(j + 1) * P], acol[:, j, hd:hd + 1], 0.0,
                             ALU.subtract, ALU.max)
                ins.then_inc(mdg_in, 1)
                dve.wait_ge(mw_exp, hd + 1)
                w4 = wsc[:, 0:S].rearrange("p (h c) -> p h c", h=NT)
                dve_link(dve, TT(w4, w4, incl2.unsqueeze(1).broadcast_to([P, NT, P]), ALU.mult))
                dve.wait_ge(msc_done, hd + 1)
                for lo, n, b in ((0, 512, 1), (512, 512, 2), (1024, 256, 3)):
                    STT(wsc[:, lo:lo + n], bank[b][:, 0:n], ND ** -0.5, wsc[:, lo:lo + n], ALU.mult, ALU.mult)\
                        .then_inc(mws, 1)
                dve.wait_ge(mnd_done, 3 * hd + 2)
                dve.wait_ge(meb_copied, hd + 1)
                if hd >= 1:
                    dve.wait_ge(mh_ready, hd)
                dve_link(dve, STT(em_b[:, :], misc[1][:, :], -1.0, em_b[:, :], ALU.mult, ALU.max))
                dve_link(dve, TT(em_b[:, :], misc[1][:, :], em_b[:, :], ALU.max))
                v.reciprocal(em_b[:, :], em_b[:, :]).then_inc(mhn, 1)
                dve.wait_ge(mnd_done, 3 * hd + 3)
                dve.wait_ge(mhn, 2 * hd + 1)
                TT(hn[:, :], misc[0][:, :], em_b[:, :], ALU.mult).then_inc(mhn, 1)
                dve.wait_ge(head_rt, 12 + hd + 1)
                dve_link(dve, v.reciprocal(mr[:, :], mr[:, :]))
                dve_link(dve, STT(hn[:, :], hn[:, :], V("head_norm", hd), mr[:, :], ALU.mult, ALU.mult))
                TT(hn[:, :], hn[:, :], so[:, hd, :], ALU.mult).then_inc(mh_y, 1)
                dve.wait_ge(mh_part, hd + 1)
                TT(m_lo[:, hd, :], hn[:, :], m_hi[:, hd, :].bitcast(F32), ALU.subtract).then_inc(mh_ready, 1)
            for m in range(DC):
                dve.wait_ge(dense_done, group_of(f"proj_m{m}"))
                dve.wait_ge(sg_done, 8 + m + 1)
                if m >= 2:
                    dve.wait_ge(mg_in, m - 1)
                dve_link(dve, TT(slot[2 + m % 2][:, :], slot[m % 2][:, :], out_bank(f"proj_m{m}")[:, :], ALU.mult))
                TT(ma[:, m, :], ma[:, m, :], slot[2 + m % 2][:, :], ALU.add).then_inc(mg_in, 1)
                dve.wait_ge(mg_part, m + 1)
                TT(mg_lo[:, m, :], ma[:, m, :], mg_hi[:, m, :].bitcast(F32), ALU.subtract).then_inc(mg_ready, 1)
            add_half("out", 1.0)
            norm_apply(4, "ffn2", (0, 40))
            ffn_gate(2, "up2")
            add_half("down2", 0.5)
            dve.wait_ge(rt_done, 6)
            dve_link(dve, v.reciprocal(hn[:, :], slot[3][:, :]))
            for c in range(DC):
                STT(result[:, c, :], h[:, c, :], V("final", c), hn[:, :], ALU.mult, ALU.mult).then_inc(f_out, 1)


def nsa_lo(dve, TT, qt, a, yb_lo, yb_hi, misc, heads):
    dve.wait_ge(a.o_part, qt + 1)
    cut = slice(qt * P, (qt + 1) * P)
    TT(yb_lo[:, :, cut], heads(misc[2 + qt % 2]), yb_hi[:, :, cut].bitcast(F32), ALU.subtract).then_inc(a.o_ready, 1)


def layout(x, inp):
    I = {k: np.asarray(v) for k, v in inp.items()}
    one = lambda n: I[n][0]
    win = one("w_in")
    o = np.cumsum([0, 512, 512, 512, 512, 4, 4, 512, 128, 128, 128, 128, 128, 128, 24, 2048])
    (qa, ka, va, za, ba, aa, qb, kcm, vcm, ksl, vsl, kwi, vwi, gn, gm) = [win[:, a:b] for a, b in zip(o[:-1], o[1:])]
    zero = lambda n: np.zeros((D, n), np.float32)
    rows1 = np.concatenate([ba, zero(28), aa, zero(28), gn, zero(40)], 1)
    order = [g * 4 + c for c in range(4) for g in range(2)]
    pick = lambda w, heads_: np.concatenate([w[:, 64 * i:64 * i + 64] for i in heads_], 1)
    twice = lambda w: np.concatenate([w, w], 1)
    w2i = one("w_in_2")
    o2 = np.cumsum([0, 1024, 256, 256, 512, 512, 1024, 1024, 8, 8, 2048])
    cut2 = [slice(a, b) for a, b in zip(o2[:-1], o2[1:])]
    worder = [(2 * p_ + s) * 4 + r for p_ in range(2) for r in range(4) for s in range(2)]
    rows2 = np.concatenate([w2i[:, cut2[7]], zero(24), w2i[:, cut2[8]], zero(88)], 1)
    rowpick = lambda w, heads_: np.concatenate([w[64 * i:64 * i + 64] for i in heads_], 0)
    w_b2d = rowpick(one("w_b2d"), order)
    w_pa = rowpick(one("w_proj_attn_2"), worder)
    up = one("w_up")

    def pairs(a, b):
        a, b = a.reshape(D, FC, 1, P), b.reshape(D, FC, 1, P)
        return np.concatenate([a, b], 2).reshape(D, 2 * FF)

    mats = {
        "qkv": np.concatenate([qa, ka, va], 1), "rows1": rows1,  "nq": pick(qb, order),
        "nk": np.concatenate([ksl, kwi], 1),
        "ncmp": np.concatenate([twice(kcm[:, :64]), twice(kcm[:, 64:]), twice(vcm[:, :64]), twice(vcm[:, 64:])], 1),
        "nv": np.concatenate([vsl, vwi], 1), "cmpk": one("cmp_w1_k"), "cmpv": one("cmp_w1_v"),
        "w_o": one("w_o"), "up": pairs(up[:, :FF], up[:, FF:]), "down": one("w_down"),
        "up1": pairs(one("ffn1_w_gate_2"), one("ffn1_w_up_2")), "down1": one("ffn1_w_down_2"),
        "up2": pairs(one("ffn2_w_gate_2"), one("ffn2_w_up_2")), "down2": one("ffn2_w_down_2"),
        "wq": pick(w2i[:, cut2[0]], worder), "wk": w2i[:, cut2[1]], "wv": w2i[:, cut2[2]],
        "mqk": np.concatenate([w2i[:, cut2[3]], w2i[:, cut2[4]]], 1), "rows2": rows2,
        "mv0": w2i[:, cut2[5]][:, :512], "mv1": w2i[:, cut2[5]][:, 512:], "mo": w2i[:, cut2[6]],
        "out": one("w_out_2"),
    }
    g2 = w2i[:, cut2[9]]
    mats.update({f"z{i}": za[:, i * P:(i + 1) * P] for i in range(GH)})
    for m in range(DC):
        c = slice(m * P, (m + 1) * P)
        mats[f"gate_a{m}"], mats[f"gate_b{m}"] = gm[:, :D][:, c], gm[:, D:][:, c]
        mats[f"a2d{m}"], mats[f"b2d{m}"] = one("w_a2d")[:, c], w_b2d[:, c]
        mats[f"ple{m}"], mats[f"ple_gate{m}"] = one("w_ple")[:, c], one("w_ple_gate")[:, c]
        mats[f"gate_w{m}"], mats[f"gate_m{m}"] = g2[:, :D][:, c], g2[:, D:][:, c]
        mats[f"proj_w{m}"], mats[f"proj_m{m}"] = w_pa[:, c], one("w_proj_mlstm_2")[:, c]
    stream = np.zeros((NSLABS * SLAB, P, P), np.float32)
    for name, chunks, k, width in dense_layers():
        at = START[name][0]
        w = mats[name]
        b = w.reshape(k, P, w.shape[1] // P, P)
        b = b.transpose(0, 2, 1, 3) if width else b.transpose(2, 0, 1, 3)
        n = b.shape[0] * b.shape[1]
        stream[at:at + n] = b.reshape(n, P, P)
    weights = np.ascontiguousarray(stream.reshape(NSLABS, SLAB, P, P).transpose(0, 2, 1, 3))

    vec = np.zeros((P, NVEC), np.float32)

    def put(name, a):
        a = np.asarray(a)
        vec[:a.shape[0], VECS[name]:VECS[name] + a.shape[1]] = a

    cols = lambda a: a.reshape(-1, P).T
    taps = lambda w: w.T.reshape(-1, P, w.shape[0]).transpose(1, 0, 2).reshape(P, -1)
    put("mix_pre", cols(one("norm_mix_pre")))
    put("conv_qkv", taps(one("conv_qkv")))
    put("gdn_norm", one("gdn_norm")[:, None])
    put("mix_post", cols(one("norm_mix_post")))
    put("ffn_pre", cols(one("norm_ffn_pre")))
    put("conv_ffn", taps(one("conv_ffn")))
    put("conv_ffn_b", cols(one("conv_ffn_b")))
    put("ffn_post", cols(one("norm_ffn_post")))
    put("ple_post", cols(one("norm_ple_post")))
    put("ffn1", cols(one("ffn1_norm_2")))
    put("mix2", cols(one("mix_norm_2")))
    bi = one("b_in_2")
    put("b_wq", cols(pick(bi[None, cut2[0]], worder)[0]))
    put("b_wk", cols(bi[cut2[1]]))
    put("b_mqk", cols(np.concatenate([bi[cut2[3]], bi[cut2[4]]])))
    put("b_mo", cols(bi[cut2[6]]))
    put("b_rows2", np.concatenate([bi[cut2[7]], np.zeros(24, np.float32), bi[cut2[8]]])[:, None])
    put("b_gate", cols(bi[cut2[9]]))
    put("mconv", taps(one("mlstm_conv_2")))
    put("head_norm", one("mlstm_head_norm_2").T)
    put("ffn2", cols(one("ffn2_norm_2")))
    put("final", cols(I["final_norm_2"]))
    put("a_log", one("a_log")[:, None])
    put("dt_bias", one("dt_bias")[:, None])
    put("sinks", np.broadcast_to(one("attn_sinks_2")[None], (P, WH)))

    j, i = np.arange(P)[:, None], np.arange(P)[None, :]
    masks = np.zeros((P, 8, P), np.float32)
    for lv in range(LEVELS):
        m = 1 << lv
        masks[:, lv] = (j // (2 * m) == i // (2 * m)) & ((i // m) % 2 == 1) & ((j // m) % 2 == 0)
    masks[:, 7] = i >= j
    rowmask = np.broadcast_to((np.arange(S) % P != 0).astype(np.float32), (P, S))
    q, xk = np.arange(P)[:, None], np.arange(S)[None, :] - 384
    slope = 2.0 ** (-8.0 * np.arange(1, NH + 1) / NH)
    alibi = np.where(xk <= q, 0, 1)[:, None, :] * -1e30 + np.where(xk <= q, xk - q, 0)[:, None, :] * slope[None, :, None]
    tq = np.arange(NT)[None, :] * P + np.arange(P)[:, None]
    dist = tq[:, :, None] - (np.arange(NCMP) * CS + CL - 1)[None, None, :]
    c_mask = (dist >= 0).astype(np.float32)
    c_bias = np.where(dist[:, :, None, :] >= 0, -slope[None, None, :, None] * dist[:, :, None, :], -1e30)
    kj, qi = np.arange(2 * P)[None, :], np.arange(P)[:, None]
    band = np.where((kj > qi) & (kj <= qi + P), 0.0, -1e30)
    pos = np.stack([one(n).reshape(16, P).T for n in ("cmp_pos_k", "cmp_pos_v")], 1)
    w2 = np.stack([one(n).reshape(2, P, ND).transpose(1, 0, 2) for n in ("cmp_w2_k", "cmp_w2_v")], 1)
    f = lambda a: np.ascontiguousarray(a, dtype=np.float32)
    fm = lambda a: f(a.T.reshape(-1, P, S).transpose(1, 0, 2))
    return {
        "weights": weights, "x": fm(x[0]), "p": fm(I["p"][0, 0]), "vec": vec,
        "ident": f(np.eye(P)), "ones": f(np.ones((P, P))), "masks": f(masks),
        "incl": f(masks[:, 7]), "rowmask": f(rowmask),
        "alibi": f(alibi), "c_bias": f(c_bias), "c_mask": f(c_mask), "band": f(band), "pos": f(pos), "w2": f(w2),
        "wvb": f(np.broadcast_to(bi[cut2[2]], (P, 256))), "mvb": f(np.broadcast_to(bi[cut2[5]], (P, 1024))),
    }


def kernel(**inputs):
    import concourse.bacc as bacc
    from concourse.bass_utils import run_bass_kernel_spmd

    x = np.asarray(inputs.pop("x"))
    arrays = layout(x, inputs)
    nc = bacc.Bacc("TRN2", target_bir_lowering=False, num_devices=1)
    t = {n: nc.dram_tensor(f"in_{n}", a.shape, mybir.dt.from_np(a.dtype), kind="ExternalInput").ap()
         for n, a in arrays.items()}
    t["out"] = nc.dram_tensor("out", (P, DC, S), F32, kind="ExternalOutput").ap()
    build(nc, t)
    r = run_bass_kernel_spmd(nc, [{f"in_{n}": a for n, a in arrays.items()}], core_ids=[0])
    out = r.results[0]["out"]
    return np.ascontiguousarray(out.transpose(1, 0, 2).reshape(D, S).T)[None]
```

```python
from contextlib import ExitStack

import numpy as np

import concourse.bass as bass
from concourse import mybir

F32 = mybir.dt.float32
F32R = mybir.dt.float32r
BF16 = mybir.dt.bfloat16
ALU = mybir.AluOpType
ACT = mybir.ActivationFunctionType
AX = mybir.AxisListType

P = 128
S = 512
NT = S // P
D = 1024
DC = D // P
KB = 1024

SLAB = 8
RAWS = 4
SPLITS = 5
LEAD = 3

GH = 4
LEVELS = 7
NH, NG, ND = 8, 2, 64
CL, CS, NCMP = 32, 16, 31
WH, WKV = 16, 4
MH = 8
FF = 2816
FC = FF // P
EARLY = 3
EPS = 1e-6
BIG = 3.0e38


def dense_layers():
    a = [("qkv", 12, 8, 0), ("rows1", 1, 8, 0), ("nq", 4, 8, 0), ("nk", 2, 8, 0),
         ("z0", 1, 8, 0), ("z1", 1, 8, 0), ("z2", 1, 8, 0), ("z3", 1, 8, 0), ("ncmp", 4, 8, 0), ("nv", NT, 8, 2),
         ("cmpk", 1, 16, 2), ("cmpv", 1, 16, 2)]
    a += [(f"gate_{x}{m}", 1, 8, 0) for m in range(EARLY) for x in "ab"]
    for m in range(DC):
        gate = lambda x: [(f"gate_{x}{m}", 1, 8, 0)] if m >= EARLY else []
        a += gate("a") + [(f"a2d{m}", 1, 4, 0)] + gate("b") + [(f"b2d{m}", 1, 4, 0)]
    a += [("w_o", 8, 8, 0), ("up", 2 * FC, 8, 0), ("down", 8, FC, 0)]
    for m in range(DC):
        a += [(f"ple{m}", 1, 2, 0), (f"ple_gate{m}", 1, 8, 0)]
    a += [("up1", 2 * FC, 8, 0), ("down1", 8, FC, 0),
          ("wq", 8, 8, 0), ("wk", 2, 8, 0), ("wv", NT, 8, 2)]
    a += [(f"gate_w{m}", 1, 8, 0) for m in range(DC)] + [(f"proj_w{m}", 1, 8, 0) for m in range(DC)]
    a += [("mqk", 8, 8, 0), ("rows2", 1, 8, 0), ("mv0", NT, 8, 4), ("mv1", NT, 8, 4), ("mo", 8, 8, 0)]
    for m in range(DC):
        a += [(f"gate_m{m}", 1, 8, 0), (f"proj_m{m}", 1, 8, 0)]
    a += [("out", 8, 8, 0), ("up2", 2 * FC, 8, 0), ("down2", 8, FC, 0)]
    return a


def dense_plan():
    tile = group = 0
    start = {}
    for name, chunks, k, width in dense_layers():
        start[name] = (tile, group)
        tile += k * (width or chunks)
        group += chunks
    return start, tile, group


START, TILES, GROUPS = dense_plan()
ABREAST = ("qkv", "up", "up1", "wq", "up2")


def tile_at(name, k, m, i):
    if name in ABREAST and m < 4:
        return START[name][0] + 4 * i + m
    return START[name][0] + k * m + i


NSLABS = -(-TILES // SLAB)

VECS = {}


def _vec_layout():
    at = 0
    for name, n in (("mix_pre", 8), ("conv_qkv", 48), ("gdn_norm", 1), ("mix_post", 8), ("ffn_pre", 8),
                    ("conv_ffn", 132), ("conv_ffn_b", 44), ("ffn_post", 8), ("ple_post", 8),
                    ("ffn1", 8), ("mix2", 8), ("b_wq", 8), ("b_wk", 2), ("b_mqk", 8), ("b_mo", 8),
                    ("b_rows2", 1), ("b_gate", 16), ("mconv", 32), ("head_norm", 8), ("ffn2", 8),
                    ("final", 8), ("a_log", 1), ("dt_bias", 1), ("sinks", 16)):
        VECS[name] = at
        at += n
    return at


NVEC = _vec_layout()


def build(nc, t):
    ctx = ExitStack()
    with ctx:
        base = 16512

        def at(name, offset, shape, dt=F32):
            return nc.alloc_sbuf_tensor_at(name, [P] + shape, dt, offset=base + offset)

        def sem(name):
            return ctx.enter_context(nc.semaphore(name))

        raw = at("raw", 0, [RAWS, SLAB, P])
        w_hi = at("w_hi", 16 * KB, [SPLITS, SLAB, P], F32R)
        w_lo = at("w_lo", 36 * KB, [SPLITS, SLAB, P], F32R)
        h = at("h", 56 * KB, [DC, S])
        u_hi = at("u_hi", 72 * KB, [DC, S], F32R)
        u_lo = at("u_lo", 88 * KB, [DC, S], F32R)
        mo_u = at("mo_u", 72 * KB, [DC, S])
        vec = at("vec", 104 * KB, [448])
        ident = at("ident", 104 * KB + 1792, [P])
        ones = at("ones", 104 * KB + 2304, [P])
        small = at("small", 104 * KB + 2816, [256])
        A = 104 * KB + 3840
        assert NVEC <= 448

        def arena(name, kb, shape, dt=F32):
            return at(name, A + int(kb * KB), shape, dt)

        slot = [arena(f"slot{i}", 88 + 2 * i, [S]) for i in range(6)]
        sq = [slot[0], slot[1], slot[3]]

        qkv = arena("qkv", 0, [12, S])
        wk_t = arena("wk_t", 24, [NT, GH, P])
        kt_t = arena("kt_t", 32, [NT, GH, P])
        vb_t = arena("vb_t", 40, [NT, GH, P])
        g_row = arena("g_row", 48, [GH, S])
        b_row = arena("b_row", 56, [GH, S])
        t_inv = arena("t_inv", 56, [NT, GH, P])
        u_inv = arena("u_inv", 16, [NT, GH, P])
        o_t = arena("o_t", 56, [GH, S])
        qk_t = arena("qk_t", 64, [NT, GH, P])
        at_t = arena("at_t", 72, [NT, GH, P])
        wt_t = arena("wt_t", 72, [NT, GH, P])
        am = arena("am", 88, [4, GH, P])
        xs = arena("xs", 80, [4, GH, P])
        dec = arena("dec", 80, [2, GH, P])
        dmask = arena("dmask", 84, [2, GH, P])
        state = arena("state", 80, [2, GH, P])
        u_new = arena("u_new", 84, [2, GH, P])
        a_gate = arena("a_gate", 24, [S])
        b_gate = arena("b_gate", 26, [S])
        sp1 = arena("sp1", 28, [S])
        n_gate = arena("n_gate", 30, [S])
        sp2 = arena("sp2", 32, [S])
        g_sum = arena("g_sum", 34, [S])
        rowmask = arena("rowmask", 40, [S])
        masks = arena("masks", 98, [8, P], BF16)
        masks_in = arena("masks_in", 64, [8, P])
        lens = arena("lens", 72, [8, S])
        ya_hi = arena("ya_hi", 0, [4, S], F32R)
        ya_lo = arena("ya_lo", 8, [4, S], F32R)
        cols1 = small[:, 0:32].rearrange("p (t c) -> p t c", t=NT)
        e_col = small[:, 32:48].rearrange("p (t c) -> p t c", t=NT)
        bg_col = small[:, 48:64].rearrange("p (t c) -> p t c", t=NT)
        tail_col = small[:, 64:80].rearrange("p (t c) -> p t c", t=NT)
        gl_col = small[:, 80:96].rearrange("p (t c) -> p t c", t=NT)
        gate_col = small[:, 96:192].rearrange("p (t c) -> p t c", t=NT)
        root_col = small[:, 240:244]
        na_col = small[:, 192:193]

        nq = at("nq", 56 * KB, [4, S])
        nk = at("nk", 64 * KB, [2, S])
        nv = arena("nv", 28, [NT, 256])
        yb_hi = arena("yb_hi", 32, [4, S], F32R)
        yb_lo = arena("yb_lo", 40, [4, S], F32R)
        alibi = arena("alibi", 48, [NH, S])
        z_raw = [arena(f"z_raw{i}", 64 + 4.25 * i, [NG, 528]) for i in range(2)]
        zc = arena("zc", 40, [2, 16, NG, 32])
        zc_hi = arena("zc_hi", 32, [2, 16, NG, 32], F32R)
        zc_lo = arena("zc_lo", 40, [2, 16, NG, 32], F32R)
        pos = arena("pos", 81, [2, 16])
        hid_t = arena("hid_t", 85, [2, 256])
        w2 = arena("w2", 82, [2, 2, ND])
        hid = arena("hid", 83, [2, 2, NG, 32])
        kc = arena("kc", 84, [32])
        vc = arena("vc", 84.25, [NG, ND])
        n_s = arena("n_s", 64, [4, S])
        n_pt = arena("n_pt", 80, [2, S])
        c_s = arena("c_s", 74, [NH, NCMP])
        c_pt = arena("c_pt", 76, [NH, P])
        c_bias = arena("c_bias", 88, [NT, NH, NCMP])
        c_mask = arena("c_mask", 92, [NT, NCMP])
        st = arena("st", 93, [64])
        early = arena("early", 16, [EARLY, 2, S])
        mx_hi = arena("mx_hi", 48, [DC, S], F32R)
        mx_lo = arena("mx_lo", 64, [DC, S], F32R)

        a_hi = arena("a_hi", 0, [FC, S], F32R)
        a_lo = arena("a_lo", 44, [FC, S], F32R)
        p_raw = arena("p_raw", 0, [2, S])
        p_hi = arena("p_hi", 4, [2, S], F32R)
        p_lo = arena("p_lo", 8, [2, S], F32R)
        mo_a = arena("mo_a", 16, [DC, S])

        wq = arena("wq", 0, [8, S])
        wk = arena("wk", 16, [2, S])
        wv = arena("wv", 20, [NT, 256])
        wvb = arena("wvb", 24, [256])
        band = arena("band", 25, [256])
        yw_hi = arena("yw_hi", 26, [8, S], F32R)
        yw_lo = arena("yw_lo", 42, [8, S], F32R)
        w_s = arena("w_s", 58, [4, 2 * P])
        w_pt = arena("w_pt", 64, [2, S])
        st2 = arena("st2", 68, [96])
        ma = arena("ma", 0, [DC, S])
        sg = arena("sg", 70, [DC, S])
        mqk = arena("mqk", 16, [8, S])
        mv = arena("mv", 32, [NT, 1024])
        mvb = arena("mvb", 80, [1024])
        m_hi = arena("m_hi", 48, [MH, S], F32R)
        m_lo = arena("m_lo", 64, [MH, S], F32R)
        so = arena("so", 64, [MH, S])
        cb2 = arena("cb2", 84, [2, S])
        wsc = arena("wsc", 80, [2, 1280])
        emx = arena("emx", 90, [S])
        em_b = arena("em_b", 92, [S])
        hn = arena("hn", 94, [2, S])
        msq = arena("msq", 98, [S])
        mxr = emx[32:40, :]
        acol = small[:, 0:32].rearrange("p (t c) -> p t c", t=NT)
        incl2 = small[:, 96:224]
        r_raw = arena("r_raw", 88, [S])
        r_i = arena("r_i", 92, [S])
        r_f = arena("r_f", 94, [S])
        r_one = arena("r_one", 96, [S])
        r_a = arena("r_a", 98, [S])
        mg_hi = arena("mg_hi", 16, [DC, S], F32R)
        mg_lo = arena("mg_lo", 32, [DC, S], F32R)

        result = arena("result", 0, [DC, S])

        bank = [ctx.enter_context(nc.psum_tensor(f"dense{i}", [P, S], F32)) for i in range(4)]
        misc = [ctx.enter_context(nc.psum_tensor(f"misc{i}", [P, S], F32)) for i in range(4)]

        def heads(ps):
            return ps[:, :].rearrange("p (h c) -> p h c", h=GH)

        def V(name, i=0, n=1):
            return vec[:, VECS[name] + i:VECS[name] + i + n]

        w_loaded = [sem(f"w_loaded{i}") for i in range(RAWS)]
        w_part = sem("w_part")
        w_split = sem("w_split")
        w_split_v = sem("w_split_v")
        w_used = sem("w_used")
        dense_done = sem("dense_done")
        in_loaded = sem("in_loaded")
        x_loaded = [sem(f"x_loaded{i}") for i in range(4)]
        c_loaded = sem("c_loaded")
        out_stored = sem("out_stored")
        h_ready = sem("h_ready")
        ux_done = sem("ux_done")
        u_part = sem("u_part")
        u_ready = sem("u_ready")
        po_copy = sem("po_copy")
        ms_sq = sem("ms_sq")
        ms_acc = sem("ms_acc")
        ms_sum = sem("ms_sum")
        ms_root = sem("ms_root")
        ms_inv = sem("ms_inv")
        po_scaled = sem("po_scaled")
        ms_row = sem("ms_row")
        cv_lin = sem("cv_lin")
        cv_done = sem("cv_done")
        cv_silu = sem("cv_silu")
        rows1_done = sem("rows1_done")
        sp_done = sem("sp_done")
        sp_exp = sem("sp_exp")
        g_done = sem("g_done")
        tr1_done = sem("tr1_done")
        cols_done = sem("cols_done")
        bc_done = sem("bc_done")
        bc_copied = sem("bc_copied")
        ecol_in = sem("ecol_in")
        ecol_done = sem("ecol_done")
        head_sq = sem("head_sq")
        head_sum = sem("head_sum")
        head_rt = sem("head_rt")
        l2_done = sem("l2_done")
        kv_tr = sem("kv_tr")
        kv_done = sem("kv_done")
        dc_in = sem("dc_in")
        dc_exp = sem("dc_exp")
        kk_done = sem("kk_done")
        at_done = sem("at_done")
        eg_done = sem("eg_done")
        qd_done = sem("qd_done")
        at_beta = sem("at_beta")
        len_done = sem("len_done")
        am_done = sem("am_done")
        x_done = sem("x_done")
        xc_done = sem("xc_done")
        txu_done = sem("txu_done")
        t_upd = sem("t_upd")
        u_upd = sem("u_upd")
        u_tr = sem("u_tr")
        u_copied = sem("u_copied")
        wt_done = sem("wt_done")
        wt_copied = sem("wt_copied")
        un_done = sem("un_done")
        un_copied = sem("un_copied")
        og_done = sem("og_done")
        og_copied = sem("og_copied")
        ds_done = sem("ds_done")
        s_upd = sem("s_upd")
        z_silu = sem("z_silu")
        y_done = sem("y_done")
        ya_part = sem("ya_part")
        ya_ready = sem("ya_ready")
        nqk_done = sem("nqk_done")
        nv_done = sem("nv_done")
        zp_zero = sem("zp_zero")
        z_copied = sem("z_copied")
        zc_sum = sem("zc_sum")
        zc_part = sem("zc_part")
        zc_ready = sem("zc_ready")
        hid_act = sem("hid_act")
        hid_tr = sem("hid_tr")
        hid_done = sem("hid_done")
        kvc_done = sem("kvc_done")
        kvc_copied = sem("kvc_copied")
        cs_done = sem("cs_done")
        cs_shift = sem("cs_shift")
        cs_exp = sem("cs_exp")
        cp_ready = sem("cp_ready")
        mixa_sig = sem("mixa_sig")
        mix_a = sem("mix_a")
        mix_b = sem("mix_b")
        mx_part = sem("mx_part")
        mx_ready = sem("mx_ready")
        up_lin = sem("up_lin")
        up_conv = sem("up_conv")
        up_act = sem("up_act")
        a_raw = sem("a_raw")
        a_part = sem("a_part")
        a_ready = sem("a_ready")
        ps_part = sem("ps_part")
        ps_ready = sem("ps_ready")
        ple_sig = sem("ple_sig")
        wq_done = sem("wq_done")
        wk_done = sem("wk_done")
        wv_done = sem("wv_done")
        sg_done = sem("sg_done")
        ma_done = sem("ma_done")
        mqk_lin = sem("mqk_lin")
        mqk_b = sem("mqk_b")
        mqk_conv = sem("mqk_conv")
        mqk_silu = sem("mqk_silu")
        mv_done = sem("mv_done")
        so_done = sem("so_done")
        r2_act = sem("r2_act")
        r2_dve = sem("r2_dve")
        ac_tr = sem("ac_tr")
        ac_done = sem("ac_done")
        mb_done = sem("mb_done")
        mdg_in = sem("mdg_in")
        mw_exp = sem("mw_exp")
        msc_done = sem("msc_done")
        mws = sem("mws")
        mnd_done = sem("mnd_done")
        meb_copied = sem("meb_copied")
        mhn = sem("mhn")
        mh_y = sem("mh_y")
        mh_part = sem("mh_part")
        mh_ready = sem("mh_ready")
        mh_norm = sem("mh_norm")
        mg_in = sem("mg_in")
        mg_part = sem("mg_part")
        mg_ready = sem("mg_ready")
        f_out = sem("f_out")
        act_step = sem("act_step")
        dve_step = sem("dve_step")
        pool_step = sem("pool_step")

        steps = {"act": 0, "dve": 0}

        def act_link(eng, ins):
            steps["act"] += 1
            ins.then_inc(act_step, 1)
            eng.wait_ge(act_step, steps["act"])

        def dve_link(eng, ins):
            steps["dve"] += 1
            ins.then_inc(dve_step, 1)
            eng.wait_ge(dve_step, steps["dve"])

        class Att:
            def __init__(self, tag):
                self.s_done = sem(f"s_done_{tag}")
                self.m_done = sem(f"m_done_{tag}")
                self.e_done = sem(f"e_done_{tag}")
                self.p_done = sem(f"p_done_{tag}")
                self.t_done = sem(f"t_done_{tag}")
                self.t_copied = sem(f"t_copied_{tag}")
                self.pv_done = sem(f"pv_done_{tag}")
                self.o_part = sem(f"o_part_{tag}")
                self.o_ready = sem(f"o_ready_{tag}")

        att = [Att("n"), Att("w")]

        freed = [None] * GROUPS

        def frees(name, s, values):
            g = START[name][1]
            for i, v in enumerate(values):
                freed[g + i] = (s, v)

        frees("qkv", cv_done, [c + 1 for c in range(12)])
        frees("rows1", rows1_done, [3])
        for hd in range(GH):
            frees(f"z{hd}", z_silu, [hd + 1])
        frees("nq", nqk_done, [1, 2, 3, 4])
        frees("nk", nqk_done, [5, 6])
        frees("ncmp", z_copied, [2, 4, 6, 8])
        frees("nv", nv_done, [1, 2, 3, 4])
        frees("cmpk", hid_act, [1])
        frees("cmpv", hid_act, [2])
        for m in range(DC):
            late = m >= EARLY
            frees(f"gate_a{m}", mixa_sig, [2 * m + 1 + late])
            frees(f"a2d{m}", mix_a, [m + 1])
            frees(f"gate_b{m}", mixa_sig, [2 * m + 2 + late])
            frees(f"b2d{m}", mix_b, [m + 1])
            frees(f"ple_gate{m}", ple_sig, [m + 1])
            frees(f"ple{m}", po_copy, [16 + m + 1])
            frees(f"gate_w{m}", sg_done, [m + 1])
            frees(f"proj_w{m}", ma_done, [m + 1])
            frees(f"gate_m{m}", sg_done, [9 + m + 1])
            frees(f"proj_m{m}", mg_in, [m + 1])
        frees("w_o", po_copy, [m + 1 for m in range(8)])
        frees("down", po_copy, [8 + m + 1 for m in range(8)])
        frees("up", up_conv, [c + 1 for c in range(2 * FC)])
        for n, name in ((0, "up1"), (1, "up2")):
            for c in range(FC):
                frees_at = START[name][1] + 2 * c
                freed[frees_at] = (up_act, FC * (n + 1) + c + 1)
                freed[frees_at + 1] = (a_raw, FC * (n + 1) + c + 1)
        frees("down1", h_ready, [24 + m + 1 for m in range(8)])
        frees("wq", wq_done, [m + 1 for m in range(8)])
        frees("wk", wk_done, [1, 2])
        frees("wv", wv_done, [1, 2, 3, 4])
        frees("mqk", mqk_lin, [m + 1 for m in range(8)])
        frees("rows2", r2_act, [1])
        frees("mv0", mv_done, [1, 2, 3, 4])
        frees("mv1", mv_done, [5, 6, 7, 8])
        frees("mo", so_done, [m + 1 for m in range(8)])
        frees("out", h_ready, [32 + m + 1 for m in range(8)])
        frees("down2", h_ready, [40 + m + 1 for m in range(8)])

        ends = {}
        last_slab = []
        done = 0
        for name, chunks, k, width in dense_layers():
            for c in range(chunks):
                tile = START[name][0] + k * width - 1 if width else tile_at(name, k, c, k - 1)
                last_slab.append(tile // SLAB)
                done += 1
                ends[tile] = done
        slab_used = []
        inside = 0
        for s in range(NSLABS):
            last = s * SLAB + SLAB - 1
            if last in ends or last >= TILES:
                slab_used.append((dense_done, ends.get(last, GROUPS)))
            else:
                inside += 1
                slab_used.append((w_used, inside))

        NORMS = ["pre0", "post0", "pre1", "post1", "post2", "pre2", "pre3", "pre4", "pre5"]

        first = START["cmpk"][0] // SLAB
        DVE_SLABS = range(first + 2, last_slab[START["cmpv"][1]] + 1, 2)

        def split_of(s):
            before = sum(d < s for d in DVE_SLABS)
            return (w_split_v, before + 1) if s in DVE_SLABS else (w_split, s - before + 1)

        bank_of = [g % 4 for g in range(GROUPS)]
        for m in range(DC):
            bank_of[START[f"gate_w{m}"][1]] = 2 + m % 2
        early_gates = [f"gate_{x}{m}" for m in range(EARLY) for x in "ab"]
        for name in early_gates:
            bank_of[START[name][1]] = 7
        psum = bank + misc
        last_in, before_in_bank = [None] * 8, []
        for g in range(GROUPS):
            before_in_bank.append(last_in[bank_of[g]])
            last_in[bank_of[g]] = g

        def group_of(name, m=0):
            return START[name][1] + m + 1

        def out_bank(name, m=0):
            return psum[bank_of[START[name][1] + m]]

        block = ctx.enter_context(nc.Block())

        @block.sync
        def _(sp):
            for i in range(4):
                sp.dma_start(h[:, 2 * i:2 * i + 2, :], t["x"][:, 2 * i:2 * i + 2, :]).then_inc(x_loaded[i], 16)
            for s in range(NSLABS):
                if s >= RAWS:
                    sp.wait_ge(*split_of(s - RAWS))
                sp.dma_start(raw[:, s % RAWS, :, :], t["weights"][s]).then_inc(w_loaded[s % RAWS], 16)
            for c in range(DC):
                sp.wait_ge(f_out, c + 1)
                sp.dma_start(t["out"][:, c, :], result[:, c, :]).then_inc(out_stored, 16)
            sp.wait_ge(out_stored, 16 * DC)

        @block.gpsimd
        def _(pool):
            for s in range(NSLABS):
                if s == last_slab[START["nk"][1] + 1] + 1:
                    for tt in range(NT):
                        pool.wait_ge(at_done, 2 * tt + 1)
                        nc.gpsimd.tensor_tensor(at_t[:, tt, :, :], at_t[:, tt, :, :],
                                                b_row[:, :, tt * P:(tt + 1) * P], ALU.mult).then_inc(at_beta, 1)
                for name, layer in (("pre1", START["w_o"][1] + 7), ("pre2", START["ple_gate7"][1])):
                    if s == last_slab[layer] + LEAD + 1:
                        r = NORMS.index(name)
                        pool.wait_ge(ms_sum, r)
                        for c in range(1, DC):
                            pool.wait_ge(ms_sq, DC * r + c + 1)
                            if c > 1:
                                pool.wait_ge(ms_acc, 7 * r + c - 1)
                            nc.gpsimd.tensor_tensor(slot[2][:, :], (slot[2] if c > 1 else sq[0])[:, :],
                                                    sq[c % 3][:, :], ALU.add).then_inc(ms_acc, 1)
                if s == last_slab[START["down"][1] + 7] + LEAD + 1:
                    for c in range(DC):
                        pool.wait_ge(po_scaled, c + 1)
                        nc.gpsimd.tensor_tensor(h[:, c, :], h[:, c, :], slot[4 + c % 2][:, :],
                                                ALU.add).then_inc(h_ready, 1)
                if s == last_slab[START["mo"][1] + 7] + LEAD + 1:
                    for hd in range(MH):
                        x = hn[:, hd % 2, :]
                        pool.wait_ge(mh_norm, hd + 1)
                        nc.gpsimd.tensor_tensor(x, x, so[:, hd, :], ALU.mult).then_inc(mh_y, 1)
                        pool.wait_ge(mh_part, hd + 1)
                        nc.gpsimd.tensor_tensor(m_lo[:, hd, :], x, m_hi[:, hd, :].bitcast(F32),
                                                ALU.subtract).then_inc(mh_ready, 1)
                if s in DVE_SLABS:
                    continue
                pool.wait_ge(w_part, s + 1)
                nc.gpsimd.tensor_tensor(w_lo[:, s % SPLITS, :, :], raw[:, s % RAWS, :, :],
                                        w_hi[:, s % SPLITS, :, :].bitcast(F32),
                                        ALU.subtract).then_inc(w_split, 1)

        @block.tensor
        def _(pe):
            mm = nc.tensor.matmul
            tr = nc.tensor.transpose
            inner = [0]

            def weight(tile, n=1):
                s, j = divmod(tile, SLAB)
                if j == 0:
                    pe.wait_ge(*split_of(s))
                return (w_hi[:, s % SPLITS, j:j + n, :].rearrange("p a b -> p (a b)"),
                        w_lo[:, s % SPLITS, j:j + n, :].rearrange("p a b -> p (a b)"))

            def used(ins, tile):
                if tile % SLAB == SLAB - 1 and tile not in ends:
                    inner[0] += 1
                    assert slab_used[tile // SLAB] == (w_used, inner[0])
                    ins.then_inc(w_used, 1)

            def wait_bank(g):
                if before_in_bank[g] is not None:
                    pe.wait_ge(*freed[before_in_bank[g]])

            def dense_part(name, m, i, src_hi, src_lo):
                tile, g = START[name][0] + DC * m + i, START[name][1] + m
                if i == 0:
                    wait_bank(g)
                out = psum[bank_of[g]][:, :]
                hi, lo = weight(tile)
                mm(out, hi, src_hi[:, i, :], start=(i == 0), stop=False)
                mm(out, hi, src_lo[:, i, :], start=False, stop=False)
                last = mm(out, lo, src_hi[:, i, :], start=False, stop=(i == DC - 1))
                used(last, tile)
                if i == DC - 1:
                    last.then_inc(dense_done, 1)

            def dense(name, src_hi, src_lo, k_ready=None, after=None):
                tile, g0 = START[name]
                n, k = next((c, k) for nm, c, k, _ in dense_layers() if nm == name)
                ahead = 4 if name in ABREAST else 0
                if ahead:
                    for m in range(4):
                        wait_bank(g0 + m)
                    for i in range(k):
                        pe.wait_ge(k_ready[0], k_ready[1] + i + 1)
                        for m in range(4):
                            out = psum[bank_of[g0 + m]][:, :]
                            hi, lo = weight(tile)
                            mm(out, hi, src_hi[:, i, :], start=(i == 0), stop=False)
                            mm(out, hi, src_lo[:, i, :], start=False, stop=False)
                            last = mm(out, lo, src_hi[:, i, :], start=False, stop=(i == k - 1))
                            used(last, tile)
                            if i == k - 1:
                                last.then_inc(dense_done, 1)
                            tile += 1
                for m in range(ahead, n):
                    g = g0 + m
                    wait_bank(g)
                    out = psum[bank_of[g]][:, :]
                    for i in range(k):
                        hi, lo = weight(tile)
                        if k_ready and m == 0:
                            pe.wait_ge(k_ready[0], k_ready[1] + i + 1)
                        mm(out, hi, src_hi[:, i, :], start=(i == 0), stop=False)
                        mm(out, hi, src_lo[:, i, :], start=False, stop=False)
                        last = mm(out, lo, src_hi[:, i, :], start=False, stop=(i == k - 1))
                        used(last, tile)
                        tile += 1
                    last.then_inc(dense_done, 1)
                    if after:
                        after(m)

            def dense_tokens(name, width):
                tile, g0 = START[name]
                for j in range(NT):
                    wait_bank(g0 + j)
                for i in range(DC):
                    hi, lo = weight(tile, width)
                    for j in range(NT):
                        out = psum[bank_of[g0 + j]][:, 0:width * P]
                        a_h, a_l = u_hi[:, i, j * P:(j + 1) * P], u_lo[:, i, j * P:(j + 1) * P]
                        mm(out, a_h, hi, start=(i == 0), stop=False)
                        mm(out, a_h, lo, start=False, stop=False)
                        last = mm(out, a_l, hi, start=False, stop=(i == DC - 1))
                        if i == DC - 1:
                            last.then_inc(dense_done, 1)
                    tile += width
                    if i < DC - 1:
                        used(last, tile - 1)

            def norm_row(name):
                r = NORMS.index(name)
                pe.wait_ge(ms_acc, 7 * r + 7)
                for j in range(NT):
                    last = mm(misc[2][:, j:j + 1], slot[2][:, j * P:(j + 1) * P], ones[:, 0:1], start=True, stop=True)
                last.then_inc(ms_sum, 1)
                pe.wait_ge(ms_inv, r + 1)
                for j in range(NT):
                    last = mm(misc[2][:, j * P:(j + 1) * P], root_col[:, j:j + 1].broadcast_to([P, P]), ident[:, :],
                              start=True, stop=True)
                last.then_inc(ms_row, 1)

            def gdn():
                for m in range(2):
                    for i in range(DC):
                        dense_part("nq", m, i, u_hi, u_lo)
                pe.wait_ge(g_done, 1)
                pe.wait_ge(rows1_done, 3)
                pe.wait_ge(head_rt, 8)
                for j in range(NT):
                    tr(misc[0][:, 8 * j:8 * j + 4], g_sum[0:4, j * P:(j + 1) * P], ident[0:4, 0:4])
                    tr(misc[0][:, 8 * j + 4:8 * j + 8], b_gate[0:4, j * P:(j + 1) * P], ident[0:4, 0:4])
                for j in range(NT):
                    last = tr(misc[0][:, 64 + 24 * j:88 + 24 * j], n_gate[0:24, j * P:(j + 1) * P],
                              ident[0:24, 0:24])
                last.then_inc(tr1_done, 1)
                for i in range(8):
                    src = g_sum if i < 4 else b_gate
                    if i >= 2:
                        pe.wait_ge(bc_copied, i - 1)
                    mm(misc[1 + i % 2][:, :], ident[0:4, i % 4:i % 4 + 1].broadcast_to([4, P]), src[0:4, :],
                       start=True, stop=True).then_inc(bc_done, 1)
                    dense_part("nq", 2, i, u_hi, u_lo)
                for j in range(2 * NT):
                    tt = j // 2
                    if j == 0:
                        pe.wait_ge(l2_done, 8)
                        pe.wait_ge(cols_done, 2)
                    if j >= 2:
                        pe.wait_ge(kv_done, 3 * ((j - 2) // 2) + (3 if j % 2 else 2))
                    for hd in range(GH):
                        last = tr(misc[3 * (j % 2)][:, hd * P:(hd + 1) * P],
                                  qkv[:, (4 if j % 2 == 0 else 8) + hd, tt * P:(tt + 1) * P], ident[:, :])
                    last.then_inc(kv_tr, 1)
                    dense_part("nq", 3, j, u_hi, u_lo)
                pe.wait_ge(bc_copied, 8)
                for tt in range(NT):
                    if tt >= 1:
                        pe.wait_ge(at_done, 2 * tt)
                    for b, c0 in ((0, 4), (1, 0)):
                        for hd in range(GH):
                            ks = qkv[:, 4 + hd, tt * P:(tt + 1) * P]
                            last = mm(misc[1 + b][:, hd * P:(hd + 1) * P], ks,
                                      qkv[:, c0 + hd, tt * P:(tt + 1) * P], start=True, stop=True)
                        last.then_inc(kk_done, 1)
                    for i in range(4 * tt, 4 * tt + 4):
                        dense_part("nk", i // DC, i % DC, u_hi, u_lo)
                pe.wait_ge(nqk_done, 6)
                n_all = LEVELS * NT

                def x_of(n):
                    tt = n % NT
                    pe.wait_ge(am_done, n + 1)
                    if n >= NT + 2:
                        pe.wait_ge(xc_done, n - NT - 1)
                    elif n >= 2:
                        pe.wait_ge(t_upd, n - 1)
                    if n >= NT:
                        pe.wait_ge(t_upd, n - NT + 1)
                    for hd in range(GH):
                        last = mm(bank[n % 2][:, hd * P:(hd + 1) * P], am[:, n % 4, hd, :],
                                  t_inv[:, tt, hd, :] if n >= NT else ident[:, :], start=True, stop=True)
                    last.then_inc(x_done, 1)

                last_level = n_all - NT

                def t_of(n):
                    tt = n % NT
                    pe.wait_ge(xc_done, n - NT + 1)
                    if n < 2 * NT:
                        pe.wait_ge(u_upd, n - NT + 1)
                    else:
                        pe.wait_ge(u_copied, n - 2 * NT + 1)
                    if n >= NT + 2:
                        pe.wait_ge(t_upd, n - 1)
                    for hd in range(GH):
                        last = mm(bank[2 + n % 2][:, hd * P:(hd + 1) * P], u_inv[:, tt, hd, :],
                                  xs[:, n % 4, hd, :], start=True, stop=True)
                    last.then_inc(txu_done, 1)

                def u_of(n):
                    pe.wait_ge(t_upd, n + 1)
                    if n >= NT + 2:
                        pe.wait_ge(u_copied, n - NT - 1)
                    for hd in range(GH):
                        last = tr(misc[n % 2][:, hd * P:(hd + 1) * P], t_inv[:, n % NT, hd, :], ident[:, :])
                    last.then_inc(u_tr, 1)

                def last_u_of(n):
                    tt = n % NT
                    pe.wait_ge(xc_done, n - NT + 1)
                    pe.wait_ge(u_copied, min(n - NT - 1, last_level - NT))
                    if n >= last_level + 2:
                        pe.wait_ge(u_upd, NT + n - 1 - last_level)
                    for hd in range(GH):
                        last = mm(misc[n % 2][:, hd * P:(hd + 1) * P], xs[:, n % 4, hd, :],
                                  u_inv[:, tt, hd, :], start=True, stop=True)
                    last.then_inc(txu_done, 1)

                for n in range(NT + 2):
                    x_of(n)
                for n in range(NT, n_all):
                    if n + 2 < n_all:
                        x_of(n + 2)
                    if n < last_level:
                        t_of(n)
                    if NT <= n - 1 < last_level:
                        u_of(n - 1)
                    if n >= last_level:
                        last_u_of(n)
                for tt in range(NT):
                    pe.wait_ge(u_upd, NT + tt + 1)
                    if tt >= 2:
                        pe.wait_ge(wt_copied, tt - 1)
                    for hd in range(GH):
                        last = mm(bank[tt % 2][:, hd * P:(hd + 1) * P], wk_t[:, tt, hd, :],
                                  u_inv[:, tt, hd, :], start=True, stop=True)
                    last.then_inc(wt_done, 1)
                pe.wait_ge(qd_done, 4)
                for tt in range(NT):
                    if tt > 0:
                        pe.wait_ge(s_upd, tt)
                        pe.wait_ge(wt_copied, tt + 1)
                        pe.wait_ge(og_copied, tt)
                    for hd in range(GH):
                        o = bank[2][:, hd * P:(hd + 1) * P]
                        last = mm(o, u_inv[:, tt, hd, :], vb_t[:, tt, hd, :], start=True, stop=(tt == 0))
                        if tt > 0:
                            last = mm(o, wt_t[:, tt, hd, :], state[:, (tt - 1) % 2, hd, :], start=False, stop=True)
                    last.then_inc(un_done, 1)
                    pe.wait_ge(un_copied, tt + 1)
                    if tt < NT - 1:
                        for hd in range(GH):
                            last = mm(bank[3][:, hd * P:(hd + 1) * P], kt_t[:, tt, hd, :],
                                      u_new[:, tt % 2, hd, :], start=True, stop=True)
                        last.then_inc(ds_done, 1)
                    for hd in range(GH):
                        o = misc[2][:, hd * P:(hd + 1) * P]
                        if tt > 0:
                            mm(o, state[:, (tt - 1) % 2, hd, :], qkv[:, hd, tt * P:(tt + 1) * P],
                               start=True, stop=False)
                        last = mm(o, u_new[:, tt % 2, hd, :], qk_t[:, tt, hd, :], start=(tt == 0), stop=True)
                    last.then_inc(og_done, 1)
                for hd in range(GH):
                    pe.wait_ge(head_sq, 8 + hd + 1)
                    if hd >= 2:
                        pe.wait_ge(head_rt, 8 + hd - 1)
                    mm(misc[hd % 2][:, :], ones[:, :], slot[hd % 2][:, :], start=True, stop=True)\
                        .then_inc(head_sum, 1)
                    dense(f"z{hd}", u_hi, u_lo)

            def compress():
                for b, name in ((0, "cmpk"), (1, "cmpv")):
                    tile, g = START[name]
                    pe.wait_ge(zc_ready, b + 1)
                    wait_bank(g)
                    out = psum[bank_of[g]][0:64, 0:256]
                    for i in range(16):
                        hi, lo = weight(tile, 2)
                        zh = zc_hi[:, b, i, :, :].rearrange("p a b -> p (a b)")
                        zl = zc_lo[:, b, i, :, :].rearrange("p a b -> p (a b)")
                        mm(out, zh, hi, start=(i == 0), stop=False)
                        mm(out, zh, lo, start=False, stop=False)
                        last = mm(out, zl, hi, start=False, stop=(i == 15))
                        tile += 2
                        if i < 15:
                            used(last, tile - 1)
                    last.then_inc(dense_done, 1)
                for b in range(2):
                    pe.wait_ge(hid_act, b + 1)
                    for m in range(2):
                        last = tr(misc[b][:, m * 64:(m + 1) * 64], hid_t[0:64, b, m * P:(m + 1) * P],
                                  ident[0:64, 0:64])
                    last.then_inc(hid_tr, 1)
                pe.wait_ge(hid_done, 2)
                for gr in range(NG):
                    for m in range(2):
                        mm(misc[0][gr * ND:(gr + 1) * ND, 0:32], w2[:, 0, m, :], hid[:, 0, m, gr, :],
                           start=(m == 0), stop=(m == 1))
                for gr in range(NG):
                    for m in range(2):
                        last = mm(misc[1][0:32, gr * ND:(gr + 1) * ND], hid[:, 1, m, gr, :], w2[:, 1, m, :],
                                  start=(m == 0), stop=(m == 1))
                last.then_inc(kvc_done, 1)

            def nsa():
                a = att[0]
                items = [(qt, hd, b) for qt in range(NT) for hd in range(NH) for b in range(2)]

                def cmp_scores(qt):
                    if qt >= 1:
                        pe.wait_ge(cs_shift, qt)
                    for hd in range(NH):
                        gr, c = divmod(hd, 4)
                        last = mm(bank[2 + gr][:, c * NCMP:(c + 1) * NCMP],
                                  nq[gr * ND:(gr + 1) * ND, c, qt * P:(qt + 1) * P],
                                  kc[gr * ND:(gr + 1) * ND, 0:NCMP], start=True, stop=True)
                    last.then_inc(cs_done, 1)

                def scores(j):
                    qt, hd, b = items[j]
                    gr, c = divmod(hd, 4)
                    if j >= 2:
                        pe.wait_ge(a.m_done, j - 1)
                    mm(bank[j % 2][:, 0:(qt + 1) * P], nq[gr * ND:(gr + 1) * ND, c, qt * P:(qt + 1) * P],
                       nk[gr * ND:(gr + 1) * ND, b, 0:(qt + 1) * P], start=True, stop=True).then_inc(a.s_done, 1)

                def turn(j):
                    qt = items[j][0]
                    u = 18 * qt + 2 + j % 16
                    pe.wait_ge(a.p_done, j + 1)
                    pe.wait_ge(a.t_copied, u - 1)
                    for kt in range(qt + 1):
                        last = tr(misc[u % 2][:, kt * P:(kt + 1) * P], n_s[:, j % 4, kt * P:(kt + 1) * P], ident[:, :])
                    last.then_inc(a.t_done, 1)

                def cmp_turn(qt):
                    pe.wait_ge(cp_ready, qt + 1)
                    for b in range(2):
                        u = 18 * qt + b
                        if u >= 2:
                            pe.wait_ge(a.t_copied, u - 1)
                        for hd in range(4):
                            last = tr(misc[u % 2][0:NCMP, hd * P:(hd + 1) * P], c_s[:, 4 * b + hd, :], ident[:, :])
                        last.then_inc(a.t_done, 1)

                def values(j):
                    qt, hd, b = items[j]
                    gr, c = divmod(hd, 4)
                    o = misc[2][gr * ND:(gr + 1) * ND, c * P:(c + 1) * P]
                    pe.wait_ge(a.t_copied, 18 * qt + 2 + j % 16 + 1)
                    if j % 16 == 0 and qt >= 1:
                        pe.wait_ge(a.o_ready, qt)
                    if b == 0:
                        mm(o, vc[0:NCMP, gr, :], c_pt[0:NCMP, hd, :], start=True, stop=False)
                    for kt in range(qt + 1):
                        last = mm(o, nv[:, kt, b * P + gr * ND:b * P + (gr + 1) * ND], n_pt[:, j % 2, kt * P:(kt + 1) * P],
                                  start=False, stop=(b == 1 and kt == qt))
                    last.then_inc(a.pv_done, 1)

                pe.wait_ge(kvc_copied, 2)
                pe.wait_ge(nv_done, 4)
                cmp_scores(0)
                for j in range(3):
                    scores(j)
                for j in range(len(items)):
                    if j + 3 < len(items):
                        scores(j + 3)
                    if j % 16 == 0:
                        if j >= 1:
                            values(j - 1)
                        cmp_turn(j // 16)
                    if j % 16 == 8 and j // 16 + 1 < NT:
                        cmp_scores(j // 16 + 1)
                    turn(j)
                    if j // 10 < 2 * EARLY and j % 10 < DC:
                        dense_part(early_gates[j // 10], 0, j % 10, u_hi, u_lo)
                    if j % 16:
                        values(j - 1)
                values(len(items) - 1)

            def window():
                a = att[1]
                items = [(qt, kv, r) for qt in range(NT) for kv in range(WKV) for r in range(4)]

                def scores(j):
                    qt, kv, r = items[j]
                    half, c = kv % 2, kv // 2
                    lo = max(qt - 1, 0) * P
                    if j >= 2:
                        pe.wait_ge(a.m_done, j - 1)
                    mm(bank[j % 2][:, 0:(qt + 1) * P - lo],
                       wq[half * ND:(half + 1) * ND, 4 * c + r, qt * P:(qt + 1) * P],
                       wk[half * ND:(half + 1) * ND, c, lo:(qt + 1) * P], start=True, stop=True).then_inc(a.s_done, 1)

                def turn(j):
                    qt = items[j][0]
                    pe.wait_ge(a.p_done, j + 1)
                    if j >= 2:
                        pe.wait_ge(a.t_copied, j - 1)
                    for kt in range(min(qt + 1, 2)):
                        last = tr(misc[j % 2][:, kt * P:(kt + 1) * P], w_s[:, j % 4, kt * P:(kt + 1) * P], ident[:, :])
                    last.then_inc(a.t_done, 1)

                def values(j):
                    qt, kv, r = items[j]
                    half, c = kv % 2, kv // 2
                    n = min(qt + 1, 2)
                    o = misc[2 + c][half * ND:(half + 1) * ND, r * P:(r + 1) * P]
                    pe.wait_ge(a.t_copied, j + 1)
                    if j % 8 == 0 and j >= 16:
                        pe.wait_ge(a.o_ready, j // 8 - 1)
                    for i in range(n):
                        kt = qt - n + 1 + i
                        last = mm(o, wv[:, kt, kv * ND:(kv + 1) * ND], w_pt[:, j % 2, i * P:(i + 1) * P],
                                  start=(i == 0), stop=(i == n - 1))
                    last.then_inc(a.pv_done, 1)

                pe.wait_ge(wq_done, 8)
                pe.wait_ge(wk_done, 2)
                pe.wait_ge(wv_done, 4)
                for j in range(3):
                    scores(j)
                for j in range(len(items)):
                    if j + 3 < len(items):
                        scores(j + 3)
                    turn(j)
                    dense_part(f"gate_w{j // DC}", 0, j % DC, u_hi, u_lo)
                    if j >= 1:
                        values(j - 1)
                values(len(items) - 1)
                pe.wait_ge(a.m_done, 64)

            off = [(0, 512, 2, 0), (2, 896, 2, 384), (1, 1024, 3, 0)]

            def mlstm():
                pe.wait_ge(r2_dve, 3)
                for j in range(NT):
                    last = tr(misc[0][:, 8 * j:8 * j + 8], r_a[0:8, j * P:(j + 1) * P], ident[0:8, 0:8])
                last.then_inc(ac_tr, 1)
                pe.wait_ge(mqk_silu, 8)
                pe.wait_ge(mv_done, 8)
                pe.wait_ge(so_done, 8)
                pe.wait_ge(ac_done, 1)
                pe.wait_ge(r2_act, 7)

                def front(hd):
                    c, half = divmod(hd, 2)
                    sel = ident[32:40, 32 + hd:33 + hd].broadcast_to([8, P])
                    if hd >= 1:
                        pe.wait_ge(mw_exp, hd)
                        pe.wait_ge(mws, 3 * hd)
                    mm(bank[0][:, :], sel, mxr, start=True, stop=True).then_inc(mb_done, 1)
                    q = lambda a, b: mqk[half * ND:(half + 1) * ND, c, a * P:b * P]
                    k = lambda a: mqk[half * ND:(half + 1) * ND, 4 + c, a * P:(a + 1) * P]
                    for j in range(NT):
                        last = mm(bank[1][:, j * P:(j + 1) * P], k(j), q(j, j + 1), start=True, stop=True)
                    for j, _, b, at_col in off:
                        last = mm(bank[b][:, at_col:at_col + (3 - j) * P], k(j), q(j + 1, NT), start=True, stop=True)
                    last.then_inc(msc_done, 1)

                def back(hd):
                    if hd >= 1:
                        pe.wait_ge(meb_copied, hd)
                        pe.wait_ge(mhn, 2 * hd)
                    mm(misc[2][:, :], ident[0:8, hd:hd + 1].broadcast_to([8, P]), emx[0:8, :],
                       start=True, stop=True).then_inc(mnd_done, 1)
                    pe.wait_ge(mws, 3 * hd + 3)
                    x = wsc[:, hd % 2, :]
                    for dst, den in ((1, True), (0, False)):
                        w = lambda j: ones[:, :] if den else mv[:, j, hd * P:(hd + 1) * P]
                        for j in range(NT):
                            mm(misc[dst][:, j * P:(j + 1) * P], w(j), x[:, j * P:(j + 1) * P],
                               start=(j == 0), stop=False)
                        for n, (j, at_col, _, _) in enumerate(off):
                            last = mm(misc[dst][:, (j + 1) * P:S], w(j), x[:, at_col:at_col + (3 - j) * P],
                                      start=False, stop=(n == 2))
                        last.then_inc(mnd_done, 1)

                def mean_square(hd):
                    pe.wait_ge(head_sq, 12 + hd + 1)
                    if hd >= 1:
                        pe.wait_ge(head_rt, 12 + hd)
                    mm(misc[3][:, :], ones[:, :], msq[:, :], start=True, stop=True).then_inc(head_sum, 1)

                front(0)
                for hd in range(MH + 1):
                    if hd + 1 < MH:
                        front(hd + 1)
                    if hd >= 1:
                        mean_square(hd - 1)
                    if hd < MH:
                        back(hd)

            def ffn(name_up, name_down, n):
                dense(name_up, u_hi, u_lo, (u_ready, DC * (n + 1)))
                dense(name_down, a_hi, a_lo, (a_ready, FC * n))

            pe.wait_ge(in_loaded, 48)
            norm_row("pre0")

            def length_sum(m):
                for c in range(0 if m == 4 else m - 2, min(m - 1, 8)):
                    pe.wait_ge(head_sq, c + 1)
                    if c >= 2:
                        pe.wait_ge(head_rt, c - 1)
                    mm(misc[c % 2][:, :], ones[:, :], slot[2 + c % 2][:, :], start=True,
                       stop=True).then_inc(head_sum, 1)

            dense("qkv", u_hi, u_lo, (u_ready, 0), length_sum)
            dense("rows1", u_hi, u_lo)
            for g in range(START["qkv"][1] + 9, START["rows1"][1] + 1):
                pe.wait_ge(*freed[g])
            gdn()
            dense("ncmp", u_hi, u_lo)
            dense_tokens("nv", 2)
            pe.wait_ge(ya_ready, 4)
            compress()
            nsa()
            pe.wait_ge(att[0].m_done, 64)
            for m in range(DC):
                if m >= EARLY:
                    dense(f"gate_a{m}", u_hi, u_lo)
                dense(f"a2d{m}", ya_hi, ya_lo)
                if m >= EARLY:
                    dense(f"gate_b{m}", u_hi, u_lo)
                if m == 0:
                    pe.wait_ge(att[0].o_ready, 4)
                dense(f"b2d{m}", yb_hi, yb_lo)
            dense("w_o", mx_hi, mx_lo, (mx_ready, 0))
            norm_row("post0")
            norm_row("pre1")
            ffn("up", "down", 0)
            norm_row("post1")
            pe.wait_ge(ps_ready, 2)
            for m in range(DC):
                dense(f"ple{m}", p_hi, p_lo)
                dense(f"ple_gate{m}", u_hi, u_lo, (u_ready, 2 * DC) if m == 0 else None)
            norm_row("post2")
            norm_row("pre2")
            dense("up1", u_hi, u_lo, (u_ready, 3 * DC))
            dense("down1", a_hi, a_lo, (a_ready, FC))
            norm_row("pre3")
            dense("wq", u_hi, u_lo, (u_ready, 4 * DC))
            dense("wk", u_hi, u_lo)
            dense_tokens("wv", 2)
            window()
            pe.wait_ge(att[1].o_ready, 8)
            for m in range(DC):
                dense(f"proj_w{m}", yw_hi, yw_lo)
            dense("mqk", u_hi, u_lo)
            dense("rows2", u_hi, u_lo)
            dense_tokens("mv0", 4)
            dense_tokens("mv1", 4)
            dense("mo", u_hi, u_lo)
            mlstm()
            for m in range(DC):
                dense(f"gate_m{m}", u_hi, u_lo)
                if m == 0:
                    pe.wait_ge(mh_ready, 8)
                dense(f"proj_m{m}", m_hi, m_lo)
            dense("out", mg_hi, mg_lo, (mg_ready, 0))
            norm_row("pre4")
            dense("up2", u_hi, u_lo, (u_ready, 5 * DC))
            dense("down2", a_hi, a_lo, (a_ready, 2 * FC))
            norm_row("pre5")

        @block.scalar
        def _(act):
            f = nc.scalar.activation
            rounded = [0]

            def feed_to(upto):
                while rounded[0] < upto:
                    s = rounded[0]
                    act.wait_ge(w_loaded[s % RAWS], 16 * (s // RAWS + 1))
                    if s >= SPLITS:
                        act.wait_ge(*slab_used[s - SPLITS])
                    f(w_hi[:, s % SPLITS, :, :], raw[:, s % RAWS, :, :], ACT.Copy).then_inc(w_part, 1)
                    rounded[0] += 1

            def feed(name, m=0):
                feed_to(min(last_slab[START[name][1] + m] + LEAD + 1, NSLABS))

            def after_group(name, m=0):
                feed(name, m)
                act.wait_ge(dense_done, group_of(name, m))

            def norm_act(n, ready, layer=None):
                f(spare_col, one_col, ACT.Sqrt)
                for c in range(DC):
                    if layer:
                        feed(layer, c)
                    if n == 0:
                        act.wait_ge(x_loaded[c // 2], 16)
                    else:
                        act.wait_ge(h_ready, ready + c + 1)
                    square(f"pre{n}", c, h)
                if n == 0:
                    feed_to(1)
                root(f"pre{n}")

            def split_hi(k0, name):
                feed_to((START[name][0] + 4 * DC - 1) // SLAB + 1)
                for c in range(DC):
                    act.wait_ge(ux_done, k0 + c + 1)
                    f(u_hi[:, c, :], slot[4 + c % 2][:, :], ACT.Copy).then_inc(u_part, 1)

            def post_act(n, name, mo):
                f(spare_col, one_col, ACT.Sqrt)
                for c in range(DC):
                    if name:
                        after_group(name, c)
                        f(mo[:, c, :], out_bank(name, c)[:, :], ACT.Copy).then_inc(po_copy, 1)
                        act.wait_ge(po_copy, DC * n + c + 1)
                    square(f"post{n}", c, mo)
                root(f"post{n}")

            def square(name, c, x):
                r = NORMS.index(name)
                if c >= 3 or r >= 1:
                    added = 0 if c < 3 else max(c - 3, 1)
                    act.wait_ge(ms_acc, 7 * r + added)
                f(sq[c % 3][:, :], x[:, c, :], ACT.Square).then_inc(ms_sq, 1)

            def root(name):
                act.wait_ge(ms_sum, NORMS.index(name) + 1)
                f(root_col, misc[2][:, 0:NT], ACT.Sqrt, bias=eps_col, scale=1.0 / D).then_inc(ms_root, 1)

            def attention(a, items, s_buf, pt_buf, st_buf, before, outs):
                for j in range(len(items) + 1):
                    if j < len(items):
                        nk_, sink, _ = items[j]
                        before(j)
                        act.wait_ge(a.m_done, j + 1)
                        if j >= 8:
                            act.wait_ge(a.p_done, j - 7)
                        if sink is None:
                            f(s_buf[:, j % 4, 0:nk_], s_buf[:, j % 4, 0:nk_], ACT.Exp, bias=st_buf[:, j % 8:j % 8 + 1],
                              scale=-1.0, accum_out=st_buf[:, 8 + j % 8:9 + j % 8]).then_inc(a.e_done, 1)
                        else:
                            f(st_buf[:, 24 + j % 8:25 + j % 8], sink, ACT.Exp, bias=st_buf[:, j % 8:j % 8 + 1])
                            f(s_buf[:, j % 4, 0:nk_], s_buf[:, j % 4, 0:nk_], ACT.Exp, bias=st_buf[:, j % 8:j % 8 + 1],
                              scale=-1.0, accum_out=st_buf[:, 8 + j % 8:9 + j % 8]).then_inc(a.e_done, 1)
                    if j >= 1:
                        i = j - 1
                        nk_, _, u = items[i]
                        act.wait_ge(a.t_done, u + 1)
                        if i >= 2:
                            act.wait_ge(a.pv_done, i - 1)
                        f(pt_buf[:, i % 2, 0:nk_], misc[u % 2][:, 0:nk_], ACT.Copy).then_inc(a.t_copied, 1)
                        outs(i - 1)
                outs(len(items) - 1)

            def ffn_swiglu(n, name):
                for c in range(FC + 1):
                    if c < FC:
                        k = FC * n + c
                        after_group(name, 2 * c)
                        if c >= 2:
                            act.wait_ge(a_ready, k - 1)
                        f(slot[c % 2][:, :], out_bank(name, 2 * c)[:, :], ACT.Silu).then_inc(up_act, 1)
                    if c >= 1:
                        act.wait_ge(a_raw, FC * n + c)
                        f(a_hi[:, c - 1, :], slot[(c - 1) % 2][:, :], ACT.Copy).then_inc(a_part, 1)

            eps_col = small[:, 250:251]
            one_col = small[:, 251:252]
            spare_col = small[:, 253:254]
            act.dma_start(vec[:, 0:NVEC], t["vec"]).then_inc(in_loaded, 16)
            act.dma_start(ident[:, :], t["ident"]).then_inc(in_loaded, 16)
            act.dma_start(ones[:, :], t["ones"]).then_inc(in_loaded, 16)
            act.dma_start(masks_in[:, :, :], t["masks"]).then_inc(c_loaded, 16)
            act.dma_start(rowmask[:, :], t["rowmask"]).then_inc(c_loaded, 16)
            act.wait_ge(pool_step, 2)
            norm_act(0, 0)
            split_hi(0, "qkv")

            for c in range(13):
                if c < 12:
                    after_group("qkv", c)
                    if c >= 2:
                        act.wait_ge(cv_silu, c - 1)
                    f(slot[c % 2][:, :], out_bank("qkv", c)[:, :], ACT.Copy,
                      scale=V("conv_qkv", 4 * c + 3)).then_inc(cv_lin, 1)
                if c >= 1:
                    act.wait_ge(cv_done, c)
                    f(qkv[:, c - 1, :], slot[(c - 1) % 2][:, :], ACT.Silu).then_inc(cv_silu, 1)
                i = c - 1
                if 0 <= i < 8:
                    act.wait_ge(cv_silu, i + 1)
                    if i == 0:
                        act.wait_ge(u_ready, 8)
                    if i >= 2:
                        act.wait_ge(head_sum, i - 1)
                    f(slot[2 + i % 2][:, :], qkv[:, i, :], ACT.Square).then_inc(head_sq, 1)
                i = c - 3
                if 0 <= i < 8:
                    act.wait_ge(head_sum, i + 1)
                    f(lens[:, i, :], misc[i % 2][:, :], ACT.Copy).then_inc(head_rt, 1)
            after_group("rows1")
            rows = out_bank("rows1")
            f(b_gate[0:4, :], rows[0:4, :], ACT.Sigmoid).then_inc(rows1_done, 1)
            f(n_gate[0:24, :], rows[64:88, :], ACT.Sigmoid).then_inc(rows1_done, 1)
            f(a_gate[0:4, :], rows[32:36, :], ACT.Copy).then_inc(rows1_done, 1)
            act.wait_ge(sp_done, 1)
            act_link(act, f(sp2[0:4, :], sp1[0:4, :], ACT.Exp))
            f(na_col[0:4, :], V("a_log")[0:4, :], ACT.Exp)
            f(sp2[0:4, :], sp2[0:4, :], ACT.Ln, bias=one_col[0:4, :]).then_inc(sp_exp, 1)
            act.wait_ge(head_rt, 8)
            act_link(act, f(lens[:, :, :], lens[:, :, :], ACT.Ln, bias=eps_col))
            f(lens[:, :, :], lens[:, :, :], ACT.Exp, scale=-0.5).then_inc(len_done, 1)

            def project(name, dst, c, scale):
                after_group(name, c)
                f(dst[:, c, :], out_bank(name, c)[:, :], ACT.Copy, scale=scale).then_inc(nqk_done, 1)

            project("nq", nq, 0, ND ** -0.5)
            project("nq", nq, 1, ND ** -0.5)
            for i in range(8):
                act.wait_ge(bc_done, i + 1)
                dst = g_row if i < 4 else b_row
                f(dst[:, i % 4, :], misc[1 + i % 2][:, :], ACT.Copy).then_inc(bc_copied, 1)
            act.wait_ge(ecol_in, 1)
            f(e_col, cols1[:, :, 0:4], ACT.Exp).then_inc(ecol_done, 1)
            f(tail_col, tail_col, ACT.Exp).then_inc(ecol_done, 1)
            act.wait_ge(bc_copied, 8)
            f(gl_col, g_row[:, :, P - 1::P].rearrange("p h t -> p t h"), ACT.Exp).then_inc(ecol_done, 1)
            project("nq", nq, 2, ND ** -0.5)
            project("nq", nq, 3, ND ** -0.5)
            for tt in range(NT):
                act.wait_ge(dc_in, tt + 1)
                f(dec[:, tt % 2, :, :], dec[:, tt % 2, :, :], ACT.Exp).then_inc(dc_exp, 1)
            project("nk", nk, 0, 1.0)
            project("nk", nk, 1, 1.0)
            act.wait_ge(kv_done, 12)
            for hd in range(GH):
                f(g_row[:, hd, :], g_row[:, hd, :], ACT.Exp).then_inc(eg_done, 1)
            act.wait_ge(at_done, 2 * NT)
            for n in range(NT, LEVELS * NT):
                act.wait_ge(x_done, n + 1)
                if n >= NT + 4:
                    act.wait_ge(t_upd, n - 3)
                f(xs[:, n % 4, :, :], heads(bank[n % 2]), ACT.Copy).then_inc(xc_done, 1)
                i = n - 2
                if NT <= i < (LEVELS - 1) * NT:
                    act.wait_ge(u_tr, i - NT + 1)
                    f(u_inv[:, i % NT, :, :], heads(misc[i % 2]), ACT.Copy).then_inc(u_copied, 1)
            for tt in range(NT):
                act.wait_ge(wt_done, tt + 1)
                f(wt_t[:, tt, :, :], heads(bank[tt % 2]), ACT.Copy, scale=-1.0).then_inc(wt_copied, 1)
            for tt in range(NT):
                act.wait_ge(un_done, tt + 1)
                f(u_new[:, tt % 2, :, :], heads(bank[2]), ACT.Copy).then_inc(un_copied, 1)
                act.wait_ge(og_done, tt + 1)
                f(o_t[:, :, tt * P:(tt + 1) * P], heads(misc[2]), ACT.Copy).then_inc(og_copied, 1)
            act.wait_ge(og_copied, NT)
            for hd in range(GH + 2):
                if hd < GH:
                    if hd >= 2:
                        act.wait_ge(head_sum, 8 + hd - 1)
                    f(slot[hd % 2][:, :], o_t[:, hd, :], ACT.Square).then_inc(head_sq, 1)
                i = hd - 1
                if 0 <= i < GH:
                    act.wait_ge(head_sum, 8 + i + 1)
                    if i >= 2:
                        act.wait_ge(y_done, i - 1)
                    f(slot[2 + i % 2][:, :], misc[i % 2][:, :], ACT.Sqrt, bias=eps_col, scale=1.0 / P).then_inc(head_rt, 1)
                    after_group(f"z{i}")
                    f(xs[:, i % 2, :, :].rearrange("p a b -> p (a b)"), out_bank(f"z{i}")[:, :],
                      ACT.Silu).then_inc(z_silu, 1)
                if i >= 1:
                    act.wait_ge(y_done, i)
                    f(ya_hi[:, i - 1, :], o_t[:, i - 1, :], ACT.Copy).then_inc(ya_part, 1)

            act.wait_ge(ya_ready, 4)
            act.dma_start(alibi[:, :, :], t["alibi"]).then_inc(c_loaded, 16)
            act.dma_start(pos[:, :, :], t["pos"]).then_inc(c_loaded, 16)
            act.dma_start(w2[:, :, :, :], t["w2"]).then_inc(c_loaded, 16)
            act.dma_start(c_bias[:, :, :, :], t["c_bias"]).then_inc(c_loaded, 16)
            act.dma_start(c_mask[:, :, :], t["c_mask"]).then_inc(c_loaded, 16)
            act.wait_ge(zp_zero, 2)
            for c in range(4):
                b, gr = divmod(c, 2)
                after_group("ncmp", c)
                ps = out_bank("ncmp", c)
                f(z_raw[b][0:ND, gr, 0:S], ps[0:ND, :], ACT.Copy).then_inc(z_copied, 1)
                f(z_raw[b][ND:P, gr, 0:S - 1], ps[ND:P, 1:S], ACT.Copy).then_inc(z_copied, 1)
            for j in range(NT):
                after_group("nv", j)
                f(nv[:, j, :], out_bank("nv", j)[:, 0:256], ACT.Copy).then_inc(nv_done, 1)
            for b in range(2):
                act.wait_ge(zc_sum, 2 * b + 2)
                f(zc_hi[:, b, :, :, :], zc[:, b, :, :, :], ACT.Copy).then_inc(zc_part, 1)
            for b in range(2):
                after_group(("cmpk", "cmpv")[b])
                f(hid_t[0:64, b, :], out_bank(("cmpk", "cmpv")[b])[0:64, 0:256],
                  ACT.Gelu_apprx_tanh).then_inc(hid_act, 1)
            for b in range(2):
                act.wait_ge(hid_tr, b + 1)
                f(hid[:, b, :, :, :].rearrange("p a b c -> p (a b c)"), misc[b][:, 0:P],
                  ACT.Copy).then_inc(hid_done, 1)
            act.wait_ge(kvc_done, 1)
            f(kc[:, :], misc[0][:, 0:32], ACT.Copy).then_inc(kvc_copied, 1)
            f(vc[0:32, :, :].rearrange("p a b -> p (a b)"), misc[1][0:32, 0:P], ACT.Copy).then_inc(kvc_copied, 1)

            a0 = att[0]

            def nsa_before(j):
                if j % 16 == 0:
                    qt = j // 16
                    act.wait_ge(cs_shift, qt + 1)
                    f(c_s[:, :, :], c_s[:, :, :], ACT.Exp).then_inc(cs_exp, 1)

            def nsa_outs(i):
                if i >= 0 and i % 16 == 15:
                    qt = i // 16
                    act.wait_ge(a0.pv_done, i + 1)
                    f(yb_hi[:, :, qt * P:(qt + 1) * P], heads(misc[2]), ACT.Copy).then_inc(a0.o_part, 1)

            def cmp_copy(qt):
                for b in range(2):
                    u = 18 * qt + b
                    act.wait_ge(a0.t_done, u + 1)
                    if qt >= 1:
                        act.wait_ge(a0.pv_done, 16 * qt)
                    f(c_pt[0:NCMP, 4 * b:4 * b + 4, :].rearrange("p a b -> p (a b)"), misc[u % 2][0:NCMP, :],
                      ACT.Copy).then_inc(a0.t_copied, 1)

            items = []
            for qt in range(NT):
                for n in range(16):
                    items.append(((qt + 1) * P, None, 18 * qt + 2 + n))
            for j in range(65):
                if j < 64:
                    nsa_before(j)
                    act.wait_ge(a0.m_done, j + 1)
                    f(n_s[:, j % 4, 0:items[j][0]], n_s[:, j % 4, 0:items[j][0]], ACT.Exp,
                      bias=st[:, j % 8:j % 8 + 1], scale=-1.0,
                      accum_out=st[:, 8 + j % 8:9 + j % 8]).then_inc(a0.e_done, 1)
                if j >= 1:
                    i = j - 1
                    nk_, _, u = items[i]
                    if i % 16 == 0:
                        if i >= 1:
                            nsa_outs(i - 1)
                        cmp_copy(i // 16)
                    act.wait_ge(a0.t_done, u + 1)
                    if i >= 2:
                        act.wait_ge(a0.pv_done, i - 1)
                    f(n_pt[:, i % 2, 0:nk_], misc[u % 2][:, 0:nk_], ACT.Copy).then_inc(a0.t_copied, 1)
                    if i // 10 < 2 * EARLY and i % 10 == DC:
                        m, b = divmod(i // 10, 2)
                        after_group(early_gates[i // 10])
                        f(early[:, m, b, :], out_bank(early_gates[i // 10])[:, :], ACT.Copy).then_inc(mixa_sig, 1)
            nsa_outs(63)

            act.dma_start(h[:, 0:4, :], t["x"][:, 0:4, :]).then_inc(x_loaded[0], 16)
            act.dma_start(h[:, 4:8, :], t["x"][:, 4:8, :]).then_inc(x_loaded[1], 16)
            for m in range(DC):
                if m < EARLY:
                    if m == 0:
                        act.wait_ge(mixa_sig, 2 * EARLY)
                        f(early[:, :, :, :], early[:, :, :, :], ACT.Sigmoid).then_inc(mixa_sig, 1)
                    feed(f"a2d{m}")
                    feed(f"b2d{m}")
                else:
                    for b, nm in ((0, "gate_a"), (1, "gate_b")):
                        after_group(f"{nm}{m}")
                        act.wait_ge((mix_a, mix_b)[b], m)
                        f(slot[b][:, :], out_bank(f"{nm}{m}")[:, :], ACT.Sigmoid).then_inc(mixa_sig, 1)
                act.wait_ge(mix_b, m + 1)
                f(mx_hi[:, m, :], slot[4 + m % 2][:, :], ACT.Copy).then_inc(mx_part, 1)
            act.wait_ge(mx_ready, 8)
            post_act(0, "w_o", mo_u)
            norm_act(1, 0)
            split_hi(8, "up")

            act.wait_ge(u_ready, 16)
            for c in range(FC + 1):
                if c < FC:
                    for b in range(2):
                        g = b * FC + c
                        after_group("up", 2 * c + b)
                        if c >= 2:
                            act.wait_ge(a_ready, c - 1)
                        f(slot[2 * b + c % 2][:, :], out_bank("up", 2 * c + b)[:, :], ACT.Identity,
                          bias=V("conv_ffn_b", g), scale=V("conv_ffn", 3 * g + 2)).then_inc(up_lin, 1)
                    act.wait_ge(up_conv, 2 * c + 1)
                    f(slot[c % 2][:, :], slot[c % 2][:, :], ACT.Gelu_apprx_tanh).then_inc(up_act, 1)
                if c >= 1:
                    act.wait_ge(a_raw, c)
                    f(a_hi[:, c - 1, :], slot[2 + (c - 1) % 2][:, :], ACT.Copy).then_inc(a_part, 1)
            act.wait_ge(a_ready, FC)
            post_act(1, "down", mo_u)
            act.dma_start(p_raw[:, :, :], t["p"]).then_inc(c_loaded, 16)
            act.wait_ge(c_loaded, 128)
            for c in range(2):
                f(p_hi[:, c, :], p_raw[:, c, :], ACT.Copy).then_inc(ps_part, 1)
            for c in range(DC):
                act.wait_ge(h_ready, 8 + c + 1)
                f(u_hi[:, c, :], h[:, c, :], ACT.Copy).then_inc(u_part, 1)
            for m in range(DC):
                after_group(f"ple_gate{m}")
                if m >= 2:
                    act.wait_ge(po_copy, 16 + m - 1)
                f(slot[4 + m % 2][:, :], out_bank(f"ple_gate{m}")[:, :], ACT.Sigmoid).then_inc(ple_sig, 1)
                act.wait_ge(po_copy, 16 + m + 1)
                square("post2", m, mo_a)
            root("post2")
            norm_act(2, 16)
            split_hi(16, "up1")
            act.wait_ge(u_ready, 32)
            ffn_swiglu(1, "up1")
            norm_act(3, 24, "down1")
            split_hi(24, "wq")
            act.dma_start(wvb[:, :], t["wvb"]).then_inc(c_loaded, 16)
            act.dma_start(band[:, :], t["band"]).then_inc(c_loaded, 16)
            for c in range(8):
                feed("wq", c)
            for c in range(2):
                after_group("wk", c)
                f(wk[:, c, :], out_bank("wk", c)[:, :], ACT.Identity, bias=V("b_wk", c)).then_inc(wk_done, 1)
            feed("wv")
            items2 = []
            for qt in range(NT):
                for kv in range(WKV):
                    for r in range(4):
                        items2.append((min(qt + 1, 2) * P, V("sinks", 4 * kv + r), len(items2)))

            def win_gate(m):
                after_group(f"gate_w{m}")
                f(sg[:, m, :], out_bank(f"gate_w{m}")[:, :], ACT.Identity, bias=V("b_gate", m)).then_inc(sg_done, 1)

            def win_outs(i):
                if i >= 0 and i % 8 == 7:
                    qt, c = divmod(i // 8, 2)
                    act.wait_ge(att[1].pv_done, i + 1)
                    f(yw_hi[:, 4 * c:4 * c + 4, qt * P:(qt + 1) * P], heads(misc[2 + c]), ACT.Copy)\
                        .then_inc(att[1].o_part, 1)
                if i >= 8 and i % 8 == 2:
                    win_gate(i // 8 - 1)

            attention(att[1], items2, w_s, w_pt, st2, lambda j: None, win_outs)
            win_gate(DC - 1)
            act.wait_ge(sg_done, DC)
            f(sg[:, :, :], sg[:, :, :], ACT.Sigmoid).then_inc(sg_done, 1)
            for m in range(DC):
                feed(f"proj_w{m}")
            act.wait_ge(ma_done, 8)
            act.dma_start(mvb[:, :], t["mvb"]).then_inc(c_loaded, 16)
            act.dma_start(incl2, t["incl"]).then_inc(c_loaded, 16)
            for c in range(9):
                if c < 8:
                    after_group("mqk", c)
                    if c >= 2:
                        act.wait_ge(mqk_conv, c - 1)
                    f(slot[c % 2][:, :], out_bank("mqk", c)[:, :], ACT.Identity, bias=V("b_mqk", c)).then_inc(mqk_lin, 1)
                if c >= 1:
                    act.wait_ge(mqk_conv, c)
                    f(mqk[:, c - 1, :], cb2[:, (c - 1) % 2, :], ACT.Silu).then_inc(mqk_silu, 1)
            after_group("rows2")
            act.wait_ge(mqk_conv, 8)
            f(r_raw[0:40, :], out_bank("rows2")[0:40, :], ACT.Identity, bias=V("b_rows2")[0:40, :]).then_inc(r2_act, 1)
            act.wait_ge(r2_act, 1)
            f(r_i[0:8, :], r_raw[0:8, :], ACT.Tanh, scale=1.0 / 15.0).then_inc(r2_act, 1)
            f(r_f[0:8, :], r_raw[32:40, :], ACT.Tanh, scale=1.0 / 15.0).then_inc(r2_act, 1)
            act.wait_ge(r2_act, 3)
            f(r_f[0:8, :], r_f[0:8, :], ACT.Exp, scale=-15.0).then_inc(r2_act, 1)
            act.wait_ge(r2_act, 4)
            f(r_f[0:8, :], r_f[0:8, :], ACT.Ln, bias=one_col[0:8, :]).then_inc(r2_act, 1)
            feed("mv0")
            feed("mv1")
            for c in range(8):
                after_group("mo", c)
                f(so[:, c, :], out_bank("mo", c)[:, :], ACT.Sigmoid, bias=V("b_mo", c)).then_inc(so_done, 1)
            act.wait_ge(r2_dve, 5)
            f(emx[0:8, :], r_raw[0:8, :], ACT.Exp, scale=-1.0).then_inc(r2_act, 1)
            act.wait_ge(mqk_silu, 8)
            f(mxr, r_f[0:8, :], ACT.Copy).then_inc(r2_act, 1)
            off = [(0, 512), (2, 896), (1, 1024)]

            def decay_weights(hd):
                act.wait_ge(mb_done, hd + 1)
                act.wait_ge(ac_done, 1)
                act.wait_ge(mv_done, 8)
                if hd >= 2:
                    act.wait_ge(mnd_done, 3 * (hd - 1))
                act.wait_ge(mdg_in, hd + 1)
                x = wsc[:, hd % 2, :]
                for j, at_col in off:
                    f(x[:, at_col:at_col + (3 - j) * P], bank[0][:, (j + 1) * P:S], ACT.Exp,
                      bias=acol[:, j, hd:hd + 1], scale=-1.0)
                f(x[:, 0:S], x[:, 0:S], ACT.Exp, scale=-1.0).then_inc(mw_exp, 1)

            decay_weights(0)
            for hd in range(MH + 1):
                if hd + 1 < MH:
                    decay_weights(hd + 1)
                if hd >= 1:
                    act.wait_ge(head_sum, 12 + hd)
                    act_link(act, f(msq[:, :], misc[3][:, :], ACT.Ln, bias=eps_col, scale=1.0 / P))
                    f(msq[:, :], msq[:, :], ACT.Exp, scale=-0.5).then_inc(head_rt, 1)
                if hd < MH:
                    act.wait_ge(mnd_done, 3 * hd + 1)
                    if hd >= 1:
                        act.wait_ge(mhn, 2 * hd)
                    f(em_b[:, :], misc[2][:, :], ACT.Copy).then_inc(meb_copied, 1)
                if hd >= 1:
                    act.wait_ge(mh_y, hd)
                    f(m_hi[:, hd - 1, :], hn[:, (hd - 1) % 2, :], ACT.Copy).then_inc(mh_part, 1)
                if hd < MH:
                    act.wait_ge(mhn, 2 * hd + 2)
                    if hd >= 1:
                        act.wait_ge(mh_norm, hd)
                    f(msq[:, :], hn[:, hd % 2, :], ACT.Square).then_inc(head_sq, 1)
            for m in range(DC):
                after_group(f"gate_m{m}")
                if m >= 1:
                    act.wait_ge(mg_in, m)
                else:
                    act.wait_ge(mh_ready, 8)
                f(slot[m % 2][:, :], out_bank(f"gate_m{m}")[:, :], ACT.Sigmoid, bias=V("b_gate", 8 + m)).then_inc(sg_done, 1)
                act.wait_ge(mg_in, m + 1)
                f(mg_hi[:, m, :], ma[:, m, :], ACT.Copy).then_inc(mg_part, 1)
            norm_act(4, 32, "out")
            split_hi(32, "up2")
            act.wait_ge(u_ready, 48)
            ffn_swiglu(2, "up2")
            norm_act(5, 40, "down2")

        @block.vector
        def _(dve):
            v = nc.vector
            TT, TS, STT = v.tensor_tensor, v.tensor_scalar, v.scalar_tensor_tensor

            def inverse(name):
                r = NORMS.index(name)
                dve.wait_ge(ms_root, r + 1)
                v.reciprocal(root_col, root_col).then_inc(ms_inv, 1)
                dve.wait_ge(ms_row, r + 1)

            def norm_apply(n, gain, k0):
                inverse(f"pre{n}")
                for c in range(DC + 1):
                    if c < DC:
                        if c >= 2:
                            dve.wait_ge(u_ready, k0[1] + c - 1)
                        STT(slot[4 + c % 2][:, :], h[:, c, :], V(gain, c), misc[2][:, :], ALU.mult, ALU.mult)\
                            .then_inc(ux_done, 1)
                    if c >= 1:
                        dve.wait_ge(u_part, k0[1] + c)
                        TT(u_lo[:, c - 1, :], slot[4 + (c - 1) % 2][:, :], u_hi[:, c - 1, :].bitcast(F32),
                           ALU.subtract).then_inc(u_ready, 1)

            def add_squares(name, c):
                r = NORMS.index(name)
                dve.wait_ge(ms_sq, DC * r + c + 1)
                if c > 1:
                    dve.wait_ge(ms_acc, 7 * r + c - 1)
                TT(slot[2][:, :], (slot[2] if c > 1 else sq[0])[:, :], sq[c % 3][:, :], ALU.add).then_inc(ms_acc, 1)

            def post_apply(n, gain, mo):
                inverse(f"post{n}")
                for c in range(DC + 1):
                    if c < DC:
                        if c >= 2:
                            dve.wait_ge(h_ready, DC * n + c - 1)
                        STT(slot[4 + c % 2][:, :], mo[:, c, :], V(gain, c), misc[2][:, :], ALU.mult, ALU.mult)\
                            .then_inc(dve_step, 1)
                        steps["dve"] += 1
                    if c >= 1:
                        dve.wait_ge(dve_step, steps["dve"] - (1 if c < DC else 0))
                        TT(h[:, c - 1, :], h[:, c - 1, :], slot[4 + (c - 1) % 2][:, :], ALU.add).then_inc(h_ready, 1)

            def attention(a, items, s_buf, st_buf, between):
                def biased(j):
                    bias, init, _, nk_ = items[j]
                    dve.wait_ge(a.s_done, j + 1)
                    if j >= 4:
                        dve.wait_ge(a.t_done, between(j - 4))
                    v.tensor_tensor_reduce(s_buf[:, j % 4, 0:nk_], bank[j % 2][:, 0:nk_], bias, -1.0, init,
                                           ALU.add, ALU.min, st_buf[:, j % 8:j % 8 + 1]).then_inc(a.m_done, 1)

                def norm(j):
                    _, init, gate, nk_ = items[j]
                    dve.wait_ge(a.e_done, j + 1)
                    den = st_buf[:, 8 + j % 8:9 + j % 8]
                    if gate is None:
                        dve_link(dve, TT(den, den, st_buf[:, 24 + j % 8:25 + j % 8], ALU.add))
                    v.reciprocal(st_buf[:, 16 + j % 8:17 + j % 8], den).then_inc(dve_step, 1)
                    steps["dve"] += 1
                    if j + 2 < len(items):
                        biased(j + 2)
                    dve.wait_ge(dve_step, steps["dve"])
                    r = st_buf[:, 16 + j % 8:17 + j % 8]
                    if gate is None:
                        ins = TS(s_buf[:, j % 4, 0:nk_], s_buf[:, j % 4, 0:nk_], r, None, ALU.mult)
                    else:
                        ins = TS(s_buf[:, j % 4, 0:nk_], s_buf[:, j % 4, 0:nk_], r, gate, ALU.mult, ALU.mult)
                    ins.then_inc(a.p_done, 1)
                return biased, norm

            def ffn_gate(n, name):
                for c in range(FC + 1):
                    if c < FC:
                        dve.wait_ge(dense_done, group_of(name, 2 * c + 1))
                        dve.wait_ge(up_act, FC * n + c + 1)
                        TT(slot[c % 2][:, :], slot[c % 2][:, :], out_bank(name, 2 * c + 1)[:, :], ALU.mult)\
                            .then_inc(a_raw, 1)
                    if c >= 1:
                        dve.wait_ge(a_part, FC * n + c)
                        TT(a_lo[:, c - 1, :], slot[(c - 1) % 2][:, :], a_hi[:, c - 1, :].bitcast(F32),
                           ALU.subtract).then_inc(a_ready, 1)

            def add_half(name, scale, norm):
                for c in range(DC):
                    dve.wait_ge(dense_done, group_of(name, c))
                    STT(h[:, c, :], out_bank(name, c)[:, :], scale, h[:, c, :], ALU.mult, ALU.add).then_inc(h_ready, 1)
                    if c >= 2:
                        add_squares(norm, c - 1)
                add_squares(norm, DC - 1)

            v.memset(small[:, 250:251], EPS).then_inc(pool_step, 1)
            v.memset(small[:, 251:252], 1.0).then_inc(pool_step, 1)
            dve.wait_ge(in_loaded, 48)
            for i in range(4):
                dve.wait_ge(x_loaded[i], 16)
            for c in range(1, DC):
                add_squares("pre0", c)
            norm_apply(0, "mix_pre", (0, 0))
            for c in range(12):
                dve.wait_ge(cv_lin, c + 1)
                src, dst = out_bank("qkv", c), slot[c % 2]
                for n, tap in ((1, 2), (2, 1), (3, 0)):
                    ins = STT(dst[:, n:S], src[:, 0:S - n], V("conv_qkv", 4 * c + tap), dst[:, n:S], ALU.mult, ALU.add)
                    if n < 3:
                        dve_link(dve, ins)
                ins.then_inc(cv_done, 1)
            dve.wait_ge(c_loaded, 32)
            dve.wait_ge(u_ready, 8)
            dve_link(dve, v.tensor_copy(masks[:, :, :], masks_in[:, :, :]))
            dve.wait_ge(rows1_done, 3)
            dve_link(dve, TS(a_gate[0:4, :], a_gate[0:4, :], V("dt_bias")[0:4, :], None, ALU.add))
            STT(sp1[0:4, :], a_gate[0:4, :], -1.0, a_gate[0:4, :], ALU.mult, ALU.min).then_inc(sp_done, 1)
            dve.wait_ge(sp_exp, 1)
            dve_link(dve, STT(sp2[0:4, :], a_gate[0:4, :], 0.0, sp2[0:4, :], ALU.max, ALU.add))
            dve_link(dve, TS(sp2[0:4, :], sp2[0:4, :], na_col[0:4, :], -1.0, ALU.mult, ALU.mult))
            dve.wait_ge(c_loaded, 32)
            v.tensor_tensor_scan(g_sum[0:4, :], rowmask[0:4, :], sp2[0:4, :], 0.0, ALU.mult, ALU.add)\
                .then_inc(g_done, 1)
            for c in range(8):
                if c == 0:
                    dve.wait_ge(len_done, 1)
                STT(qkv[:, c, :], qkv[:, c, :], P ** -0.5 if c < 4 else 1.0, lens[:, c, :], ALU.mult,
                    ALU.mult).then_inc(l2_done, 1)
            dve.wait_ge(tr1_done, 1)
            v.tensor_copy(small[:, 0:32], misc[0][:, 0:32]).then_inc(cols_done, 1)
            v.tensor_copy(small[:, 96:192], misc[0][:, 64:160]).then_inc(cols_done, 1)
            dve.wait_ge(bc_copied, 4)
            dve.wait_ge(cols_done, 2)
            TT(tail_col, g_row[:, :, P - 1::P].rearrange("p h t -> p t h"), cols1[:, :, 0:4], ALU.subtract)\
                .then_inc(ecol_in, 1)
            dve.wait_ge(ecol_done, 3)
            dve_link(dve, TT(bg_col, e_col, cols1[:, :, 4:8], ALU.mult))

            def wide(col, tt):
                return col[:, tt, :].unsqueeze(2).broadcast_to([P, GH, P])

            for tt in range(NT):
                dve.wait_ge(kv_tr, 2 * tt + 1)
                TT(wk_t[:, tt, :, :], heads(misc[0]), wide(bg_col, tt), ALU.mult).then_inc(kv_done, 1)
                TT(kt_t[:, tt, :, :], heads(misc[0]), wide(tail_col, tt), ALU.mult).then_inc(kv_done, 1)
                dve.wait_ge(kv_tr, 2 * tt + 2)
                TT(vb_t[:, tt, :, :], heads(misc[3]), wide(cols1[:, :, 4:8], tt), ALU.mult).then_inc(kv_done, 1)

            def head_mask(i):
                return masks[:, i, :].unsqueeze(1).broadcast_to([P, GH, P])

            dve.wait_ge(l2_done, 8)
            for tt in range(NT):
                cut = slice(tt * P, (tt + 1) * P)
                for hd in range(GH):
                    ins = TS(dec[:, tt % 2, hd, :], g_row[:, hd, cut], cols1[:, tt, hd:hd + 1], 0.0, ALU.subtract, ALU.min)
                ins.then_inc(dc_in, 1)
                dve.wait_ge(dc_exp, tt + 1)
                dve_link(dve, TT(dmask[:, tt % 2, :, :], dec[:, tt % 2, :, :], head_mask(7), ALU.mult))
                dve.wait_ge(kk_done, 2 * tt + 1)
                TT(at_t[:, tt, :, :], heads(misc[1]), dmask[:, tt % 2, :, :], ALU.mult).then_inc(at_done, 1)
                dve.wait_ge(kk_done, 2 * tt + 2)
                TT(qk_t[:, tt, :, :], heads(misc[2]), dmask[:, tt % 2, :, :], ALU.mult).then_inc(at_done, 1)
            eye = ident[:, :].unsqueeze(1).broadcast_to([P, GH, P])

            def level_cut(n):
                if n < NT:
                    dve.wait_ge(at_beta, n + 1)
                else:
                    dve.wait_ge(x_done, n - 3)
                    if n < 2 * NT:
                        dve.wait_ge(u_upd, n - 3)
                TT(am[:, n % 4, :, :], at_t[:, n % NT, :, :], head_mask(n // NT), ALU.mult).then_inc(am_done, 1)

            n_all = LEVELS * NT
            for n in range(3):
                level_cut(n)
            for n in range(n_all):
                tt, final = n % NT, n >= n_all - NT
                if n + 3 < n_all:
                    level_cut(n + 3)
                if n < NT:
                    dve.wait_ge(at_beta, NT)
                    dve.wait_ge(am_done, n + 1)
                    TT(u_inv[:, tt, :, :], eye, am[:, n % 4, :, :], ALU.subtract).then_inc(u_upd, 1)
                    dve.wait_ge(x_done, n + 1)
                    TT(t_inv[:, tt, :, :], eye, heads(bank[n % 2]), ALU.subtract).then_inc(t_upd, 1)
                    dve.wait_ge(eg_done, n + 1)
                    TT(qkv[:, n, :], qkv[:, n, :], g_row[:, n, :], ALU.mult).then_inc(qd_done, 1)
                    continue
                dve.wait_ge(txu_done, n - NT + 1)
                if not final:
                    TT(t_inv[:, tt, :, :], t_inv[:, tt, :, :], heads(bank[2 + n % 2]), ALU.subtract).then_inc(t_upd, 1)
                else:
                    TT(u_inv[:, tt, :, :], u_inv[:, tt, :, :], heads(misc[n % 2]), ALU.subtract).then_inc(u_upd, 1)
            for tt in range(NT - 1):
                dve.wait_ge(ds_done, tt + 1)
                if tt == 0:
                    v.tensor_copy(state[:, 0, :, :], heads(bank[3])).then_inc(s_upd, 1)
                else:
                    dve.wait_ge(s_upd, tt)
                    for hd in range(GH):
                        ins = STT(state[:, tt % 2, hd, :], state[:, (tt - 1) % 2, hd, :], gl_col[:, tt, hd:hd + 1],
                                  bank[3][:, hd * P:(hd + 1) * P], ALU.mult, ALU.add)
                    ins.then_inc(s_upd, 1)
            for hd in range(GH):
                dve.wait_ge(head_rt, 8 + hd + 1)
                r = slot[2 + hd % 2]
                dve_link(dve, v.reciprocal(r[:, :], r[:, :]))
                dve_link(dve, STT(o_t[:, hd, :], o_t[:, hd, :], V("gdn_norm"), r[:, :], ALU.mult, ALU.mult))
                dve.wait_ge(z_silu, hd + 1)
                TT(o_t[:, hd, :], o_t[:, hd, :], xs[:, hd % 2, :, :].rearrange("p a b -> p (a b)"), ALU.mult)\
                    .then_inc(y_done, 1)
                dve.wait_ge(ya_part, hd + 1)
                TT(ya_lo[:, hd, :], o_t[:, hd, :], ya_hi[:, hd, :].bitcast(F32), ALU.subtract).then_inc(ya_ready, 1)

            for b in range(2):
                v.memset(z_raw[b][:, :, S - 1:528], 0.0).then_inc(zp_zero, 1)
            dve.wait_ge(c_loaded, 112)
            for b in range(2):
                dve.wait_ge(z_copied, 4 * b + 4)
                for half in range(2):
                    src = z_raw[b][:, :, 16 * half:16 * half + S].rearrange("p g (w i two) -> p g w i two", i=8, two=2)
                    i8 = slice(8 * half, 8 * half + 8)
                    dst = zc[:, b, i8, :, :].rearrange("p i g w -> p g w i")
                    for gr in range(NG):
                        add = pos[:, b, i8].unsqueeze(1).broadcast_to([P, 32, 8])
                        ins = TT(dst[:, gr, :, :], src[:, gr, :, :, 0], add, ALU.add)
                    ins.then_inc(zc_sum, 1)
            for b in range(2):
                dve.wait_ge(zc_part, b + 1)
                TT(zc_lo[:, b, :, :, :], zc[:, b, :, :, :], zc_hi[:, b, :, :, :].bitcast(F32), ALU.subtract)\
                    .then_inc(zc_ready, 1)
            for s in DVE_SLABS:
                dve.wait_ge(w_part, s + 1)
                TT(w_lo[:, s % SPLITS, :, :], raw[:, s % RAWS, :, :], w_hi[:, s % SPLITS, :, :].bitcast(F32),
                   ALU.subtract).then_inc(w_split_v, 1)
            a0 = att[0]
            c_m, c_r = st[:, 32:40], st[:, 40:48]

            def cmp_front(qt):
                dve.wait_ge(cs_done, qt + 1)
                if qt >= 1:
                    dve.wait_ge(a0.t_done, 18 * qt - 16)
                for gr in range(NG):
                    ins = TT(c_s[:, 4 * gr:4 * gr + 4, :], bank[2 + gr][:, 0:4 * NCMP].rearrange("p (h n) -> p h n", h=4),
                             c_bias[:, qt, 4 * gr:4 * gr + 4, :], ALU.add)
                dve_link(dve, ins)
                dve_link(dve, v.tensor_reduce(c_m, c_s[:, :, :], AX.X, ALU.max))
                TT(c_s[:, :, :], c_s[:, :, :], c_m.unsqueeze(2).broadcast_to([P, NH, NCMP]), ALU.subtract)\
                    .then_inc(cs_shift, 1)

            def cmp_back(qt):
                dve.wait_ge(cs_exp, qt + 1)
                dve_link(dve, v.tensor_reduce(c_r, c_s[:, :, :], AX.X, ALU.add))
                dve_link(dve, v.reciprocal(c_r, c_r))
                dve_link(dve, TT(c_r, c_r, gate_col[:, qt, 0:24:3], ALU.mult))
                dve_link(dve, TT(c_s[:, :, :], c_s[:, :, :],
                                 c_mask[:, qt, :].unsqueeze(1).broadcast_to([P, NH, NCMP]), ALU.mult))
                TT(c_s[:, :, :], c_s[:, :, :], c_r.unsqueeze(2).broadcast_to([P, NH, NCMP]), ALU.mult)\
                    .then_inc(cp_ready, 1)

            items = []
            for qt in range(NT):
                for hd in range(NH):
                    for b in range(2):
                        items.append((alibi[:, hd, (3 - qt) * P:S], BIG,
                                      gate_col[:, qt, 3 * hd + 1 + b:3 * hd + 2 + b], (qt + 1) * P))
            biased, norm = attention(a0, items, n_s, st, lambda i: 18 * (i // 16) + 2 + i % 16 + 1)
            dve.wait_ge(c_loaded, 112)
            dve.wait_ge(hid_done, 2)
            cmp_front(0)
            biased(0)
            biased(1)
            for j in range(64):
                if j % 16 == 0:
                    if j > 0:
                        cmp_front(j // 16)
                    cmp_back(j // 16)
                norm(j)
                if j % 16 == 1 and j > 16:
                    nsa_lo(dve, TT, j // 16 - 1, a0, yb_lo, yb_hi, misc, heads)
            nsa_lo(dve, TT, 3, a0, yb_lo, yb_hi, misc, heads)

            for m in range(DC):
                dve.wait_ge(dense_done, group_of(f"a2d{m}"))
                a_gate_m, b_gate_m = (early[:, m, 0, :], early[:, m, 1, :]) if m < EARLY else (slot[0][:, :], slot[1][:, :])
                dve.wait_ge(mixa_sig, 2 * max(m, EARLY) + (1 if m < EARLY else 2))
                if m >= 2:
                    dve.wait_ge(mx_ready, m - 1)
                TT(slot[4 + m % 2][:, :], a_gate_m, out_bank(f"a2d{m}")[:, :], ALU.mult).then_inc(mix_a, 1)
                dve.wait_ge(dense_done, group_of(f"b2d{m}"))
                dve.wait_ge(mixa_sig, 2 * max(m, EARLY) + (1 if m < EARLY else 3))
                dve.wait_ge(mix_a, m + 1)
                if m >= 1:
                    dve.wait_ge(mix_b, m)
                dve_link(dve, TT(slot[2][:, :], b_gate_m, out_bank(f"b2d{m}")[:, :], ALU.mult))
                TT(slot[4 + m % 2][:, :], slot[4 + m % 2][:, :], slot[2][:, :], ALU.add).then_inc(mix_b, 1)
                dve.wait_ge(mx_part, m + 1)
                TT(mx_lo[:, m, :], slot[4 + m % 2][:, :], mx_hi[:, m, :].bitcast(F32), ALU.subtract)\
                    .then_inc(mx_ready, 1)
            for c in range(1, DC):
                add_squares("post0", c)
            dve.wait_ge(x_loaded[0], 32)
            dve.wait_ge(x_loaded[1], 32)
            post_apply(0, "mix_post", mo_u)
            norm_apply(1, "ffn_pre", (0, 8))
            for c in range(FC + 1):
                if c < FC:
                    for b in range(2):
                        g = b * FC + c
                        dve.wait_ge(up_lin, 2 * c + b + 1)
                        src, dst = out_bank("up", 2 * c + b), slot[2 * b + c % 2]
                        dve_link(dve, STT(dst[:, 1:S], src[:, 0:S - 1], V("conv_ffn", 3 * g + 1), dst[:, 1:S], ALU.mult, ALU.add))
                        STT(dst[:, 2:S], src[:, 0:S - 2], V("conv_ffn", 3 * g), dst[:, 2:S], ALU.mult, ALU.add)\
                            .then_inc(up_conv, 1)
                if c >= 1:
                    dve.wait_ge(a_part, c)
                    TT(a_lo[:, c - 1, :], slot[2 + (c - 1) % 2][:, :], a_hi[:, c - 1, :].bitcast(F32),
                       ALU.subtract).then_inc(a_ready, 1)
                if c < FC:
                    dve.wait_ge(up_act, c + 1)
                    dve.wait_ge(up_conv, 2 * c + 2)
                    TT(slot[2 + c % 2][:, :], slot[2 + c % 2][:, :], slot[c % 2][:, :], ALU.mult).then_inc(a_raw, 1)
            for c in range(1, DC):
                add_squares("post1", c)
            inverse("post1")
            for c in range(DC + 2):
                if c < DC:
                    if c >= 2:
                        dve.wait_ge(h_ready, 8 + c - 1)
                    STT(slot[4 + c % 2][:, :], mo_u[:, c, :], V("ffn_post", c), misc[2][:, :], ALU.mult, ALU.mult)\
                        .then_inc(po_scaled, 1)
                if c in (4, 5):
                    dve.wait_ge(ps_part, c - 3)
                    TT(p_lo[:, c - 4, :], p_raw[:, c - 4, :], p_hi[:, c - 4, :].bitcast(F32), ALU.subtract)\
                        .then_inc(ps_ready, 1)
                if c >= 2:
                    dve.wait_ge(u_part, 16 + c - 1)
                    TT(u_lo[:, c - 2, :], h[:, c - 2, :], u_hi[:, c - 2, :].bitcast(F32), ALU.subtract)\
                        .then_inc(u_ready, 1)
            for m in range(DC):
                dve.wait_ge(ple_sig, m + 1)
                TT(mo_a[:, m, :], slot[4 + m % 2][:, :], out_bank(f"ple{m}")[:, :], ALU.mult).then_inc(po_copy, 1)
                if m >= 2:
                    add_squares("post2", m - 1)
            add_squares("post2", DC - 1)
            post_apply(2, "ple_post", mo_a)
            norm_apply(2, "ffn1", (0, 24))
            ffn_gate(1, "up1")
            add_half("down1", 0.5, "pre3")
            norm_apply(3, "mix2", (0, 32))
            for c in range(8):
                dve.wait_ge(dense_done, group_of("wq", c))
                TS(wq[:, c, :], out_bank("wq", c)[:, :], V("b_wq", c), ND ** -0.5, ALU.add, ALU.mult).then_inc(wq_done, 1)
            dve.wait_ge(c_loaded, 160)
            for j in range(NT):
                dve.wait_ge(dense_done, group_of("wv", j))
                TT(wv[:, j, :], out_bank("wv", j)[:, 0:256], wvb[:, :], ALU.add).then_inc(wv_done, 1)
            nsink = st2[:, 64:80]
            dve_link(dve, TS(nsink, V("sinks", 0, 16), -1.0, None, ALU.mult))
            items = []
            for qt in range(NT):
                for hd in range(WH):
                    items.append((band[:, P:256] if qt == 0 else band[:, :], nsink[:, hd:hd + 1], None,
                                  min(qt + 1, 2) * P))
            a1 = att[1]
            biased, norm = attention(a1, items, w_s, st2, lambda i: i + 1)

            def win_lo(n):
                qt, c = divmod(n, 2)
                dve.wait_ge(a1.o_part, n + 1)
                cut = slice(qt * P, (qt + 1) * P)
                TT(yw_lo[:, 4 * c:4 * c + 4, cut], heads(misc[2 + c]), yw_hi[:, 4 * c:4 * c + 4, cut].bitcast(F32),
                   ALU.subtract).then_inc(a1.o_ready, 1)

            biased(0)
            biased(1)
            for j in range(64):
                norm(j)
                if j % 8 == 3 and j > 8:
                    win_lo(j // 8 - 1)
            win_lo(7)
            for m in range(DC):
                dve.wait_ge(dense_done, group_of(f"proj_w{m}"))
                dve.wait_ge(sg_done, 9)
                STT(ma[:, m, :], out_bank(f"proj_w{m}")[:, :], 1.0, sg[:, m, :], ALU.mult, ALU.mult)\
                    .then_inc(ma_done, 1)
            for c in range(8):
                dve.wait_ge(mqk_lin, c + 1)
                if c >= 2:
                    dve.wait_ge(mqk_silu, c - 1)
                src, dst = slot[c % 2], cb2[:, c % 2, :]
                dve_link(dve, TS(dst, src[:, :], V("mconv", 4 * c + 3), None, ALU.mult))
                for n, tap in ((1, 2), (2, 1), (3, 0)):
                    ins = STT(dst[:, n:S], src[:, 0:S - n], V("mconv", 4 * c + tap), dst[:, n:S], ALU.mult, ALU.add)
                    if n < 3:
                        dve_link(dve, ins)
                ins.then_inc(mqk_conv, 1)
            dve_link(dve, v.memset(r_one[0:8, :], 1.0))
            dve.wait_ge(r2_act, 5)
            v.tensor_tensor_scan(r_raw[0:8, :], r_one[0:8, :], r_f[0:8, :], 0.0, ALU.mult, ALU.subtract)\
                .then_inc(r2_dve, 1)
            dve.wait_ge(r2_dve, 1)
            STT(r_a[0:8, :], r_i[0:8, :], 15.0, r_raw[0:8, :], ALU.mult, ALU.subtract).then_inc(r2_dve, 1)
            dve.wait_ge(r2_dve, 2)
            v.tensor_tensor_scan(r_f[0:8, :], r_one[0:8, :], r_a[0:8, :], 0.0, ALU.mult, ALU.max).then_inc(r2_dve, 1)
            dve.wait_ge(r2_dve, 3)
            TT(r_raw[0:8, :], r_raw[0:8, :], r_f[0:8, :], ALU.add).then_inc(r2_dve, 1)
            dve.wait_ge(c_loaded, 192)
            for hf in range(2):
                for j in range(NT):
                    dve.wait_ge(dense_done, group_of(f"mv{hf}", j))
                    TT(mv[:, j, hf * S:(hf + 1) * S], out_bank(f"mv{hf}", j)[:, :], mvb[:, hf * S:(hf + 1) * S], ALU.add)\
                        .then_inc(mv_done, 1)
            dve.wait_ge(ac_tr, 1)
            v.tensor_copy(small[:, 0:32], misc[0][:, 0:32]).then_inc(ac_done, 1)
            dve.wait_ge(mqk_silu, 8)
            v.memset(small[:, 252:253], 0.0).then_inc(r2_dve, 1)

            def diagonal_in(hd):
                dve.wait_ge(mb_done, hd + 1)
                dve.wait_ge(ac_done, 1)
                if hd >= 2:
                    dve.wait_ge(mnd_done, 3 * (hd - 1))
                for j in range(NT):
                    ins = TS(wsc[:, hd % 2, j * P:(j + 1) * P], bank[0][:, j * P:(j + 1) * P], acol[:, j, hd:hd + 1],
                             0.0, ALU.subtract, ALU.max)
                ins.then_inc(mdg_in, 1)

            def weigh(hd):
                x = wsc[:, hd % 2, :]
                dve.wait_ge(mw_exp, hd + 1)
                w4 = x[:, 0:S].rearrange("p (h c) -> p h c", h=NT)
                dve_link(dve, TT(w4, w4, incl2.unsqueeze(1).broadcast_to([P, NT, P]), ALU.mult))
                dve.wait_ge(msc_done, hd + 1)
                for lo, n, b in ((0, 512, 1), (512, 512, 2), (1024, 256, 3)):
                    STT(x[:, lo:lo + n], bank[b][:, 0:n], ND ** -0.5, x[:, lo:lo + n], ALU.mult, ALU.mult)\
                        .then_inc(mws, 1)

            def quotient(hd):
                dve.wait_ge(mnd_done, 3 * hd + 2)
                dve.wait_ge(meb_copied, hd + 1)
                dve_link(dve, STT(em_b[:, :], misc[1][:, :], -1.0, em_b[:, :], ALU.mult, ALU.max))
                dve_link(dve, TT(em_b[:, :], misc[1][:, :], em_b[:, :], ALU.max))
                v.reciprocal(em_b[:, :], em_b[:, :]).then_inc(mhn, 1)
                dve.wait_ge(mnd_done, 3 * hd + 3)
                dve.wait_ge(mhn, 2 * hd + 1)
                if hd >= 2:
                    dve.wait_ge(mh_ready, hd - 1)
                TT(hn[:, hd % 2, :], misc[0][:, :], em_b[:, :], ALU.mult).then_inc(mhn, 1)

            diagonal_in(0)
            weigh(0)
            for hd in range(MH + 1):
                if hd + 1 < MH:
                    diagonal_in(hd + 1)
                if hd >= 1:
                    dve.wait_ge(head_rt, 12 + hd)
                    x = hn[:, (hd - 1) % 2, :]
                    STT(x, x, V("head_norm", hd - 1), msq[:, :], ALU.mult, ALU.mult).then_inc(mh_norm, 1)
                if hd + 1 < MH:
                    weigh(hd + 1)
                if hd < MH:
                    quotient(hd)
            for m in range(DC):
                dve.wait_ge(dense_done, group_of(f"proj_m{m}"))
                dve.wait_ge(sg_done, 9 + m + 1)
                if m >= 2:
                    dve.wait_ge(mg_in, m - 1)
                dve_link(dve, TT(slot[2 + m % 2][:, :], slot[m % 2][:, :], out_bank(f"proj_m{m}")[:, :], ALU.mult))
                TT(ma[:, m, :], ma[:, m, :], slot[2 + m % 2][:, :], ALU.add).then_inc(mg_in, 1)
                dve.wait_ge(mg_part, m + 1)
                TT(mg_lo[:, m, :], ma[:, m, :], mg_hi[:, m, :].bitcast(F32), ALU.subtract).then_inc(mg_ready, 1)
            add_half("out", 1.0, "pre4")
            norm_apply(4, "ffn2", (0, 40))
            ffn_gate(2, "up2")
            add_half("down2", 0.5, "pre5")
            inverse("pre5")
            for c in range(DC):
                STT(result[:, c, :], h[:, c, :], V("final", c), misc[2][:, :], ALU.mult, ALU.mult).then_inc(f_out, 1)


def nsa_lo(dve, TT, qt, a, yb_lo, yb_hi, misc, heads):
    dve.wait_ge(a.o_part, qt + 1)
    cut = slice(qt * P, (qt + 1) * P)
    TT(yb_lo[:, :, cut], heads(misc[2]), yb_hi[:, :, cut].bitcast(F32), ALU.subtract).then_inc(a.o_ready, 1)


def layout(x, inp):
    I = {k: np.asarray(v) for k, v in inp.items()}
    one = lambda n: I[n][0]
    win = one("w_in")
    o = np.cumsum([0, 512, 512, 512, 512, 4, 4, 512, 128, 128, 128, 128, 128, 128, 24, 2048])
    (qa, ka, va, za, ba, aa, qb, kcm, vcm, ksl, vsl, kwi, vwi, gn, gm) = [win[:, a:b] for a, b in zip(o[:-1], o[1:])]
    zero = lambda n: np.zeros((D, n), np.float32)
    rows1 = np.concatenate([ba, zero(28), aa, zero(28), gn, zero(40)], 1)
    order = [g * 4 + c for c in range(4) for g in range(2)]
    pick = lambda w, heads_: np.concatenate([w[:, 64 * i:64 * i + 64] for i in heads_], 1)
    twice = lambda w: np.concatenate([w, w], 1)
    w2i = one("w_in_2")
    o2 = np.cumsum([0, 1024, 256, 256, 512, 512, 1024, 1024, 8, 8, 2048])
    cut2 = [slice(a, b) for a, b in zip(o2[:-1], o2[1:])]
    worder = [(2 * p_ + s) * 4 + r for p_ in range(2) for r in range(4) for s in range(2)]
    rows2 = np.concatenate([w2i[:, cut2[7]], zero(24), w2i[:, cut2[8]], zero(88)], 1)
    rowpick = lambda w, heads_: np.concatenate([w[64 * i:64 * i + 64] for i in heads_], 0)
    w_b2d = rowpick(one("w_b2d"), order)
    w_pa = rowpick(one("w_proj_attn_2"), worder)
    up = one("w_up")

    def pairs(a, b):
        a, b = a.reshape(D, FC, 1, P), b.reshape(D, FC, 1, P)
        return np.concatenate([a, b], 2).reshape(D, 2 * FF)

    mats = {
        "qkv": np.concatenate([qa, ka, va], 1), "rows1": rows1,  "nq": pick(qb, order),
        "nk": np.concatenate([ksl, kwi], 1),
        "ncmp": np.concatenate([twice(kcm[:, :64]), twice(kcm[:, 64:]), twice(vcm[:, :64]), twice(vcm[:, 64:])], 1),
        "nv": np.concatenate([vsl, vwi], 1), "cmpk": one("cmp_w1_k"), "cmpv": one("cmp_w1_v"),
        "w_o": one("w_o"), "up": pairs(up[:, :FF], up[:, FF:]), "down": one("w_down"),
        "up1": pairs(one("ffn1_w_gate_2"), one("ffn1_w_up_2")), "down1": one("ffn1_w_down_2"),
        "up2": pairs(one("ffn2_w_gate_2"), one("ffn2_w_up_2")), "down2": one("ffn2_w_down_2"),
        "wq": pick(w2i[:, cut2[0]], worder), "wk": w2i[:, cut2[1]], "wv": w2i[:, cut2[2]],
        "mqk": np.concatenate([w2i[:, cut2[3]], w2i[:, cut2[4]]], 1), "rows2": rows2,
        "mv0": w2i[:, cut2[5]][:, :512], "mv1": w2i[:, cut2[5]][:, 512:], "mo": w2i[:, cut2[6]],
        "out": one("w_out_2"),
    }
    g2 = w2i[:, cut2[9]]
    mats.update({f"z{i}": za[:, i * P:(i + 1) * P] for i in range(GH)})
    for m in range(DC):
        c = slice(m * P, (m + 1) * P)
        mats[f"gate_a{m}"], mats[f"gate_b{m}"] = gm[:, :D][:, c], gm[:, D:][:, c]
        mats[f"a2d{m}"], mats[f"b2d{m}"] = one("w_a2d")[:, c], w_b2d[:, c]
        mats[f"ple{m}"], mats[f"ple_gate{m}"] = one("w_ple")[:, c], one("w_ple_gate")[:, c]
        mats[f"gate_w{m}"], mats[f"gate_m{m}"] = g2[:, :D][:, c], g2[:, D:][:, c]
        mats[f"proj_w{m}"], mats[f"proj_m{m}"] = w_pa[:, c], one("w_proj_mlstm_2")[:, c]
    stream = np.zeros((NSLABS * SLAB, P, P), np.float32)
    for name, chunks, k, width in dense_layers():
        at = START[name][0]
        w = mats[name]
        b = w.reshape(k, P, w.shape[1] // P, P)
        if width:
            stream[at:at + k * width] = b.transpose(0, 2, 1, 3).reshape(k * width, P, P)
        else:
            for c in range(chunks):
                for i in range(k):
                    stream[tile_at(name, k, c, i)] = b[i, :, c]
    weights = np.ascontiguousarray(stream.reshape(NSLABS, SLAB, P, P).transpose(0, 2, 1, 3))

    vec = np.zeros((P, NVEC), np.float32)

    def put(name, a):
        a = np.asarray(a)
        vec[:a.shape[0], VECS[name]:VECS[name] + a.shape[1]] = a

    cols = lambda a: a.reshape(-1, P).T
    taps = lambda w: w.T.reshape(-1, P, w.shape[0]).transpose(1, 0, 2).reshape(P, -1)
    put("mix_pre", cols(one("norm_mix_pre")))
    put("conv_qkv", taps(one("conv_qkv")))
    put("gdn_norm", one("gdn_norm")[:, None])
    put("mix_post", cols(one("norm_mix_post")))
    put("ffn_pre", cols(one("norm_ffn_pre")))
    put("conv_ffn", taps(one("conv_ffn")))
    put("conv_ffn_b", cols(one("conv_ffn_b")))
    put("ffn_post", cols(one("norm_ffn_post")))
    put("ple_post", cols(one("norm_ple_post")))
    put("ffn1", cols(one("ffn1_norm_2")))
    put("mix2", cols(one("mix_norm_2")))
    bi = one("b_in_2")
    put("b_wq", cols(pick(bi[None, cut2[0]], worder)[0]))
    put("b_wk", cols(bi[cut2[1]]))
    put("b_mqk", cols(np.concatenate([bi[cut2[3]], bi[cut2[4]]])))
    put("b_mo", cols(bi[cut2[6]]))
    put("b_rows2", np.concatenate([bi[cut2[7]], np.zeros(24, np.float32), bi[cut2[8]]])[:, None])
    put("b_gate", cols(bi[cut2[9]]))
    put("mconv", taps(one("mlstm_conv_2")))
    put("head_norm", one("mlstm_head_norm_2").T)
    put("ffn2", cols(one("ffn2_norm_2")))
    put("final", cols(I["final_norm_2"]))
    put("a_log", one("a_log")[:, None])
    put("dt_bias", one("dt_bias")[:, None])
    put("sinks", np.broadcast_to(one("attn_sinks_2")[None], (P, WH)))

    j, i = np.arange(P)[:, None], np.arange(P)[None, :]
    masks = np.zeros((P, 8, P), np.float32)
    for lv in range(LEVELS):
        m = 1 << lv
        masks[:, lv] = (j // (2 * m) == i // (2 * m)) & ((i // m) % 2 == 1) & ((j // m) % 2 == 0)
    masks[:, 7] = i >= j
    rowmask = np.broadcast_to((np.arange(S) % P != 0).astype(np.float32), (P, S))
    q, xk = np.arange(P)[:, None], np.arange(S)[None, :] - 384
    slope = 2.0 ** (-8.0 * np.arange(1, NH + 1) / NH)
    alibi = np.where(xk <= q, 0, 1)[:, None, :] * -1e30 + np.where(xk <= q, xk - q, 0)[:, None, :] * slope[None, :, None]
    tq = np.arange(NT)[None, :] * P + np.arange(P)[:, None]
    dist = tq[:, :, None] - (np.arange(NCMP) * CS + CL - 1)[None, None, :]
    c_mask = (dist >= 0).astype(np.float32)
    c_bias = np.where(dist[:, :, None, :] >= 0, -slope[None, None, :, None] * dist[:, :, None, :], -1e30)
    kj, qi = np.arange(2 * P)[None, :], np.arange(P)[:, None]
    band = np.where((kj > qi) & (kj <= qi + P), 0.0, -1e30)
    pos = np.stack([one(n).reshape(16, P).T for n in ("cmp_pos_k", "cmp_pos_v")], 1)
    w2 = np.stack([one(n).reshape(2, P, ND).transpose(1, 0, 2) for n in ("cmp_w2_k", "cmp_w2_v")], 1)
    f = lambda a: np.ascontiguousarray(a, dtype=np.float32)
    fm = lambda a: f(a.T.reshape(-1, P, S).transpose(1, 0, 2))
    return {
        "weights": weights, "x": fm(x[0]), "p": fm(I["p"][0, 0]), "vec": vec,
        "ident": f(np.eye(P)), "ones": f(np.ones((P, P))), "masks": f(masks),
        "incl": f(masks[:, 7]), "rowmask": f(rowmask),
        "alibi": f(alibi), "c_bias": f(c_bias), "c_mask": f(c_mask), "band": f(band), "pos": f(pos), "w2": f(w2),
        "wvb": f(np.broadcast_to(bi[cut2[2]], (P, 256))), "mvb": f(np.broadcast_to(bi[cut2[5]], (P, 1024))),
    }


def kernel(**inputs):
    import concourse.bacc as bacc
    from concourse.bass_utils import run_bass_kernel_spmd

    x = np.asarray(inputs.pop("x"))
    arrays = layout(x, inputs)
    nc = bacc.Bacc("TRN2", target_bir_lowering=False, num_devices=1)
    t = {n: nc.dram_tensor(f"in_{n}", a.shape, mybir.dt.from_np(a.dtype), kind="ExternalInput").ap()
         for n, a in arrays.items()}
    t["out"] = nc.dram_tensor("out", (P, DC, S), F32, kind="ExternalOutput").ap()
    build(nc, t)
    r = run_bass_kernel_spmd(nc, [{f"in_{n}": a for n, a in arrays.items()}], core_ids=[0])
    out = r.results[0]["out"]
    return np.ascontiguousarray(out.transpose(1, 0, 2).reshape(D, S).T)[None]
```
